# Optimizing a Trainium2 kernel written in Bass

```python
import math
import jax, jax.numpy as jnp
from jax import lax
import numpy as np

D_MODEL = 1024
BATCH = 1
SEQ = 256
DEPTH = 2

CHUNK = 64
Q_BLOCK = 128

SSD_HEADS = 16
SSD_HEAD_DIM = 64
SSD_INNER = SSD_HEADS * SSD_HEAD_DIM
SSD_GROUPS = 2
SSD_STATE = 128
SSD_CONV = 4
SSD_CONV_DIM = SSD_INNER + 2 * SSD_GROUPS * SSD_STATE

SB_HEADS = 8
SB_HEAD_DIM = 64
SB_WIDTH = SB_HEADS * SB_HEAD_DIM

MLA_HEADS = 8
MLA_Q_RANK = 256
MLA_KV_RANK = 128
MLA_NOPE = 64
MLA_ROPE = 32
MLA_V = 64
ROPE_THETA = 10000.0

FOX_HEADS = 8
FOX_HEAD_DIM = 64
FOX_WIDTH = FOX_HEADS * FOX_HEAD_DIM

EVEN_IN = SSD_INNER + SSD_CONV_DIM + SSD_HEADS + 3 * SB_WIDTH
EVEN_OUT = SSD_INNER + SB_WIDTH
ODD_IN = MLA_Q_RANK + MLA_KV_RANK + MLA_ROPE + 3 * FOX_WIDTH + FOX_HEADS
ODD_OUT = MLA_HEADS * MLA_V + FOX_WIDTH

MOE_GROUPS = 4
MOE_EXPERTS_PER_GROUP = 4
MOE_EXPERTS = MOE_GROUPS * MOE_EXPERTS_PER_GROUP
MOE_TOP_K = 2
MOE_FF = 256

DEEPNORM_ALPHA = (2.0 * DEPTH) ** 0.25
DEEPNORM_BETA = (8.0 * DEPTH) ** -0.25
LN_EPS = 1e-5
RMS_EPS = 1e-6

N_EVEN = (DEPTH + 1) // 2
N_ODD = DEPTH // 2


def _layer_norm(x, g, b):
    x32 = x.astype(jnp.float32)
    mu = jnp.mean(x32, -1, keepdims=True)
    var = jnp.mean(jnp.square(x32 - mu), -1, keepdims=True)
    return ((x32 - mu) * lax.rsqrt(var + LN_EPS) * g + b).astype(x.dtype)

def _rms_norm(x, g):
    x32 = x.astype(jnp.float32)
    return (x32 * lax.rsqrt(jnp.mean(x32 * x32, -1, keepdims=True) + RMS_EPS) * g).astype(x.dtype)

def _split(h, sizes):
    idx = [int(i) for i in np.cumsum(sizes)[:-1]]
    return jnp.split(h, idx, axis=-1)

def _rope(x, cos, sin):
    x1, x2 = jnp.split(x, 2, axis=-1)
    return jnp.concatenate([x1 * cos - x2 * sin, x2 * cos + x1 * sin], axis=-1).astype(x.dtype)

def _causal_depthwise_conv(x, w, b):
    k, c = w.shape
    y = lax.conv_general_dilated(x, w[:, None, :], window_strides=(1,), padding=[(k - 1, 0)],
                                 dimension_numbers=('NWC', 'WIO', 'NWC'), feature_group_count=c)
    return y + b

def _ssd_scan(x, dt, a, b_in, c_in):
    f32 = jnp.float32
    bsz, s, h, p = x.shape
    g, n = b_in.shape[2], b_in.shape[3]
    r = h // g
    nc = s // CHUNK
    xs = (x.astype(f32) * dt[..., None]).reshape(bsz, nc, CHUNK, g, r, p)
    da = (dt * a).reshape(bsz, nc, CHUNK, g, r).transpose(0, 3, 4, 1, 2)
    a_cum = jnp.cumsum(da, axis=-1)
    bc = b_in.astype(f32).reshape(bsz, nc, CHUNK, g, n)
    cc = c_in.astype(f32).reshape(bsz, nc, CHUNK, g, n)
    causal = jnp.tril(jnp.ones((CHUNK, CHUNK), dtype=bool))
    seg = a_cum[..., :, None] - a_cum[..., None, :]
    decay_in = jnp.exp(jnp.where(causal, seg, -jnp.inf))
    cb = jnp.einsum('bclgn,bcsgn->bgcls', cc, bc)
    y_diag = jnp.einsum('bgcls,bgrcls,bcsgrp->bclgrp', cb, decay_in, xs)
    decay_to_end = jnp.exp(a_cum[..., -1:] - a_cum)
    states = jnp.einsum('bclgn,bgrcl,bclgrp->bcgrpn', bc, decay_to_end, xs)
    chunk_decay = jnp.exp(a_cum[..., -1])

    def step(hstate, inp):
        st, dec = inp
        return hstate * dec[..., None, None] + st, hstate

    h0 = jnp.zeros((bsz, g, r, p, n), f32)
    _, prev = lax.scan(step, h0, (jnp.moveaxis(states, 1, 0), jnp.moveaxis(chunk_decay, -1, 0)))
    y_off = jnp.einsum('bclgn,cbgrpn,bgrcl->bclgrp', cc, prev, jnp.exp(a_cum))
    return (y_diag + y_off).reshape(bsz, s, h, p)

def _stick_breaking_attention(q, k, v):
    s, d = q.shape[1], q.shape[3]
    scale = 1.0 / math.sqrt(d)
    outs = []
    for q0 in range(0, s, Q_BLOCK):
        end = q0 + Q_BLOCK
        z = jnp.einsum('bthd,bshd->bhts', q[:, q0:end], k[:, :end]).astype(jnp.float32) * scale
        t_pos = q0 + jnp.arange(Q_BLOCK)[:, None]
        s_pos = jnp.arange(end)[None, :]
        strict = s_pos < t_pos
        log_1m = jnp.where(strict, jax.nn.log_sigmoid(-z), 0.0)
        later = lax.cumsum(log_1m, axis=3, reverse=True) - log_1m
        w = jnp.where(strict, jnp.exp(jax.nn.log_sigmoid(z) + later), 0.0)
        outs.append(jnp.einsum('bhts,bshd->bthd', w.astype(v.dtype), v[:, :end]))
    return jnp.concatenate(outs, axis=1)

def _mla_attention(q_nope, q_pe, k_nope, k_pe, v):
    s = q_nope.shape[1]
    scale = 1.0 / math.sqrt(MLA_NOPE + MLA_ROPE)
    outs = []
    for q0 in range(0, s, Q_BLOCK):
        end = q0 + Q_BLOCK
        z = (jnp.einsum('bthd,bshd->bhts', q_nope[:, q0:end], k_nope[:, :end])
             + jnp.einsum('bthd,bsd->bhts', q_pe[:, q0:end], k_pe[:, :end])).astype(jnp.float32) * scale
        t_pos = q0 + jnp.arange(Q_BLOCK)[:, None]
        s_pos = jnp.arange(end)[None, :]
        allowed = (s_pos // CHUNK) <= (t_pos // CHUNK)
        prob = jax.nn.softmax(jnp.where(allowed, z, -jnp.inf), axis=-1)
        outs.append(jnp.einsum('bhts,bshd->bthd', prob.astype(v.dtype), v[:, :end]))
    return jnp.concatenate(outs, axis=1)

def _forgetting_attention(q, k, v, log_f):
    s, d = q.shape[1], q.shape[3]
    scale = 1.0 / math.sqrt(d)
    fh = jnp.cumsum(log_f, axis=1).transpose(0, 2, 1)
    outs = []
    for q0 in range(0, s, Q_BLOCK):
        end = q0 + Q_BLOCK
        z = jnp.einsum('bthd,bshd->bhts', q[:, q0:end], k[:, :end]).astype(jnp.float32) * scale
        z = z + fh[:, :, q0:end, None] - fh[:, :, None, :end]
        t_pos = q0 + jnp.arange(Q_BLOCK)[:, None]
        s_pos = jnp.arange(end)[None, :]
        prob = jax.nn.softmax(jnp.where(s_pos <= t_pos, z, -jnp.inf), axis=-1)
        outs.append(jnp.einsum('bhts,bshd->bthd', prob.astype(v.dtype), v[:, :end]))
    return jnp.concatenate(outs, axis=1)

def _even_mixer(x, w_in, conv_w, conv_b, dt_bias, a_log, d_skip, norm_g, w_out):
    f32 = jnp.float32
    bsz, s, _ = x.shape
    h = x @ w_in
    z, xbc, dt_raw, q, k, v = _split(h, [SSD_INNER, SSD_CONV_DIM, SSD_HEADS, SB_WIDTH, SB_WIDTH, SB_WIDTH])
    xbc = jax.nn.silu(_causal_depthwise_conv(xbc, conv_w, conv_b))
    xs, bs, cs = _split(xbc, [SSD_INNER, SSD_GROUPS * SSD_STATE, SSD_GROUPS * SSD_STATE])
    xs = xs.reshape(bsz, s, SSD_HEADS, SSD_HEAD_DIM)
    dt = jax.nn.softplus((dt_raw + dt_bias).astype(f32))
    a = -jnp.exp(a_log.astype(f32))
    y = _ssd_scan(xs, dt, a, bs.reshape(bsz, s, SSD_GROUPS, SSD_STATE), cs.reshape(bsz, s, SSD_GROUPS, SSD_STATE))
    y = (y + d_skip[:, None] * xs).reshape(bsz, s, SSD_INNER).astype(x.dtype)
    y = _rms_norm(y * jax.nn.silu(z), norm_g)
    sb = _stick_breaking_attention(q.reshape(bsz, s, SB_HEADS, SB_HEAD_DIM), k.reshape(bsz, s, SB_HEADS, SB_HEAD_DIM),
                                   v.reshape(bsz, s, SB_HEADS, SB_HEAD_DIM)).reshape(bsz, s, SB_WIDTH)
    return jnp.concatenate([y, sb], axis=-1) @ w_out

def _odd_mixer(x, w_in, q_norm_g, w_q_up, kv_norm_g, w_kv_up, f_bias, w_out, cos, sin):
    bsz, s, _ = x.shape
    h = x @ w_in
    c_q, c_kv, k_pe, q, k, v, f_raw = _split(h, [MLA_Q_RANK, MLA_KV_RANK, MLA_ROPE, FOX_WIDTH, FOX_WIDTH, FOX_WIDTH, FOX_HEADS])
    q_m = (_rms_norm(c_q, q_norm_g) @ w_q_up).reshape(bsz, s, MLA_HEADS, MLA_NOPE + MLA_ROPE)
    q_nope = q_m[..., :MLA_NOPE]
    q_pe = _rope(q_m[..., MLA_NOPE:], cos[:, None, :], sin[:, None, :])
    kv = (_rms_norm(c_kv, kv_norm_g) @ w_kv_up).reshape(bsz, s, MLA_HEADS, MLA_NOPE + MLA_V)
    k_nope, v_m = kv[..., :MLA_NOPE], kv[..., MLA_NOPE:]
    k_pe = _rope(k_pe, cos, sin)
    mla = _mla_attention(q_nope, q_pe, k_nope, k_pe, v_m).reshape(bsz, s, MLA_HEADS * MLA_V)
    log_f = jax.nn.log_sigmoid((f_raw + f_bias).astype(jnp.float32))
    fox = _forgetting_attention(q.reshape(bsz, s, FOX_HEADS, FOX_HEAD_DIM), k.reshape(bsz, s, FOX_HEADS, FOX_HEAD_DIM),
                                v.reshape(bsz, s, FOX_HEADS, FOX_HEAD_DIM), log_f).reshape(bsz, s, FOX_WIDTH)
    return jnp.concatenate([mla, fox], axis=-1) @ w_out

def _hier_moe(x, w_group, b_group, w_expert, b_expert, w_gate, w_up, w_down):
    f32 = jnp.float32
    bsz, s, d = x.shape
    t = x.reshape(bsz * s, d)
    n_tok = t.shape[0]
    g_prob = jax.nn.softmax((t @ w_group + b_group).astype(f32), axis=-1)
    g_p, g_sel = lax.top_k(g_prob, 1)
    e_logits = (t @ w_expert + b_expert).astype(f32).reshape(n_tok, MOE_GROUPS, MOE_EXPERTS_PER_GROUP)
    idx = jnp.broadcast_to(g_sel[:, :, None], (n_tok, 1, MOE_EXPERTS_PER_GROUP))
    e_prob = jax.nn.softmax(jnp.take_along_axis(e_logits, idx, axis=1)[:, 0], axis=-1)
    top_p, top_i = lax.top_k(e_prob, MOE_TOP_K)
    weights = g_p * top_p / jnp.sum(top_p, axis=-1, keepdims=True)
    expert_id = g_sel * MOE_EXPERTS_PER_GROUP + top_i
    gate = jnp.sum(jax.nn.one_hot(expert_id, MOE_EXPERTS, dtype=f32) * weights[..., None], axis=1)
    y = jnp.zeros((n_tok, d), f32)
    for e in range(MOE_EXPERTS):
        hid = jax.nn.silu(t @ w_gate[e]) * (t @ w_up[e])
        y = y + gate[:, e:e + 1] * (hid @ w_down[e])
    return y.astype(x.dtype).reshape(bsz, s, d)

def first_inputs(seed: int = 0) -> dict:
    key = jax.random.key(seed)
    ks = iter(jax.random.split(key, 40))
    nrm = lambda shape, scale: jax.random.normal(next(ks), shape, jnp.float32) * scale
    gain = lambda shape: 1.0 + nrm(shape, 0.02)
    dt0 = jnp.exp(jax.random.uniform(next(ks), (N_EVEN, SSD_HEADS), jnp.float32, math.log(1e-3), math.log(1e-1)))
    return {
        'x': nrm((BATCH, SEQ, D_MODEL), 1.0),
        'ev_w_in': nrm((N_EVEN, D_MODEL, EVEN_IN), D_MODEL ** -0.5),
        'ev_conv_w': nrm((N_EVEN, SSD_CONV, SSD_CONV_DIM), SSD_CONV ** -0.5),
        'ev_conv_b': nrm((N_EVEN, SSD_CONV_DIM), 0.02),
        'ev_dt_bias': dt0 + jnp.log(-jnp.expm1(-dt0)),
        'ev_a_log': jnp.log(jax.random.uniform(next(ks), (N_EVEN, SSD_HEADS), jnp.float32, 1.0, 16.0)),
        'ev_d_skip': gain((N_EVEN, SSD_HEADS)),
        'ev_norm_g': gain((N_EVEN, SSD_INNER)),
        'ev_w_out': nrm((N_EVEN, EVEN_OUT, D_MODEL), EVEN_OUT ** -0.5 * DEEPNORM_BETA),
        'od_w_in': nrm((N_ODD, D_MODEL, ODD_IN), D_MODEL ** -0.5),
        'od_q_norm_g': gain((N_ODD, MLA_Q_RANK)),
        'od_w_q_up': nrm((N_ODD, MLA_Q_RANK, MLA_HEADS * (MLA_NOPE + MLA_ROPE)), MLA_Q_RANK ** -0.5),
        'od_kv_norm_g': gain((N_ODD, MLA_KV_RANK)),
        'od_w_kv_up': nrm((N_ODD, MLA_KV_RANK, MLA_HEADS * (MLA_NOPE + MLA_V)), MLA_KV_RANK ** -0.5),
        'od_f_bias': nrm((N_ODD, FOX_HEADS), 0.1),
        'od_w_out': nrm((N_ODD, ODD_OUT, D_MODEL), ODD_OUT ** -0.5 * DEEPNORM_BETA),
        'ln1_g': gain((DEPTH, D_MODEL)),
        'ln1_b': nrm((DEPTH, D_MODEL), 0.02),
        'ln2_g': gain((DEPTH, D_MODEL)),
        'ln2_b': nrm((DEPTH, D_MODEL), 0.02),
        'moe_w_group': nrm((DEPTH, D_MODEL, MOE_GROUPS), D_MODEL ** -0.5),
        'moe_b_group': nrm((DEPTH, MOE_GROUPS), 0.01),
        'moe_w_expert': nrm((DEPTH, D_MODEL, MOE_EXPERTS), D_MODEL ** -0.5),
        'moe_b_expert': nrm((DEPTH, MOE_EXPERTS), 0.01),
        'moe_w_gate': nrm((DEPTH, MOE_EXPERTS, D_MODEL, MOE_FF), D_MODEL ** -0.5),
        'moe_w_up': nrm((DEPTH, MOE_EXPERTS, D_MODEL, MOE_FF), D_MODEL ** -0.5 * DEEPNORM_BETA),
        'moe_w_down': nrm((DEPTH, MOE_EXPERTS, MOE_FF, D_MODEL), MOE_FF ** -0.5 * DEEPNORM_BETA),
    }

def first_block(x, ev_w_in, ev_conv_w, ev_conv_b, ev_dt_bias, ev_a_log, ev_d_skip, ev_norm_g, ev_w_out,
              od_w_in, od_q_norm_g, od_w_q_up, od_kv_norm_g, od_w_kv_up, od_f_bias, od_w_out,
              ln1_g, ln1_b, ln2_g, ln2_b, moe_w_group, moe_b_group, moe_w_expert, moe_b_expert,
              moe_w_gate, moe_w_up, moe_w_down):
    s = x.shape[1]
    inv_freq = ROPE_THETA ** (-(jnp.arange(0, MLA_ROPE, 2, dtype=jnp.float32) / MLA_ROPE))
    ang = jnp.arange(s, dtype=jnp.float32)[:, None] * inv_freq[None, :]
    cos, sin = jnp.cos(ang), jnp.sin(ang)
    for i in range(DEPTH):
        j = i // 2
        if i % 2 == 0:
            mix = _even_mixer(x, ev_w_in[j], ev_conv_w[j], ev_conv_b[j], ev_dt_bias[j], ev_a_log[j],
                              ev_d_skip[j], ev_norm_g[j], ev_w_out[j])
        else:
            mix = _odd_mixer(x, od_w_in[j], od_q_norm_g[j], od_w_q_up[j], od_kv_norm_g[j], od_w_kv_up[j],
                             od_f_bias[j], od_w_out[j], cos, sin)
        x = _layer_norm(DEEPNORM_ALPHA * x + mix, ln1_g[i], ln1_b[i])
        ffn = _hier_moe(x, moe_w_group[i], moe_b_group[i], moe_w_expert[i], moe_b_expert[i],
                        moe_w_gate[i], moe_w_up[i], moe_w_down[i])
        x = _layer_norm(DEEPNORM_ALPHA * x + ffn, ln2_g[i], ln2_b[i])
    return x


SG_WIDTH = 2 * D_MODEL
SG_GROUPS = 8
SG_CHUNK = 128
DA_HEADS = D_MODEL // 128
DA_HEAD_DIM = 64
ROT_DIM = DA_HEAD_DIM // 4
ROPE_THETA_2 = 500000.0
FFN_DENSE = 2816
N_EXPERTS = 8
TOP_K = 2
FFN_EXPERT = 3584
NORM_EPS = 1e-6


def _rmsnorm(x, gain, eps=NORM_EPS):
    xf = x.astype(jnp.float32)
    y = xf * lax.rsqrt(jnp.mean(xf * xf, axis=-1, keepdims=True) + eps)
    return (y * gain.astype(jnp.float32)).astype(x.dtype)

def _swiglu(h, w_gate, w_up, w_down):
    return (jax.nn.silu(h @ w_gate) * (h @ w_up)) @ w_down

def _spatial_gating_mixer(h, w_in, v_gain, w_spatial, b_spatial, w_out):
    B, S, _ = h.shape
    z = jax.nn.gelu(h @ w_in)
    u, v = jnp.split(z, 2, axis=-1)
    v = _rmsnorm(v, v_gain)
    n_chunks = S // SG_CHUNK
    cg = SG_WIDTH // SG_GROUPS
    v = v.reshape(B, n_chunks, SG_CHUNK, SG_GROUPS, cg)
    causal = jnp.tril(jnp.ones((SG_CHUNK, SG_CHUNK), dtype=w_spatial.dtype))
    w_masked = w_spatial * causal[None]
    mixed = jnp.einsum('gts,bnsgc->bntgc', w_masked, v) + b_spatial.T[None, None, :, :, None]
    y = u * mixed.reshape(B, S, SG_WIDTH)
    return y @ w_out

def _rope_tables(positions):
    inv_freq = 1.0 / (ROPE_THETA_2 ** (jnp.arange(0, ROT_DIM, 2, dtype=jnp.float32) / ROT_DIM))
    ang = positions.astype(jnp.float32)[..., None] * inv_freq
    return jnp.cos(ang), jnp.sin(ang)

def _partial_rope(x, cos, sin):
    half = ROT_DIM // 2
    xf = x.astype(jnp.float32)
    x1 = xf[..., :half]
    x2 = xf[..., half:ROT_DIM]
    out = jnp.concatenate([x1 * cos - x2 * sin, x2 * cos + x1 * sin, xf[..., ROT_DIM:]], axis=-1)
    return out.astype(x.dtype)

def _diff_attention(h, positions, w_qkv, q_gain, k_gain, lam_q1, lam_k1, lam_q2, lam_k2,
                    subln_gain, w_out, lambda_init):
    B, S, _ = h.shape
    H, Dh = DA_HEADS, DA_HEAD_DIM
    qkv = h @ w_qkv
    q, k, v = jnp.split(qkv, 3, axis=-1)
    q = _rmsnorm(q.reshape(B, S, H, 2, Dh), q_gain)
    k = _rmsnorm(k.reshape(B, S, H, 2, Dh), k_gain)
    v = v.reshape(B, S, H, 2 * Dh)
    cos, sin = _rope_tables(positions)
    cos = cos[:, :, None, None, :]
    sin = sin[:, :, None, None, :]
    q = _partial_rope(q, cos, sin)
    k = _partial_rope(k, cos, sin)

    f32 = jnp.float32
    lam = (jnp.exp(jnp.sum(lam_q1.astype(f32) * lam_k1.astype(f32)))
           - jnp.exp(jnp.sum(lam_q2.astype(f32) * lam_k2.astype(f32))) + lambda_init)
    scale = 1.0 / math.sqrt(Dh)

    n_blocks = S // Q_BLOCK
    k_t = k.transpose(0, 2, 3, 1, 4)
    v_t = v.transpose(0, 2, 1, 3)
    q_b = q.transpose(0, 2, 3, 1, 4).reshape(B, H, 2, n_blocks, Q_BLOCK, Dh)
    q_b = jnp.moveaxis(q_b, 3, 0)
    key_pos = jnp.arange(S)[None, :]

    def block(args):
        q_blk, blk = args
        s = jnp.einsum('bhcqd,bhckd->bhcqk', q_blk, k_t,
                       preferred_element_type=jnp.float32) * scale
        q_pos = blk * Q_BLOCK + jnp.arange(Q_BLOCK)[:, None]
        s = jnp.where(key_pos <= q_pos, s, -jnp.inf)
        p = jax.nn.softmax(s, axis=-1)
        a = (p[:, :, 0] - lam * p[:, :, 1]).astype(v_t.dtype)
        return jnp.einsum('bhqk,bhkd->bhqd', a, v_t)

    o = lax.map(block, (q_b, jnp.arange(n_blocks)))
    o = o.transpose(1, 0, 3, 2, 4).reshape(B, S, H, 2 * Dh)
    o = (_rmsnorm(o, subln_gain).astype(jnp.float32) * (1.0 - lambda_init)).astype(h.dtype)
    return o.reshape(B, S, H * 2 * Dh) @ w_out

def _moe_swiglu(h, w_router, w_gate, w_up, w_down):
    logits = (h @ w_router).astype(jnp.float32)
    top_vals, top_idx = lax.top_k(logits, TOP_K)
    top_w = jax.nn.softmax(top_vals, axis=-1)
    gates = jnp.sum(jax.nn.one_hot(top_idx, N_EXPERTS, dtype=jnp.float32) * top_w[..., None], axis=-2)
    out = jnp.zeros_like(h)
    for e in range(N_EXPERTS):
        y = _swiglu(h, w_gate[e], w_up[e], w_down[e])
        out = out + gates[..., e:e + 1].astype(h.dtype) * y
    return out

def second_inputs(seed: int = 0) -> dict:
    key = jax.random.key(seed)
    ks = iter(jax.random.split(key, 40))
    f32 = jnp.float32

    def w(shape, fan_in):
        return jax.random.normal(next(ks), shape, f32) * (fan_in ** -0.5)

    def gain(shape):
        return 1.0 + 0.02 * jax.random.normal(next(ks), shape, f32)

    x = jax.random.normal(next(ks), (BATCH, SEQ, D_MODEL), f32)
    offset = jax.random.randint(next(ks), (BATCH, 1), 0, 1024, dtype=jnp.int32)
    positions = offset + jnp.arange(SEQ, dtype=jnp.int32)[None, :]
    qkv_width = 3 * DA_HEADS * 2 * DA_HEAD_DIM
    return {
        "x": x,
        "positions": positions,
        "l0_mix_norm": gain((D_MODEL,)),
        "l0_sg_w_in": w((D_MODEL, 2 * SG_WIDTH), D_MODEL),
        "l0_sg_v_norm": gain((SG_WIDTH,)),
        "l0_sg_w_spatial": w((SG_GROUPS, SG_CHUNK, SG_CHUNK), SG_CHUNK),
        "l0_sg_b_spatial": gain((SG_GROUPS, SG_CHUNK)),
        "l0_sg_w_out": w((SG_WIDTH, D_MODEL), SG_WIDTH),
        "l0_ffn_norm": gain((D_MODEL,)),
        "l0_ffn_w_gate": w((D_MODEL, FFN_DENSE), D_MODEL),
        "l0_ffn_w_up": w((D_MODEL, FFN_DENSE), D_MODEL),
        "l0_ffn_w_down": w((FFN_DENSE, D_MODEL), FFN_DENSE),
        "l1_mix_norm": gain((D_MODEL,)),
        "l1_da_w_qkv": w((D_MODEL, qkv_width), D_MODEL),
        "l1_da_q_norm": gain((DA_HEAD_DIM,)),
        "l1_da_k_norm": gain((DA_HEAD_DIM,)),
        "l1_da_lambda_q1": 0.1 * jax.random.normal(next(ks), (DA_HEAD_DIM,), f32),
        "l1_da_lambda_k1": 0.1 * jax.random.normal(next(ks), (DA_HEAD_DIM,), f32),
        "l1_da_lambda_q2": 0.1 * jax.random.normal(next(ks), (DA_HEAD_DIM,), f32),
        "l1_da_lambda_k2": 0.1 * jax.random.normal(next(ks), (DA_HEAD_DIM,), f32),
        "l1_da_subln": gain((2 * DA_HEAD_DIM,)),
        "l1_da_w_out": w((DA_HEADS * 2 * DA_HEAD_DIM, D_MODEL), DA_HEADS * 2 * DA_HEAD_DIM),
        "l1_moe_norm": gain((D_MODEL,)),
        "l1_moe_w_router": w((D_MODEL, N_EXPERTS), D_MODEL),
        "l1_moe_w_gate": w((N_EXPERTS, D_MODEL, FFN_EXPERT), D_MODEL),
        "l1_moe_w_up": w((N_EXPERTS, D_MODEL, FFN_EXPERT), D_MODEL),
        "l1_moe_w_down": w((N_EXPERTS, FFN_EXPERT, D_MODEL), FFN_EXPERT),
    }

def second_block(x, positions,
              l0_mix_norm, l0_sg_w_in, l0_sg_v_norm, l0_sg_w_spatial, l0_sg_b_spatial, l0_sg_w_out,
              l0_ffn_norm, l0_ffn_w_gate, l0_ffn_w_up, l0_ffn_w_down,
              l1_mix_norm, l1_da_w_qkv, l1_da_q_norm, l1_da_k_norm,
              l1_da_lambda_q1, l1_da_lambda_k1, l1_da_lambda_q2, l1_da_lambda_k2,
              l1_da_subln, l1_da_w_out,
              l1_moe_norm, l1_moe_w_router, l1_moe_w_gate, l1_moe_w_up, l1_moe_w_down):
    mixers = [
        (l0_mix_norm, (l0_sg_w_in, l0_sg_v_norm, l0_sg_w_spatial, l0_sg_b_spatial, l0_sg_w_out)),
        (l1_mix_norm, (l1_da_w_qkv, l1_da_q_norm, l1_da_k_norm, l1_da_lambda_q1, l1_da_lambda_k1,
                       l1_da_lambda_q2, l1_da_lambda_k2, l1_da_subln, l1_da_w_out)),
    ]
    channel = [
        (l0_ffn_norm, (l0_ffn_w_gate, l0_ffn_w_up, l0_ffn_w_down)),
        (l1_moe_norm, (l1_moe_w_router, l1_moe_w_gate, l1_moe_w_up, l1_moe_w_down)),
    ]
    h = x
    for i in range(DEPTH):
        norm_g, p = mixers[i]
        hn = _rmsnorm(h, norm_g)
        if i % 2 == 0:
            h = h + _spatial_gating_mixer(hn, *p)
        else:
            lambda_init = 0.8 - 0.6 * math.exp(-0.3 * i)
            h = h + _diff_attention(hn, positions, *p[:-1], p[-1], lambda_init)
        norm_g, p = channel[i]
        hn = _rmsnorm(h, norm_g)
        if i % 2 == 0:
            h = h + _swiglu(hn, *p)
        else:
            h = h + _moe_swiglu(hn, *p)
    return h


def setup_inputs(seed=0):
    out = dict(first_inputs(seed))
    for name, value in second_inputs(seed + 1).items():
        if name != "x":
            out[name + "_2"] = value
    return out


def reference(
    x, ev_w_in, ev_conv_w, ev_conv_b, ev_dt_bias, ev_a_log, ev_d_skip, ev_norm_g, ev_w_out,
    od_w_in, od_q_norm_g, od_w_q_up, od_kv_norm_g, od_w_kv_up, od_f_bias, od_w_out, ln1_g,
    ln1_b, ln2_g, ln2_b, moe_w_group, moe_b_group, moe_w_expert, moe_b_expert, moe_w_gate,
    moe_w_up, moe_w_down, positions_2, l0_mix_norm_2, l0_sg_w_in_2, l0_sg_v_norm_2,
    l0_sg_w_spatial_2, l0_sg_b_spatial_2, l0_sg_w_out_2, l0_ffn_norm_2, l0_ffn_w_gate_2,
    l0_ffn_w_up_2, l0_ffn_w_down_2, l1_mix_norm_2, l1_da_w_qkv_2, l1_da_q_norm_2,
    l1_da_k_norm_2, l1_da_lambda_q1_2, l1_da_lambda_k1_2, l1_da_lambda_q2_2, l1_da_lambda_k2_2,
    l1_da_subln_2, l1_da_w_out_2, l1_moe_norm_2, l1_moe_w_router_2, l1_moe_w_gate_2,
    l1_moe_w_up_2, l1_moe_w_down_2,
):
    x = first_block(
        x, ev_w_in, ev_conv_w, ev_conv_b, ev_dt_bias, ev_a_log, ev_d_skip, ev_norm_g, ev_w_out,
        od_w_in, od_q_norm_g, od_w_q_up, od_kv_norm_g, od_w_kv_up, od_f_bias, od_w_out, ln1_g,
        ln1_b, ln2_g, ln2_b, moe_w_group, moe_b_group, moe_w_expert, moe_b_expert, moe_w_gate,
        moe_w_up, moe_w_down,
    )
    return second_block(
        x, positions_2, l0_mix_norm_2, l0_sg_w_in_2, l0_sg_v_norm_2, l0_sg_w_spatial_2,
        l0_sg_b_spatial_2, l0_sg_w_out_2, l0_ffn_norm_2, l0_ffn_w_gate_2, l0_ffn_w_up_2,
        l0_ffn_w_down_2, l1_mix_norm_2, l1_da_w_qkv_2, l1_da_q_norm_2, l1_da_k_norm_2,
        l1_da_lambda_q1_2, l1_da_lambda_k1_2, l1_da_lambda_q2_2, l1_da_lambda_k2_2,
        l1_da_subln_2, l1_da_w_out_2, l1_moe_norm_2, l1_moe_w_router_2, l1_moe_w_gate_2,
        l1_moe_w_up_2, l1_moe_w_down_2,
    )


_drawn_inputs = setup_inputs


def setup_inputs(seed=0):
    import zlib

    import numpy as np

    out = dict(_drawn_inputs(seed))
    spreads = {}
    factors = {'ev_d_skip': 6.202,
     'ev_norm_g': 2.96,
     'od_q_norm_g': 8.0,
     'od_kv_norm_g': 8.0,
     'moe_b_group': 8.0,
     'moe_b_expert': 4.306,
     'l1_da_q_norm_2': 3.183,
     'l1_da_k_norm_2': 3.714,
     'l1_da_lambda_q1_2': 2.964,
     'l1_da_lambda_q2_2': 3.185,
     'l1_da_subln_2': 3.279,
     'l1_moe_norm_2': 3.969}
    for name, (base, spread) in spreads.items():
        noise = np.random.default_rng([zlib.crc32(name.encode()), seed]).standard_normal(out[name].shape)
        drawn = base * np.exp(spread * noise) if base else spread * noise
        out[name] = __import__('jax').numpy.asarray(drawn.astype(out[name].dtype))
    for name, factor in factors.items():
        out[name] = (out[name] * factor).astype(out[name].dtype)
    return out
```

```python
import math

import numpy as np

import concourse.bass as bass
from concourse import mybir

F32 = mybir.dt.float32
I32 = mybir.dt.int32
ALU = mybir.AluOpType
ACT = mybir.ActivationFunctionType
AX = mybir.AxisListType.X

P = 128
D = 1024
S = 256
T = S // P
DC = D // P
SSD_H, SSD_P, SSD_G, SSD_N = 16, 64, 2, 128
SSD_INNER = SSD_H * SSD_P
CONV_K = 4
CONV_DIM = SSD_INNER + 2 * SSD_G * SSD_N
CONV_C = CONV_DIM // P
SB_H = 8
HD = 64
SB_W = SB_H * HD
Q_RANK, KV_RANK, NOPE, ROPE, V_DIM = 256, 128, 64, 32, 64
MLA_H = 8
MLA_K = NOPE + ROPE
FOX_H = 8
FOX_W = FOX_H * HD
SG_W = 2 * D
SG_G = 8
SG_C = SG_W // SG_G
DA_H = 8
ROT = 16
BLK = 256
MOE_E, MOE_GRP = 16, 4
MOE2_E, MOE2_FF = 8, 3584
DENSE_FF = 2816
ALPHA = 4.0 ** 0.25
LN_EPS, RMS_EPS = 1e-5, 1e-6
LAMBDA_INIT = 0.8 - 0.6 * math.exp(-0.3)
NEG = -1.0e30
PW = 4096
PSLOTS = 2
ROPE_THETA, ROPE_THETA_2 = 10000.0, 500000.0


def shape_tables():
    inv = (np.float32(ROPE_THETA) ** (-(np.arange(0, ROPE, 2, dtype=np.float32) / np.float32(ROPE)))).astype(np.float32)
    ang = (np.arange(S, dtype=np.float32)[:, None] * inv[None, :]).astype(np.float32)
    inv2 = (np.float32(1.0) / (np.float32(ROPE_THETA_2) ** (np.arange(0, ROT, 2, dtype=np.float32) / np.float32(ROT)))).astype(np.float32)
    return np.concatenate([np.cos(ang), np.sin(ang), np.tile(inv2[None, :], (S, 1))], axis=1).astype(np.float32)


def build(nc, w, out):
    sems = {}

    def sem(name):
        if name not in sems:
            sems[name] = nc.alloc_semaphore(name)
        return sems[name]

    def sb(name, shape, dt=F32):
        return nc.alloc_sbuf_tensor(name, shape, dt).ap()

    h = sb("h", [P, T, D])
    xT = sb("xT", [P, DC, S])
    ffw_g = sb("ffw_g", [P, 2, DC, BLK])
    ffw_u = sb("ffw_u", [P, 2, DC, BLK])
    ffw_d = sb("ffw_d", [P, 2, BLK // P, D])
    pieces = sb("pieces", [P, PSLOTS, PW])
    norm_vec = sb("norm_vec", [P, 2 * D])
    ident = sb("ident", [P, P])
    ones = sb("ones", [P, P])
    upto = sb("upto", [P, P])
    above = sb("above", [P, P])
    atleast = sb("atleast", [P, P])
    mask_causal = sb("mask_causal", [P, 3, P])
    mask_strict = sb("mask_strict", [P, 3, P])
    keep_strict = sb("keep_strict", [P, 3, P])
    ARENA = 22312
    SMALL = 896
    arena = sb("arena", [P, ARENA])
    small = sb("small", [P, SMALL])

    psum = [nc.alloc_psum_tensor(f"bank{i}", [P, 512], F32).ap() for i in range(8)]

    par = {}
    par_loads = []

    def param(name, shape, src, dt=F32):
        par[name] = sb("par_" + name, shape, dt)
        par_loads.append((par[name], src))

    def bcast(v):
        return v.partition_broadcast(P)

    param("conv_w", [P, CONV_K, CONV_C], w["ev_conv_w"][0].rearrange("k (c p) -> p k c", p=P))
    param("conv_b", [P, CONV_C], w["ev_conv_b"][0].rearrange("(c p) -> p c", p=P))
    param("dt_bias", [P, SSD_H], bcast(w["ev_dt_bias"][0]))
    param("a_log", [P, SSD_H], bcast(w["ev_a_log"][0]))
    param("d_skip", [P, SSD_H], bcast(w["ev_d_skip"][0]))
    param("ssd_norm", [P, 2, 4], w["ev_norm_g"][0].rearrange("(k p c) -> p k c", k=2, c=4))
    param("q_norm", [P, 2], w["od_q_norm_g"][0].rearrange("(c p) -> p c", p=P))
    param("kv_norm", [P, 1], w["od_kv_norm_g"][0].rearrange("(c p) -> p c", p=P))
    param("f_bias", [P, FOX_H], bcast(w["od_f_bias"][0]))
    for i in range(2):
        param(f"route_b{i}", [P, 20], None)
        par_loads.pop()
        par_loads.append((par[f"route_b{i}"][:, 0:4], bcast(w["moe_b_group"][i])))
        par_loads.append((par[f"route_b{i}"][:, 4:20], bcast(w["moe_b_expert"][i])))
        param(f"route_w{i}", [P, DC, 20], None)
        par_loads.pop()
        par_loads.append((par[f"route_w{i}"][:, :, 0:4], w["moe_w_group"][i].rearrange("(p c) n -> p c n", c=DC)))
        par_loads.append((par[f"route_w{i}"][:, :, 4:20], w["moe_w_expert"][i].rearrange("(p c) n -> p c n", c=DC)))
    param("route_w2", [P, DC, MOE2_E], w["l1_moe_w_router_2"].rearrange("(p c) n -> p c n", c=DC))
    for name in ("l0_mix_norm_2", "l0_ffn_norm_2", "l1_mix_norm_2", "l1_moe_norm_2"):
        param(name, [P, DC], w[name].rearrange("(p c) -> p c", c=DC))
    param("b_spatial", [P, SG_G], w["l0_sg_b_spatial_2"].rearrange("g t -> t g"))
    param("da_q_norm", [P, HD], bcast(w["l1_da_q_norm_2"]))
    param("da_k_norm", [P, HD], bcast(w["l1_da_k_norm_2"]))
    param("lam", [P, 4, HD], None)
    par_loads.pop()
    for i, name in enumerate(("q1", "k1", "q2", "k2")):
        par_loads.append((par["lam"][:, i, :], bcast(w[f"l1_da_lambda_{name}_2"])))
    param("subln", [P, P], bcast(w["l1_da_subln_2"]))
    param("tables", [P, T, 40], w["tables"].rearrange("(j p) n -> p j n", p=P))
    param("positions", [P, T], w["positions_2"].rearrange("a (j p) -> p (a j)", p=P), I32)

    piece_list = []

    def piece(src, shape):
        piece_list.append((src, shape))
        return len(piece_list) - 1

    def piece_ap(n):
        shape = piece_list[n][1]
        size = int(np.prod(shape[1:]))
        flat = pieces[:, n % PSLOTS, 0:size]
        if len(shape) == 2:
            return flat
        return flat.rearrange("p (a b) -> p a b", a=shape[1])

    def columns(mat, c0, c1):
        return piece(mat[:, c0:c1].rearrange("(p c) n -> p c n", c=DC), [P, DC, c1 - c0])

    def rows(mat, k):
        return piece(mat[512 * k:512 * (k + 1), :].rearrange("(p c) n -> p c n", c=4), [P, 4, D])

    ev = w["ev_w_in"][0]
    o = SSD_INNER
    even_pieces = [("z", "tok", columns(ev, 0, 512), 512), ("z", "tok", columns(ev, 512, 1024), 512)]
    even_pieces += [("xbc", "feat", columns(ev, o + 512 * i, o + 512 * (i + 1)), 512) for i in range(3)]
    o += CONV_DIM
    even_pieces += [("dt", "tok", columns(ev, o, o + SSD_H), SSD_H)]
    o += SSD_H
    even_pieces += [("q", "feat", columns(ev, o, o + 512), 512), ("k", "feat", columns(ev, o + 512, o + 1024), 512),
                    ("v", "tok", columns(ev, o + 1024, o + 1536), 512)]
    even_out = [rows(w["ev_w_out"][0], k) for k in range(3)]
    EVEN_END = len(piece_list)
    od = w["od_w_in"][0]
    o = Q_RANK + KV_RANK + ROPE
    odd_pieces = [("c", "tok", columns(od, 0, o), o), ("q", "feat", columns(od, o, o + 512), 512),
                  ("k", "feat", columns(od, o + 512, o + 1024), 512),
                  ("v", "tok", columns(od, o + 1024, o + 1536), 512),
                  ("f", "tok", columns(od, o + 1536, o + 1536 + FOX_H), FOX_H)]
    odd_qup = piece(w["od_w_q_up"][0].rearrange("(c p) n -> p c n", p=P), [P, 2, MLA_H * MLA_K])
    odd_kvup = piece(w["od_w_kv_up"][0], [P, MLA_H * (NOPE + V_DIM)])
    odd_out = [rows(w["od_w_out"][0], k) for k in range(2)]
    ODD_END = len(piece_list)
    sg_in = w["l0_sg_w_in_2"]
    sg_pieces = [("z", "tok", columns(sg_in, 512 * i, 512 * (i + 1)), 512) for i in range(8)]
    sg_spatial = piece(w["l0_sg_w_spatial_2"].rearrange("g t s -> t g s"), [P, SG_G, P])
    sg_out = [rows(w["l0_sg_w_out_2"], k) for k in range(4)]
    SG_END = len(piece_list)
    qkv = w["l1_da_w_qkv_2"]
    da_pieces = [("qkv", "tok", columns(qkv, 512 * i, 512 * (i + 1)), 512) for i in range(6)]
    da_out = [rows(w["l1_da_w_out_2"], k) for k in range(2)]
    DA_END = len(piece_list)

    FIRST_P, FIRST_O, PHASE, MIXER = {}, {}, {}, {}
    at_p = at_o = 0
    for k, (t, plan, outs) in enumerate((("ev", even_pieces, even_out), ("od", odd_pieces, odd_out),
                                         ("sg", sg_pieces, sg_out), ("da", da_pieces, da_out))):
        FIRST_P[t], FIRST_O[t], MIXER[t] = at_p, at_o, k
        at_p, at_o = at_p + len(plan), at_o + len(outs)
    for k, t in enumerate(("ev", "m0", "od", "m1", "sg", "ff", "da", "m2")):
        PHASE[t] = k
    FIRST_U = {"mla": 0, "fox": MLA_H, "dat": MLA_H + FOX_H}
    ROUTER = {"m0": 0, "m1": 1, "m2": 2}

    def full_wait(eng, t, half, n):
        eng.wait_ge(sem(f"bank{half}_full"), FIRST_P[t] + n + 1)

    def read_wait(eng, t, half, n):
        eng.wait_ge(sem(f"bank{half}_read"), FIRST_P[t] + n)

    released = {}
    for t, plan, outs in (("ev", even_pieces, even_out), ("od", odd_pieces, odd_out), ("sg", sg_pieces, sg_out),
                          ("da", da_pieces, da_out)):
        for k, (_, _, n, _) in enumerate(plan):
            released[n] = ("bank1_full", FIRST_P[t] + k + 1)
        for k, n in enumerate(outs):
            released[n] = ("out_piece", FIRST_O[t] + k + 1)
    released[odd_qup], released[odd_kvup] = ("od_qup", 1), ("od_kvup", 1)
    released[sg_spatial] = ("sg_w_turned", 1)

    def piece_wait(eng, n):
        eng.wait_ge(sem(f"piece_landed{n % PSLOTS}"), 16 * (n // PSLOTS + 1))

    counts = {"dve": 0, "act": 0}

    def vlink(ins, *also):
        counts["dve"] += 1
        ins.then_inc(sem("vector_step"), 1)
        nc.vector.wait_ge(sem("vector_step"), counts["dve"])
        for s in also:
            nc.vector.sem_inc(s, 1)

    V = nc.vector

    arena_used = []

    def minus_abs(dst, x):
        return V.scalar_tensor_tensor(out=dst, in0=x, scalar=-1.0, in1=x, op0=ALU.mult, op1=ALU.min)

    def carver():
        used = [0]

        def carve(*shape):
            size = int(np.prod(shape))
            at = used[0]
            used[0] += size
            assert used[0] <= ARENA, used[0]
            arena_used.append(used[0])
            flat = arena[:, at:at + size]
            if len(shape) == 1:
                return flat
            names = "abcd"[:len(shape)]
            return flat.rearrange(f"p ({' '.join(names)}) -> p {' '.join(names)}",
                                  **{n: s for n, s in zip(names, shape)})
        return carve

    small_at = [0]

    def tiny(*shape):
        size = int(np.prod(shape))
        at = small_at[0]
        small_at[0] += size
        assert small_at[0] <= SMALL, small_at[0]
        flat = small[:, at:at + size]
        if len(shape) == 1:
            return flat
        names = "abcd"[:len(shape)]
        return flat.rearrange(f"p ({' '.join(names)}) -> p {' '.join(names)}",
                              **{n: s for n, s in zip(names, shape)})

    def over(ap, axis, n):
        a = ap.unsqueeze(axis)
        shape = list(a.shape)
        shape[axis] = n
        return a.to_broadcast(shape)

    stats, moments = tiny(T, 2, 6), tiny(T, 2)
    sq, rstd = tiny(T), tiny(T)
    root_y, root_t = tiny(T * 2 * 16), tiny(T * 2 * 16)
    roots = {"asked": 0, "answered": 0}

    def rsqrt_scalar(act, x, n):
        roots["answered"] += 1
        act.wait_ge(sem("root_asked"), roots["answered"])
        nc.scalar.activation(root_y[:, 0:n], x, ACT.Ln).then_inc(sem("root_ln"), 1)
        act.wait_ge(sem("root_ln"), roots["answered"])
        nc.scalar.activation(root_y[:, 0:n], root_y[:, 0:n], ACT.Exp, scale=-0.5).then_inc(sem("root_found"), 1)

    def rsqrt_vector(x, dst, n):
        roots["asked"] += 1
        V.sem_inc(sem("root_asked"), 1)
        V.wait_ge(sem("root_found"), roots["asked"])
        y, u = root_y[:, 0:n], root_t[:, 0:n]
        vlink(V.tensor_tensor(u, y, y, ALU.mult))
        vlink(V.tensor_tensor(u, u, x, ALU.mult))
        vlink(V.tensor_scalar(u, u, -0.5, 1.5, ALU.mult, ALU.add))
        vlink(V.tensor_tensor(dst, u, y, ALU.mult))

    def layer_norm():
        for j in range(T):
            for k in range(2):
                vlink(V.bn_stats(out=stats[:, j, k, :], in_=h[:, j, 512 * k:512 * (k + 1)]))
            vlink(V.bn_aggr(out=moments[:, j, :], in_=stats[:, j]))
        vlink(V.tensor_scalar(sq, moments[:, :, 1], LN_EPS, None, ALU.add))
        rsqrt_vector(sq, rstd, T)
        for j in range(T):
            vlink(V.tensor_scalar(h[:, j, :], h[:, j, :], moments[:, j, 0:1], rstd[:, j:j + 1], ALU.subtract, ALU.mult))
            vlink(V.tensor_tensor(h[:, j, :], h[:, j, :], norm_vec[:, 0:D], ALU.mult))
            vlink(V.tensor_tensor(h[:, j, :], h[:, j, :], norm_vec[:, D:2 * D], ALU.add))

    def rms_scale(src, junk, n, scale_out):
        for j in range(T):
            vlink(V.tensor_tensor_reduce(out=junk, in0=src[:, j, :], in1=src[:, j, :], scale=1.0, scalar=0.0,
                                         op0=ALU.mult, op1=ALU.add, accum_out=sq[:, j:j + 1]))
        vlink(V.tensor_scalar(sq, sq, 1.0 / n, RMS_EPS, ALU.mult, ALU.add))
        rsqrt_vector(sq, scale_out, T)

    def to_features_tensor(pe, t, src):
        for c in range(DC):
            for j in range(T):
                bank = psum[c // 2]
                last = nc.tensor.transpose(bank[:, (c % 2) * S + j * P:(c % 2) * S + (j + 1) * P],
                                           src[:, j, :].rearrange("t (p c) -> t c p", c=DC)[:, c, :], ident)
            if c % 2:
                last.then_inc(sem("xt_turned"), 1)

    def to_features_vector(t, gain=None):
        for b in range(DC // 2):
            V.wait_ge(sem("xt_turned"), DC // 2 * PHASE[t] + b + 1)
            src = psum[b].rearrange("p (c t) -> p c t", c=2)
            if gain is None:
                ins = V.tensor_copy(xT[:, 2 * b:2 * b + 2, :], src)
            else:
                ins = V.tensor_tensor(xT[:, 2 * b:2 * b + 2, :], src, over(gain[:, 2 * b:2 * b + 2], 2, S), ALU.mult)
            vlink(ins, *([sem("xt_ready")] if b == DC // 2 - 1 else []))

    def project_tensor(pe, t, plan):
        pe.wait_ge(sem("xt_ready"), PHASE[t] + 1)
        for n, (_, kind, g, cols) in enumerate(plan):
            piece_wait(pe, g)
            if n >= 3:
                read_wait(pe, t, 0, n - 2)
                read_wait(pe, t, 1, n - 2)
            wt = piece_ap(g)
            for half in range(2):
                bank = psum[2 * (n % 3) + half]
                if kind == "tok":
                    for c in range(DC):
                        last = nc.tensor.matmul(bank[:, 0:cols], xT[:, c, half * P:(half + 1) * P], wt[:, c, :],
                                                start=(c == 0), stop=(c == DC - 1))
                else:
                    for m in range(2):
                        m0 = (2 * half + m) * P
                        for c in range(DC):
                            last = nc.tensor.matmul(bank[:, m * S:(m + 1) * S], wt[:, c, m0:m0 + P], xT[:, c, :],
                                                    start=(c == 0), stop=(c == DC - 1))
                last.then_inc(sem(f"bank{half}_full"), 1)

    def out_tensor(pe, t, mix, mixT, plan):
        pe.wait_ge(sem("mix_ready"), MIXER[t] + 1)
        g = 0
        for k in range(len(plan)):
            for c in range(4):
                for j in range(T):
                    b = 4 + g // 4 % 2
                    if g % 4 == 0 and g >= 8:
                        pe.wait_ge(sem("mixt_read"), 2 * FIRST_O[t] + g // 4 - 1)
                    last = nc.tensor.transpose(psum[b][:, (g % 4) * P:(g % 4 + 1) * P],
                                               mix[:, j, 512 * k:512 * (k + 1)].rearrange("t (p c) -> t c p", c=4)[:, c, :],
                                               ident)
                    g += 1
                    if g % 4 == 0:
                        last.then_inc(sem("mixt_turned"), 1)
        for k, n in enumerate(plan):
            piece_wait(pe, n)
            pe.wait_ge(sem("mixt_read"), 2 * FIRST_O[t] + 2 * k + 2)
            wt = piece_ap(n)
            for j in range(T):
                for half in range(2):
                    for c in range(4):
                        last = nc.tensor.matmul(psum[2 * j + half], mixT[:, k, c, j * P:(j + 1) * P],
                                                wt[:, c, half * 512:(half + 1) * 512],
                                                start=(k == 0 and c == 0), stop=(k == len(plan) - 1 and c == 3))
            last.then_inc(sem("out_piece"), 1)

    def out_vector(t, mixT, n_pieces, scale, gain=None):
        for g in range(2 * n_pieces):
            V.wait_ge(sem("mixt_turned"), 2 * FIRST_O[t] + g + 1)
            k, c0 = g // 2, 2 * (g % 2)
            src = psum[4 + g % 2].rearrange("p (c t) -> p c t", c=2)
            dst = mixT[:, k, c0:c0 + 2, :]
            if gain is not None and k < gain.shape[1]:
                ins = V.tensor_tensor(dst, src, over(gain[:, k, c0:c0 + 2], 2, S), ALU.mult)
            else:
                ins = V.tensor_copy(dst, src)
            ins.then_inc(sem("mixt_read"), 1)
        V.wait_ge(sem("out_piece"), FIRST_O[t] + n_pieces)
        for j in range(T):
            for half in range(2):
                hv = h[:, j, half * 512:(half + 1) * 512]
                vlink(V.scalar_tensor_tensor(out=hv, in0=hv, scalar=scale, in1=psum[2 * j + half],
                                             op0=ALU.mult, op1=ALU.add))

    TRI = [(0, 0), (1, 0), (1, 1)]

    def attention_tensor(pe, t, units, logits, probs, probsT, value, dv):
        U0 = FIRST_U[t]
        for u in range(units + 2):
            if u < units:
                if u >= 2:
                    pe.wait_ge(sem("at_masked"), U0 + u - 1)
                logits(u, psum[u % 2]).then_inc(sem("at_logits"), 1)
            if 1 <= u <= units:
                v = u - 1
                pe.wait_ge(sem("at_probs"), U0 + v + 1)
                if v >= 2:
                    pe.wait_ge(sem("at_probst"), U0 + v - 1)
                for i in range(3):
                    last = nc.tensor.transpose(psum[2 + v % 2][:, i * P:(i + 1) * P], probs[:, v % 2, i, :], ident)
                last.then_inc(sem("at_turned"), 1)
            if u >= 2:
                v = u - 2
                pe.wait_ge(sem("at_probst"), U0 + v + 1)
                if v >= 2:
                    pe.wait_ge(sem("at_written"), U0 + v - 1)
                for i, (j, s) in enumerate(TRI):
                    last = nc.tensor.matmul(psum[4 + v % 2][:, j * dv:(j + 1) * dv], probsT[:, v % 2, i, :], value(v, s),
                                            start=(s == 0), stop=(s == j))
                last.then_inc(sem("at_outputs"), 1)

    def attention_scalar(act, t, units, scale, masked, nbias, probs, sums, probsT):
        U0 = FIRST_U[t]
        for u in range(units + 1):
            if u < units:
                act.wait_ge(sem("at_masked"), U0 + u + 1)
                if u >= 2:
                    act.wait_ge(sem("at_turned"), U0 + u - 1)
                for j, (a, b) in enumerate(((0, 1), (1, 3))):
                    ins = nc.scalar.activation(probs[:, u % 2, a:b, :], masked[:, u % 2, a:b, :], ACT.Exp,
                                               bias=nbias[:, u, j:j + 1], scale=scale, accum_out=sums[:, u, j:j + 1])
                ins.then_inc(sem("at_probs"), 1)
            if u >= 1:
                v = u - 1
                act.wait_ge(sem("at_turned"), U0 + v + 1)
                if v >= 2:
                    act.wait_ge(sem("at_outputs"), U0 + v - 1)
                nc.scalar.copy(probsT[:, v % 2, :, :], psum[2 + v % 2][:, 0:3 * P].rearrange("p (i t) -> p i t", i=3))\
                    .then_inc(sem("at_probst"), 1)

    def attention_vector(t, units, scale, mask_of, masked, nbias, sums, write):
        U0 = FIRST_U[t]
        for u in range(units + 1):
            if u < units:
                V.wait_ge(sem("at_logits"), U0 + u + 1)
                if u >= 2:
                    V.wait_ge(sem("at_probs"), U0 + u - 1)
                z = psum[u % 2][:, 0:3 * P].rearrange("p (i s) -> p i s", i=3)
                mask = mask_of(u)
                for j, (a, b) in enumerate(((0, 1), (1, 3))):
                    vlink(V.tensor_tensor_reduce(out=masked[:, u % 2, a:b, :], in0=z[:, a:b, :], in1=mask[:, a:b, :],
                                                 scale=1.0, scalar=-3.0e38, op0=ALU.add, op1=ALU.max,
                                                 accum_out=nbias[:, u, j:j + 1]))
                vlink(V.tensor_scalar(nbias[:, u, :], nbias[:, u, :], -scale, None, ALU.mult), sem("at_masked"))
            if u >= 1:
                v = u - 1
                V.wait_ge(sem("at_outputs"), U0 + v + 1)
                vlink(V.reciprocal(sums[:, v, :], sums[:, v, :]))
                write(v, psum[4 + v % 2], sums[:, v, :], sem("at_written"))

    def setup_gpsimd(pool):
        for ap, src in par_loads:
            pool.dma_start(ap, src, allow_slow_non_contiguous=True).then_inc(sem("params_landed"), 16)
        g = nc.gpsimd
        for m, v in ((ident, 0.0), (ones, 1.0), (upto, 1.0), (above, 1.0), (atleast, 1.0), (mask_causal, 0.0),
                     (mask_strict, 0.0), (keep_strict, 1.0)):
            last = g.memset(m, v)
        last.then_inc(sem("const_filled"), 1)
        pool.wait_ge(sem("const_filled"), 1)

        def select(m, op, fill, cm, step, base=0):
            return g.affine_select(out=m, in_=m, compare_op=op, fill=fill, base=base, pattern=[[step, P]],
                                   channel_multiplier=cm)
        select(ident, ALU.not_equal, 1.0, 1, -1)
        select(upto, ALU.is_ge, 0.0, -1, 1)
        select(above, ALU.is_gt, 0.0, 1, -1)
        select(atleast, ALU.is_ge, 0.0, 1, -1)
        for i in (0, 2):
            select(mask_causal[:, i, :], ALU.is_ge, NEG, 1, -1)
            select(mask_strict[:, i, :], ALU.is_gt, NEG, -1, 1)
            last = select(keep_strict[:, i, :], ALU.is_gt, 0.0, -1, 1)
        last.then_inc(sem("const_ready"), 1)

    def norm_loads_gpsimd(pool):
        plan = [(None, w["ln1_g"][0], w["ln1_b"][0]), (1, w["ln2_g"][0], w["ln2_b"][0]),
                (2, w["ln1_g"][1], w["ln1_b"][1]), (3, w["ln2_g"][1], w["ln2_b"][1]),
                (4, w["l0_sg_v_norm_2"], None)]
        for phase, a, b in plan:
            if phase is not None:
                pool.wait_ge(sem("phase_done"), phase)
            if b is None:
                a, b = a[0:D], a[D:2 * D]
            pool.dma_start(norm_vec[:, 0:D], bcast(a)).then_inc(sem("norm_landed"), 16)
            pool.dma_start(norm_vec[:, D:2 * D], bcast(b)).then_inc(sem("norm_landed"), 16)

    ca = carver()
    zs = ca(T, SSD_INNER)
    xp_flat = ca(CONV_C * (S + CONV_K - 1))
    xp = xp_flat.rearrange("p (c t) -> p c t", c=CONV_C)
    xc = ca(CONV_C, S)
    sbq, sbk, sbv = ca(4, S), ca(4, S), ca(T, SB_W)
    xs_tok, xdt = ca(T, SSD_INNER), ca(T, SSD_INNER)
    ev_mix = ca(T, SSD_INNER + SB_W)
    b_tok = ca(T, SSD_G, P)
    cbm = ca(T, SSD_G, P)
    steps = ca(2, 4, P)
    decay = ca(2, 4, P)
    sb_w = ca(2, 3, P)
    sb_e = xc[:, 0:3, :].rearrange("p c t -> p (c t)").rearrange("p (b i t) -> p b i t", b=2, i=3)
    sb_l = xc[:, 3:6, :].rearrange("p c t -> p (c t)").rearrange("p (b i t) -> p b i t", b=2, i=3)
    ev_mixT = xp_flat[:, 0:3 * 4 * S].rearrange("p (k c t) -> p k c t", k=3, c=4)
    xdd = xT[:, 0:4, :].rearrange("p c t -> p (c t)")
    state = xT[:, 4:8, :].rearrange("p c t -> p (c t)")
    dt_raw, dt, dt_e, da = tiny(T, SSD_H), tiny(T, SSD_H), tiny(T, SSD_H), tiny(T, SSD_H)
    a_neg = tiny(SSD_H)
    carry = tiny(2, T, SSD_H)
    y_bank = {(0, 0): 2, (0, 1): 3, (1, 0): 0, (1, 1): 1}

    def even_tensor(pe):
        t = "ev"
        pe.wait_ge(sem("const_ready"), 1)
        pe.wait_ge(sem("x_landed"), 16)
        to_features_tensor(pe, t, h)
        project_tensor(pe, t, even_pieces)
        groups = [[(j, 4 * k + c) for c in range(4)] for k in range(2) for j in range(T)]
        groups.append([(j, 8 + g) for j in range(T) for g in range(SSD_G)])
        pe.wait_ge(sem("ev_conv_out"), CONV_C)
        for n, group in enumerate(groups):
            if n >= 2:
                pe.wait_ge(sem("ev_tok_read"), n - 1)
            for i, (j, c) in enumerate(group):
                last = nc.tensor.transpose(psum[6 + n % 2][:, i * P:(i + 1) * P], xc[:, c, j * P:(j + 1) * P], ident)
            last.then_inc(sem("ev_tok_turned"), 1)
        read_wait(pe, "ev", 0, len(even_pieces))
        read_wait(pe, "ev", 1, len(even_pieces))
        for j in range(T):
            for g in range(SSD_G):
                i = j * SSD_G + g
                last = nc.tensor.matmul(psum[4][:, i * P:(i + 1) * P], xc[:, 8 + g, j * P:(j + 1) * P],
                                        xc[:, 10 + g, j * P:(j + 1) * P], start=True, stop=True)
        last.then_inc(sem("ev_cb"), 1)
        pe.wait_ge(sem("ev_da_ready"), 1)
        dav = da.rearrange("p j h -> p (j h)")
        nc.tensor.matmul(psum[5][:, 0:32], upto, dav, start=True, stop=True)
        nc.tensor.matmul(psum[5][:, 32:64], above, dav, start=True, stop=True).then_inc(sem("ev_sums"), 1)
        pe.wait_ge(sem("ev_xdd_ready"), 1)
        for g in range(SSD_G):
            last = nc.tensor.matmul(psum[g], b_tok[:, 0, g, :], xdd[:, g * 512:(g + 1) * 512], start=True, stop=True)
        last.then_inc(sem("ev_state_full"), 1)
        for s in range(9):
            if s < 8:
                j, q = divmod(s, 4)
                pe.wait_ge(sem("ev_steps"), s + 1)
                if s >= 2:
                    pe.wait_ge(sem("ev_decay"), s - 1)
                for i in range(4):
                    last = nc.tensor.matmul(psum[6 + s % 2][:, i * P:(i + 1) * P], steps[:, s % 2, i, :], upto,
                                            start=True, stop=True)
                last.then_inc(sem("ev_seg"), 1)
            if s >= 1:
                j, q = divmod(s - 1, 4)
                pe.wait_ge(sem("ev_weights"), s)
                if s - 1 == 4:
                    pe.wait_ge(sem("ev_state"), 1)
                for i in range(4):
                    head = 4 * q + i
                    b = psum[y_bank[j, q // 2]]
                    last = nc.tensor.matmul(b[:, (q % 2) * 256 + i * 64:(q % 2) * 256 + (i + 1) * 64],
                                            decay[:, (s - 1) % 2, i, :], xdt[:, j, head * 64:(head + 1) * 64],
                                            start=True, stop=True)
                last.then_inc(sem("ev_diag"), 1)
        for g in range(SSD_G):
            last = nc.tensor.matmul(psum[4 + g], xc[:, 10 + g, P:S], state[:, g * 512:(g + 1) * 512], start=True, stop=True)
        last.then_inc(sem("ev_off"), 1)
        pe.wait_ge(sem("ev_ssd_read"), 1)
        for s in range(SB_H + 2):
            if s < SB_H:
                if s >= 2:
                    pe.wait_ge(sem("ev_sb_expo"), s - 1)
                r = slice((s % 2) * 64, (s % 2) * 64 + 64)
                kk, qq = sbk[r, s // 2, :], sbq[r, s // 2, :]
                nc.tensor.matmul(psum[s % 2][:, 0:S], kk[:, 0:P], qq, start=True, stop=True)
                nc.tensor.matmul(psum[s % 2][:, S:3 * P], kk[:, P:S], qq[:, P:S], start=True, stop=True)\
                    .then_inc(sem("ev_sb_z"), 1)
            if 1 <= s <= SB_H:
                v = s - 1
                pe.wait_ge(sem("ev_sb_l"), v + 1)
                lv = sb_l[:, v % 2].rearrange("p i t -> p (i t)")
                cum = psum[2 + v % 2]
                nc.tensor.matmul(cum[:, 0:P], atleast, lv[:, 0:P], start=True, stop=True)
                nc.tensor.matmul(cum[:, P:S], atleast, lv[:, P:S], start=True, stop=False)
                nc.tensor.matmul(cum[:, P:S], ones, lv[:, S:3 * P], start=False, stop=True)
                nc.tensor.matmul(cum[:, S:3 * P], atleast, lv[:, S:3 * P], start=True, stop=True)\
                    .then_inc(sem("ev_sb_cum"), 1)
            if s >= 2:
                v = s - 2
                pe.wait_ge(sem("ev_sb_w"), v + 1)
                vc = slice(v * 64, (v + 1) * 64)
                nc.tensor.matmul(psum[4][:, vc], sb_w[:, v % 2, 0, :], sbv[:, 0, vc], start=True, stop=True)
                nc.tensor.matmul(psum[5][:, vc], sb_w[:, v % 2, 1, :], sbv[:, 0, vc], start=True, stop=False)
                nc.tensor.matmul(psum[5][:, vc], sb_w[:, v % 2, 2, :], sbv[:, 1, vc], start=False, stop=True)\
                    .then_inc(sem("ev_sb_out"), 1)
        out_tensor(pe, t, ev_mix, ev_mixT, even_out)

    def even_scalar(act):
        A = nc.scalar
        n = 0
        for n, (name, _, _, _) in enumerate(even_pieces):
            full_wait(act, "ev", 0, n)
            b0 = psum[2 * (n % 3)]
            if name == "z":
                A.activation(zs[:, 0, n * 512:(n + 1) * 512], b0, ACT.Silu).then_inc(sem("bank0_read"), 1)
            elif name == "xbc":
                c = 4 * (n - 2)
                A.copy(xp[:, c:c + 2, 3:], b0.rearrange("p (c t) -> p c t", c=2)).then_inc(sem("bank0_read"), 1)
            elif name == "dt":
                A.copy(dt_raw[:, 0, :], b0[:, 0:SSD_H]).then_inc(sem("bank0_read"), 1)
            elif name == "q":
                A.mul(sbq[:, 0:2, :], b0.rearrange("p (c t) -> p c t", c=2), HD ** -0.5)\
                    .then_inc(sem("bank0_read"), 1)
            elif name == "k":
                A.copy(sbk[:, 0:2, :], b0.rearrange("p (c t) -> p c t", c=2)).then_inc(sem("bank0_read"), 1)
            else:
                A.copy(sbv[:, 0, :], b0).then_inc(sem("bank0_read"), 1)
        read_wait(act, "ev", 1, 2)
        A.activation(zs[:, 1, :], zs[:, 1, :], ACT.Silu).then_inc(sem("ev_z_ready"), 1)
        for c in range(CONV_C):
            act.wait_ge(sem("ev_conv_sum"), c + 1)
            A.activation(xc[:, c, :], xc[:, c, :], ACT.Silu, bias=par["conv_b"][:, c:c + 1])\
                .then_inc(sem("ev_conv_out"), 1)
        act.wait_ge(sem("ev_dt_negabs"), 1)
        A.activation(dt_e, dt_e, ACT.Exp).then_inc(sem("ev_dt_exp"), 1)
        act.wait_ge(sem("ev_dt_exp"), 1)
        A.activation(dt_e, dt_e, ACT.Ln, bias=1.0).then_inc(sem("ev_dt_ln"), 1)
        A.activation(a_neg, par["a_log"], ACT.Exp).then_inc(sem("ev_a_exp"), 1)
        act.wait_ge(sem("ev_sums"), 1)
        A.activation(carry.rearrange("p a j h -> p (a j h)"), psum[5][:, 0:64], ACT.Exp).then_inc(sem("ev_carry"), 1)
        act.wait_ge(sem("ev_state_full"), 1)
        A.copy(state[:, 0:512], psum[0])
        A.copy(state[:, 512:1024], psum[1]).then_inc(sem("ev_state"), 1)
        for s in range(8):
            act.wait_ge(sem("ev_seg"), s + 1)
            if s >= 2:
                act.wait_ge(sem("ev_diag"), s - 1)
            A.activation(decay[:, s % 2], psum[6 + s % 2].rearrange("p (i l) -> p i l", i=4), ACT.Exp)\
                .then_inc(sem("ev_decay"), 1)
        for s in range(SB_H + 2):
            if s >= 2:
                v = s - 2
                act.wait_ge(sem("ev_sb_expo"), v + 1)
                A.activation(sb_w[:, v % 2], sb_w[:, v % 2], ACT.Exp).then_inc(sem("ev_sb_w"), 1)
            if s < SB_H:
                act.wait_ge(sem("ev_sb_z"), s + 1)
                if s >= 2:
                    act.wait_ge(sem("ev_sb_l"), s - 1)
                A.activation(sb_e[:, s % 2], psum[s % 2][:, 0:3 * P].rearrange("p (i t) -> p i t", i=3), ACT.Abs)\
                    .then_inc(sem("ev_sb_abs"), 1)
                act.wait_ge(sem("ev_sb_abs"), s + 1)
                A.activation(sb_e[:, s % 2], sb_e[:, s % 2], ACT.Exp, scale=-1.0).then_inc(sem("ev_sb_exp"), 1)
                act.wait_ge(sem("ev_sb_exp"), s + 1)
                A.activation(sb_e[:, s % 2], sb_e[:, s % 2], ACT.Ln, bias=1.0).then_inc(sem("ev_sb_ln"), 1)
        rsqrt_scalar(act, sq, T)
        rsqrt_scalar(act, sq, T)

    def even_vector(dve):
        V.memset(xp[:, :, 0:3], 0.0).then_inc(sem("ev_pad"), 1)
        dve.wait_ge(sem("ev_pad"), 1)
        to_features_vector("ev")
        dve.wait_ge(sem("params_landed"), 16 * len(par_loads))
        for n, (name, _, _, _) in enumerate(even_pieces):
            full_wait(dve, "ev", 1, n)
            b1 = psum[2 * (n % 3) + 1]
            b1c = b1.rearrange("p (c t) -> p c t", c=2)
            read = sem("bank1_read")
            if name == "z":
                vlink(V.tensor_copy(zs[:, 1, n * 512:(n + 1) * 512], b1), read)
            elif name == "xbc":
                c = 4 * (n - 2)
                vlink(V.tensor_copy(xp[:, c + 2:c + 4, 3:], b1c), read)
                read_wait(dve, "ev", 0, n + 1)
                for c in range(c, c + 4):
                    vlink(V.tensor_scalar(xc[:, c, :], xp[:, c, 0:S], par["conv_w"][:, 0, c:c + 1], None, ALU.mult))
                    for k in range(1, CONV_K):
                        vlink(V.scalar_tensor_tensor(out=xc[:, c, :], in0=xp[:, c, k:k + S],
                                                     scalar=par["conv_w"][:, k, c:c + 1], in1=xc[:, c, :],
                                                     op0=ALU.mult, op1=ALU.add),
                              *([sem("ev_conv_sum")] if k == CONV_K - 1 else []))
            elif name == "dt":
                vlink(V.tensor_copy(dt_raw[:, 1, :], b1[:, 0:SSD_H]), read)
            elif name == "q":
                vlink(V.tensor_scalar(sbq[:, 2:4, :], b1c, HD ** -0.5, None, ALU.mult), read)
            elif name == "k":
                vlink(V.tensor_copy(sbk[:, 2:4, :], b1c), read)
            else:
                vlink(V.tensor_copy(sbv[:, 1, :], b1), read)
        read_wait(dve, "ev", 0, 6)
        vlink(V.tensor_tensor(dt_raw, dt_raw, over(par["dt_bias"], 1, T), ALU.add))
        vlink(minus_abs(dt_e, dt_raw), sem("ev_dt_negabs"))
        dve.wait_ge(sem("ev_dt_ln"), 1)
        vlink(V.scalar_tensor_tensor(out=dt, in0=dt_raw, scalar=0.0, in1=dt_e, op0=ALU.max, op1=ALU.add))
        dve.wait_ge(sem("ev_a_exp"), 1)
        vlink(V.scalar_tensor_tensor(out=da, in0=dt, scalar=-1.0, in1=over(a_neg, 1, T), op0=ALU.mult, op1=ALU.mult),
              sem("ev_da_ready"))
        for n in range(5):
            dve.wait_ge(sem("ev_tok_turned"), n + 1)
            if n < 4:
                k, j = divmod(n, 2)
                vlink(V.tensor_copy(xs_tok[:, j, k * 512:(k + 1) * 512], psum[6 + n % 2]), sem("ev_tok_read"))
            else:
                vlink(V.tensor_copy(b_tok, psum[6].rearrange("p (j g n) -> p j g n", j=T, g=SSD_G)), sem("ev_tok_read"))
        dve.wait_ge(sem("ev_cb"), 1)
        vlink(V.tensor_tensor(cbm.rearrange("p j g l -> p (j g) l"), psum[4].rearrange("p (i l) -> p i l", i=4),
                              over(upto, 1, 4), ALU.mult))
        for j in range(T):
            vlink(V.tensor_tensor(xdt[:, j, :].rearrange("p (h d) -> p h d", d=SSD_P),
                                  xs_tok[:, j, :].rearrange("p (h d) -> p h d", d=SSD_P),
                                  over(dt[:, j, :], 2, SSD_P), ALU.mult))
        dve.wait_ge(sem("ev_carry"), 1)
        vlink(V.tensor_tensor(xdd.rearrange("p (h d) -> p h d", d=SSD_P),
                              xdt[:, 0, :].rearrange("p (h d) -> p h d", d=SSD_P),
                              over(carry[:, 1, 0, :], 2, SSD_P), ALU.mult), sem("ev_xdd_ready"))
        for s in range(9):
            if s < 8:
                j, q = divmod(s, 4)
                if s >= 2:
                    dve.wait_ge(sem("ev_seg"), s - 1)
                vlink(V.tensor_tensor(steps[:, s % 2], over(above, 1, 4), over(da[:, j, 4 * q:4 * q + 4], 2, P), ALU.mult),
                      sem("ev_steps"))
            if s >= 1:
                j, q = divmod(s - 1, 4)
                dve.wait_ge(sem("ev_decay"), s)
                vlink(V.tensor_tensor(decay[:, (s - 1) % 2], decay[:, (s - 1) % 2], over(cbm[:, j, q // 2, :], 1, 4),
                                      ALU.mult), sem("ev_weights"))
        dve.wait_ge(sem("ev_diag"), 8)
        dve.wait_ge(sem("ev_off"), 1)
        dve.wait_ge(sem("ev_z_ready"), 1)
        for j in range(T):
            for half in range(2):
                heads = slice(8 * half, 8 * half + 8)
                cols = slice(512 * half, 512 * half + 512)

                def by_head(ap):
                    return ap.rearrange("p (h d) -> p h d", d=SSD_P)
                y = ev_mix[:, j, cols]
                vlink(V.tensor_tensor(by_head(y), by_head(xs_tok[:, j, cols]), over(par["d_skip"][:, heads], 2, SSD_P),
                                      ALU.mult))
                vlink(V.tensor_tensor(y, y, psum[y_bank[j, half]], ALU.add))
                if j == 1:
                    off = xdt[:, 0, cols]
                    vlink(V.tensor_tensor(by_head(off), by_head(psum[4 + half]), over(carry[:, 0, 1, heads], 2, SSD_P),
                                          ALU.mult))
                    vlink(V.tensor_tensor(y, y, off, ALU.add))
                vlink(V.tensor_tensor(y, y, zs[:, j, cols], ALU.mult),
                      *([sem("ev_ssd_read")] if (j, half) == (1, 1) else []))
        for s in range(SB_H + 2):
            if s >= 2:
                v = s - 2
                dve.wait_ge(sem("ev_sb_cum"), v + 1)
                if v >= 2:
                    dve.wait_ge(sem("ev_sb_out"), v - 1)
                zv = psum[v % 2][:, 0:3 * P].rearrange("p (i t) -> p i t", i=3)
                cv = psum[2 + v % 2][:, 0:3 * P].rearrange("p (i t) -> p i t", i=3)
                vlink(V.tensor_copy(sb_w[:, v % 2], zv))
                vlink(V.tensor_tensor(sb_w[:, v % 2], sb_w[:, v % 2], cv, ALU.subtract))
                vlink(V.tensor_tensor(sb_w[:, v % 2], sb_w[:, v % 2], mask_strict, ALU.add), sem("ev_sb_expo"))
            if 1 <= s <= SB_H:
                v = s - 1
                dve.wait_ge(sem("ev_sb_ln"), v + 1)
                if v >= 2:
                    dve.wait_ge(sem("ev_sb_cum"), v - 1)
                zv = psum[v % 2][:, 0:3 * P].rearrange("p (i t) -> p i t", i=3)
                vlink(V.scalar_tensor_tensor(out=sb_l[:, v % 2], in0=zv, scalar=0.0, in1=sb_e[:, v % 2],
                                             op0=ALU.max, op1=ALU.add))
                vlink(V.tensor_tensor(sb_l[:, v % 2], sb_l[:, v % 2], keep_strict, ALU.mult), sem("ev_sb_l"))
        rms_scale(ev_mix[:, :, 0:SSD_INNER], xdt[:, 1, :], SSD_INNER, rstd)
        for j in range(T):
            vlink(V.tensor_scalar(ev_mix[:, j, 0:SSD_INNER], ev_mix[:, j, 0:SSD_INNER], rstd[:, j:j + 1], None, ALU.mult))
        dve.wait_ge(sem("ev_sb_out"), SB_H)
        for j in range(T):
            vlink(V.tensor_copy(ev_mix[:, j, SSD_INNER:], psum[4 + j]), *([sem("mix_ready")] if j else []))
        out_vector("ev", ev_mixT, 3, ALPHA, par["ssd_norm"])
        dve.wait_ge(sem("norm_landed"), 32)
        layer_norm()
        dve.sem_inc(sem("phase_done"), 1)

    ca = carver()
    ca(3 * D)
    sg_out_buf = ca(2, 2 * S)
    hidT = ca(2, 2, S)
    block_gate = tiny(2, T)
    gates = tiny(T, MOE_E)

    CREDIT = 2

    def free_slots_tensor(pe):
        for name in ("gate_done", "up_done", "hidden_ready"):
            pe.sem_inc(sem(name), CREDIT)
        for k in range(4):
            pe.sem_inc(sem(f"down_done{k}"), CREDIT)
            pe.sem_inc(sem(f"down_read{k}"), 1)

    def gate_up_tensor(pe, G, b, slot):
        for name, wt, bank0 in (("gate", ffw_g, 0), ("up", ffw_u, 2)):
            pe.wait_ge(sem(f"{name}_landed{slot}"), G["landed"])
            if name == "gate":
                pe.wait_ge(sem("hidden_ready"), G["n"] + 1)
            bank = psum[bank0 + slot]
            for f in range(2):
                for c in range(DC):
                    last = nc.tensor.matmul(bank[:, f * S:(f + 1) * S], wt[:, slot, c, f * P:(f + 1) * P], xT[:, c, :],
                                            start=(c == 0), stop=(c == DC - 1))
            last.then_inc(sem(f"{name}_done"), 1)

    def down_tensor(pe, G, slot):
        pe.wait_ge(sem(f"down_landed{slot}"), G["landed"])
        pe.wait_ge(sem("hidden_ready"), G["n"] + 1 + CREDIT)
        for j in range(T):
            for half in range(2):
                k = 2 * j + half
                pe.wait_ge(sem(f"down_read{k}"), G["n"] + 1)
                for f in range(2):
                    last = nc.tensor.matmul(psum[4 + k], hidT[:, slot, f, j * P:(j + 1) * P],
                                            ffw_d[:, slot, f, half * 512:(half + 1) * 512], start=(f == 0), stop=(f == 1))
                last.then_inc(sem(f"down_done{k}"), 1)

    def silu_scalar(act, G, slot):
        act.wait_ge(sem("gate_done"), G["n"] + 1 + CREDIT)
        act.wait_ge(sem("hidden_ready"), G["n"] + 1)
        nc.scalar.activation(sg_out_buf[:, slot, :], psum[slot], ACT.Silu).then_inc(sem("silu_done"), 1)

    def hidden_vector(dve, G, slot):
        dve.wait_ge(sem("silu_done"), G["n"] + 1)
        dve.wait_ge(sem("up_done"), G["n"] + 1 + CREDIT)
        V.tensor_tensor(hidT[:, slot].rearrange("p f t -> p (f t)"), sg_out_buf[:, slot, :], psum[2 + slot], ALU.mult)\
            .then_inc(sem("hidden_ready"), 1)

    def add_vector(dve, G, weight):
        for j in range(T):
            for half in range(2):
                k = 2 * j + half
                dve.wait_ge(sem(f"down_done{k}"), G["n"] + 1 + CREDIT)
                hv = h[:, j, half * 512:(half + 1) * 512]
                V.scalar_tensor_tensor(out=hv, in0=psum[4 + k], scalar=weight[:, j:j + 1], in1=hv,
                                       op0=ALU.mult, op1=ALU.add).then_inc(sem(f"down_read{k}"), 1)

    def number(base, b, i, e=0, per=0):
        n = base + b + 2 * i + per * e
        k = (base + b) // 2 + i + per // 2 * e
        return {"n": n, "landed": (k + 1) * 16}

    FFS = {
        "m0": (0, MOE_E, 1), "m1": (16, MOE_E, 1), "ff": (32, 1, DENSE_FF // BLK), "m2": (43, MOE2_E, MOE2_FF // BLK)}

    def blocks(eng, t, body, expert=None):
        base, E, B = FFS[t]
        if B == 1:
            with eng.Fori(0, E // 2) as i:
                body([(number(base, b, i), (base + b) % 2, 2 * i + b, 0) for b in range(2)])
        elif E == 1:
            with eng.Fori(0, B // 2) as i:
                body([(number(base, b, i), (base + b) % 2, 0, 2 * i + b) for b in range(2)])
            body([(number(base, B - 1, 0), (base + B - 1) % 2, 0, B - 1)])
        else:
            with eng.Fori(0, E) as e:
                if expert:
                    expert(e)
                with eng.Fori(0, B // 2) as i:
                    body([(number(base, b, i, e, B), (base + b) % 2, e, 2 * i + b) for b in range(2)])

    def ff_sync(sp, t, wg, wu, wd):
        base, E, B = FFS[t]

        def body(pair):
            for G, slot, e, b in pair:
                for name, wt, buf in (("gate", wg, ffw_g), ("up", wu, ffw_u)):
                    sp.wait_ge(sem(f"{name}_done"), G["n"] + 1)
                    src = wt[bass.ds(e, 1)].rearrange("a (p c) n -> p (a c) n", c=DC) if E > 1 else \
                        wt.rearrange("(p c) n -> p c n", c=DC)
                    if B > 1:
                        src = src[:, :, bass.ds(b * BLK, BLK)]
                    sp.dma_start(buf[:, slot], src).then_inc(sem(f"{name}_landed{slot}"), 16)
                sp.wait_ge(sem("down_done3"), G["n"] + 1)
                src = wd[bass.ds(e, 1)] if E > 1 else wd.unsqueeze(0)
                if B > 1:
                    src = src[:, bass.ds(b * BLK, BLK), :]
                sp.dma_start(ffw_d[:, slot], src.rearrange("a (f p) n -> p (a f) n", p=P))\
                    .then_inc(sem(f"down_landed{slot}"), 16)
        blocks(sp, t, body)

    def ff_tensor(pe, t, phase, route):
        pe.wait_ge(sem("phase_done"), phase)
        src = h
        if t in ("ff", "m2"):
            pe.wait_ge(sem("normed"), PHASE[t] - 3)
            src = normed
        to_features_tensor(pe, t, src)
        pe.wait_ge(sem("xt_ready"), PHASE[t] + 1)
        if route is not None:
            n = route.shape[2]
            for j in range(T):
                for c in range(DC):
                    last = nc.tensor.matmul(psum[4][:, 32 * j:32 * j + n], xT[:, c, j * P:(j + 1) * P], route[:, c, :],
                                            start=(c == 0), stop=(c == DC - 1))
            last.then_inc(sem("route_logits"), 1)
            pe.wait_ge(sem("route_logits_read"), ROUTER[t] + 1)

        def body(pair):
            for G, slot, _, _ in pair:
                gate_up_tensor(pe, G, 0, slot)
            for G, slot, _, _ in pair:
                down_tensor(pe, G, slot)
        blocks(pe, t, body)

    def ff_scalar(act, t):
        if t in ("ff", "m2"):
            rsqrt_scalar(act, sq, T)
        if t in FFR:
            act.wait_ge(sem("route_masked"), ROUTER[t] + 1)
            nc.scalar.activation(r_e, r_e, ACT.Exp).then_inc(sem("route_exp"), 1)
        blocks(act, t, lambda pair: [silu_scalar(act, G, slot) for G, slot, _, _ in pair])
        if t in ("m0", "m1"):
            rsqrt_scalar(act, sq, T)

    def ff_vector(dve, t, fixed=None):
        base, _, B = FFS[t]

        def pick(n, e, done):
            for k in range(4):
                dve.wait_ge(sem(f"down_read{k}"), done + 1)
            V.tensor_copy(block_gate[:, n, :], gates[:, :, bass.ds(e, 1)].rearrange("p j a -> p (j a)"))\
                .then_inc(sem("gate_picked"), 1)

        def expert(e):
            pick(0, e, base + B * e)

        def body(pair):
            for n, (G, slot, e, b) in enumerate(pair):
                if B == 1:
                    pick(n, e, G["n"] - n)
                hidden_vector(dve, G, slot)
                if fixed is None:
                    dve.wait_ge(sem("gate_picked"), G["n"] + 1 if B == 1 else 2 * MOE_E + 1 + e)
            for n, (G, slot, e, b) in enumerate(pair):
                if fixed is not None:
                    weight = fixed
                else:
                    weight = block_gate[:, n if FFS[t][2] == 1 else 0, :]
                add_vector(dve, G, weight)
        blocks(dve, t, body, expert if fixed is None else None)
        for k in range(4):
            dve.wait_ge(sem(f"down_read{k}"), FFS[t][0] + FFS[t][1] * FFS[t][2] + 1)

    FFR = {"m0": True, "m1": True, "m2": False}
    logit = tiny(T, 20)
    r_m, r_m2, r_sum, r_g = tiny(T, 1), tiny(T, 1), tiny(T, 1), tiny(T, 1)
    r_eq, r_sc = tiny(T, 8), tiny(T, 8)
    r_grp, r_one, r_two = tiny(T, 4), tiny(T, 8), tiny(T, 8)
    r_e = tiny(T, 12)
    r_sel = tiny(T, 8)
    r_tmp = tiny(T, 4, 4)
    rank = tiny(8)

    def first_max(vals, n, value, onehot):
        vlink(V.tensor_reduce(out=value, in_=vals, axis=AX, op=ALU.max))
        vlink(V.tensor_tensor(r_eq[:, :, 0:n], vals, value.to_broadcast([P, T, n]), ALU.is_equal))
        vlink(V.tensor_tensor(r_sc[:, :, 0:n], r_eq[:, :, 0:n], over(rank[:, 0:n], 1, T), ALU.mult))
        vlink(V.tensor_reduce(out=r_m2, in_=r_sc[:, :, 0:n], axis=AX, op=ALU.max))
        vlink(V.tensor_tensor(onehot, r_sc[:, :, 0:n], r_m2.to_broadcast([P, T, n]), ALU.is_equal))

    def route_vector(dve, t, bias):
        grouped = FFR[t]
        n = 4 if grouped else MOE2_E
        cols = 20 if grouped else MOE2_E
        dve.wait_ge(sem("route_logits"), ROUTER[t] + 1)
        src = psum[4][:, 0:32 * T].rearrange("p (j n) -> p j n", j=T)[:, :, 0:cols]
        if grouped:
            vlink(V.tensor_tensor(logit, src, over(bias, 1, T), ALU.add), sem("route_logits_read"))
            first_max(logit[:, :, 0:4], 4, r_m, r_grp)
            vlink(V.tensor_tensor(r_e[:, :, 0:4], logit[:, :, 0:4], r_m.to_broadcast([P, T, 4]), ALU.subtract))
            for j in range(T):
                vlink(V.tensor_tensor(r_tmp[:, j], logit[:, j, 4:20].rearrange("p (g e) -> p g e", g=4),
                                      over(r_grp[:, j, :], 2, 4), ALU.mult))
                vlink(V.tensor_reduce(out=r_sel[:, j, 0:4], in_=r_tmp[:, j].rearrange("p g e -> p e g"), axis=AX,
                                      op=ALU.add))
            vals = r_sel[:, :, 0:4]
        else:
            vlink(V.tensor_copy(r_sel, src), sem("route_logits_read"))
            vals = r_sel
        first_max(vals, n, r_m, r_one[:, :, 0:n])
        vlink(V.tensor_tensor(r_e[:, :, 4:4 + n], vals, r_m.to_broadcast([P, T, n]), ALU.subtract))
        vlink(V.scalar_tensor_tensor(out=r_two[:, :, 0:n], in0=r_one[:, :, 0:n], scalar=NEG, in1=vals,
                                     op0=ALU.mult, op1=ALU.add))
        if not grouped:
            vlink(V.tensor_copy(r_e[:, :, 0:4], r_e[:, :, 4:8]))
        else:
            vlink(V.memset(r_e[:, :, 8:12], 0.0))
        first_max(r_two[:, :, 0:n], n, r_g, r_sc[:, :, 0:n])
        vlink(V.tensor_tensor(r_one[:, :, 0:n], r_one[:, :, 0:n], r_sc[:, :, 0:n], ALU.add), sem("route_masked"))
        dve.wait_ge(sem("route_exp"), ROUTER[t] + 1)
        vlink(V.tensor_tensor(r_two[:, :, 0:n], r_e[:, :, 4:4 + n], r_one[:, :, 0:n], ALU.mult))
        vlink(V.tensor_reduce(out=r_sum, in_=r_two[:, :, 0:n], axis=AX, op=ALU.add))
        vlink(V.reciprocal(r_sum, r_sum))
        vlink(V.tensor_tensor(r_two[:, :, 0:n], r_two[:, :, 0:n], r_sum.to_broadcast([P, T, n]), ALU.mult))
        if grouped:
            vlink(V.tensor_reduce(out=r_g, in_=r_e[:, :, 0:4], axis=AX, op=ALU.add))
            vlink(V.reciprocal(r_g, r_g))
            vlink(V.tensor_tensor(r_two[:, :, 0:4], r_two[:, :, 0:4], r_g.to_broadcast([P, T, 4]), ALU.mult))
            for j in range(T):
                vlink(V.tensor_tensor(gates[:, j, :].rearrange("p (g e) -> p g e", g=4), over(r_grp[:, j, :], 2, 4),
                                      over(r_two[:, j, 0:4], 1, 4), ALU.mult))
        else:
            vlink(V.tensor_copy(gates[:, :, 0:8], r_two))

    def moe_first_vector(dve, t, i):
        to_features_vector(t)
        for j in range(T):
            vlink(V.tensor_scalar(h[:, j, :], h[:, j, :], ALPHA, None, ALU.mult))
        route_vector(dve, t, par[f"route_b{i}"])
        ff_vector(dve, t)
        dve.wait_ge(sem("norm_landed"), 32 * (2 * i + 2))
        layer_norm()
        dve.sem_inc(sem("phase_done"), 1)

    normed = arena[:, 0:T * D].rearrange("p (j d) -> p j d", j=T)
    junk_row = arena[:, T * D:T * D + D]

    def normed_vector(t):
        rms_scale(h, junk_row, D, rstd)
        for j in range(T):
            vlink(V.tensor_scalar(normed[:, j, :], h[:, j, :], rstd[:, j:j + 1], None, ALU.mult),
                  *([sem("normed")] if j else []))

    ca = carver()
    c_tok = ca(T, Q_RANK + KV_RANK + ROPE)
    fox_q, fox_k, fox_v = ca(4, S), ca(4, S), ca(T, FOX_W)
    c_norm = ca(T, Q_RANK + KV_RANK)
    cT = ca(3, S)
    q_cat, k_cat = ca(T, MLA_H, MLA_K), ca(T, MLA_H, MLA_K)
    v_mla = ca(T, MLA_H, V_DIM)
    mla_qT, mla_kT = ca(MLA_H, S), ca(MLA_H, S)
    odd_mix = ca(T, D)
    odd_mixT = ca(2, 4, S)
    at_masked, at_probs, at_probsT = ca(2, 3, P), ca(2, 3, P), ca(2, 3, P)
    fox_sum, fox_neg = ca(S), ca(S)
    mask_chunk = ca(3, P)
    rope_a, rope_b, rope_c, rope_d = (ca(8, 16) for _ in range(4))
    sel = odd_mixT.rearrange("p k c t -> p (k c) t")
    fox_bias = ca(2, 3, P)
    at_nbias, at_sums = tiny(16, 2), tiny(16, 2)
    log_f, f_e, f_x = tiny(T, FOX_H), tiny(T, FOX_H), tiny(T, FOX_H)
    c_rstd = tiny(2, T)

    def odd_tensor(pe):
        t = "od"
        pe.wait_ge(sem("phase_done"), 2)
        to_features_tensor(pe, t, h)
        project_tensor(pe, t, odd_pieces)
        n_p = len(odd_pieces)
        read_wait(pe, "od", 0, n_p)
        read_wait(pe, "od", 1, n_p)
        pe.wait_ge(sem("od_c_normed"), 1)
        for c in range(3):
            for j in range(T):
                last = nc.tensor.transpose(psum[6 + c // 2][:, (c % 2) * S + j * P:(c % 2) * S + (j + 1) * P],
                                           c_norm[:, j, c * P:(c + 1) * P], ident)
        last.then_inc(sem("od_c_turned"), 1)
        pe.wait_ge(sem("od_ct_ready"), 1)
        piece_wait(pe, odd_qup)
        wq = piece_ap(odd_qup)
        for j in range(T):
            for half, (a, b) in enumerate(((0, 512), (512, MLA_H * MLA_K))):
                for c in range(2):
                    last = nc.tensor.matmul(psum[2 * j + half][:, 0:b - a], cT[:, c, j * P:(j + 1) * P], wq[:, c, a:b],
                                            start=(c == 0), stop=(c == 1))
        last.then_inc(sem("od_qup"), 1)
        piece_wait(pe, odd_kvup)
        wkv = piece_ap(odd_kvup)
        for j in range(T):
            for half in range(2):
                last = nc.tensor.matmul(psum[4 + 2 * j + half], cT[:, 2, j * P:(j + 1) * P],
                                        wkv[:, half * 512:(half + 1) * 512], start=True, stop=True)
        last.then_inc(sem("od_kvup"), 1)
        pe.wait_ge(sem("od_cat_ready"), 1)
        for n in range(8):
            src = (q_cat, k_cat)[n // 4]
            if n >= 2:
                pe.wait_ge(sem("od_cat_read"), n - 1)
            for i in range(4):
                hd, j = 2 * (n % 4) + i // 2, i % 2
                last = nc.tensor.transpose(psum[6 + n % 2][0:MLA_K, i * P:(i + 1) * P], src[:, j, hd, :], ident)
            last.then_inc(sem("od_cat_turned"), 1)
        pe.wait_ge(sem("od_cat_read"), 8)

        def mla_logits(u, bank):
            nc.tensor.matmul(bank[:, 0:P], mla_qT[0:MLA_K, u, 0:P], mla_kT[0:MLA_K, u, 0:P], start=True, stop=True)
            return nc.tensor.matmul(bank[:, P:3 * P], mla_qT[0:MLA_K, u, P:S], mla_kT[0:MLA_K, u, :],
                                    start=True, stop=True)
        attention_tensor(pe, "mla", MLA_H, mla_logits, at_probs, at_probsT, lambda u, s: v_mla[:, s, u, :], V_DIM)
        pe.wait_ge(sem("od_logf"), 1)
        nc.tensor.matmul(psum[6][0:FOX_H, 0:P], log_f[:, 0, :], upto, start=True, stop=True)
        nc.tensor.matmul(psum[6][0:FOX_H, P:S], log_f[:, 0, :], ones, start=True, stop=False)
        nc.tensor.matmul(psum[6][0:FOX_H, P:S], log_f[:, 1, :], upto, start=False, stop=True)\
            .then_inc(sem("od_fsum"), 1)
        pe.wait_ge(sem("od_fsum_read"), 1)
        pe.wait_ge(sem("at_written"), MLA_H)

        def fox_logits(u, bank):
            if u >= 2:
                pe.wait_ge(sem("fox_biased"), u - 1)
            fb = psum[6 + u % 2]
            for j, (a, b) in enumerate(((0, P), (P, 3 * P))):
                nc.tensor.matmul(fb[:, a:b], fox_sum[0:FOX_H, j * P:(j + 1) * P], sel[0:FOX_H, u, 0:b - a],
                                 start=True, stop=False)
                last = nc.tensor.matmul(fb[:, a:b], sel[0:FOX_H, u, 0:P], fox_neg[0:FOX_H, 0:b - a],
                                        start=False, stop=True)
            last.then_inc(sem("fox_term"), 1)
            r = slice((u % 2) * 64, (u % 2) * 64 + 64)
            qq, kk = fox_q[r, u // 2, :], fox_k[r, u // 2, :]
            nc.tensor.matmul(bank[:, 0:P], qq[:, 0:P], kk[:, 0:P], start=True, stop=True)
            return nc.tensor.matmul(bank[:, P:3 * P], qq[:, P:S], kk, start=True, stop=True)
        attention_tensor(pe, "fox", FOX_H, fox_logits, at_probs, at_probsT,
                         lambda u, s: fox_v[:, s, u * HD:(u + 1) * HD], HD)
        out_tensor(pe, t, odd_mix, odd_mixT, odd_out)

    def odd_scalar(act):
        A = nc.scalar
        for n, (name, _, _, cols) in enumerate(odd_pieces):
            full_wait(act, "od", 0, n)
            b0 = psum[2 * (n % 3)]
            b0c = b0.rearrange("p (c t) -> p c t", c=2)
            if name == "q":
                ins = A.mul(fox_q[:, 0:2, :], b0c, HD ** -0.5)
            elif name == "k":
                ins = A.copy(fox_k[:, 0:2, :], b0c)
            else:
                ins = A.copy({"c": c_tok, "v": fox_v, "f": f_x}[name][:, 0, :], b0[:, 0:cols])
            ins.then_inc(sem("bank0_read"), 1)
            if name == "c":
                rsqrt_scalar(act, sq, T)
                rsqrt_scalar(act, sq, T)
        act.wait_ge(sem("od_qup"), 1)
        for j in range(T):
            qv = q_cat[:, j].rearrange("p h d -> p (h d)")
            A.copy(qv[:, 0:512], psum[2 * j])
            ins = A.copy(qv[:, 512:], psum[2 * j + 1][:, 0:MLA_H * MLA_K - 512])
        ins.then_inc(sem("od_qcat"), 1)
        act.wait_ge(sem("od_f_negabs"), 1)
        A.activation(f_e, f_e, ACT.Exp).then_inc(sem("od_f_exp"), 1)
        act.wait_ge(sem("od_f_exp"), 1)
        A.activation(f_e, f_e, ACT.Ln, bias=1.0).then_inc(sem("od_f_ln"), 1)
        attention_scalar(act, "mla", MLA_H, MLA_K ** -0.5, at_masked, at_nbias, at_probs, at_sums, at_probsT)
        attention_scalar(act, "fox", FOX_H, 1.0, at_masked, at_nbias[:, 8:], at_probs, at_sums[:, 8:], at_probsT)
        rsqrt_scalar(act, sq, T)

    def rope(x1, x2, cos, sin, tmps):
        a, b, c, d = tmps
        vlink(V.tensor_tensor(a, x1, cos, ALU.mult))
        vlink(V.tensor_tensor(b, x2, sin, ALU.mult))
        vlink(V.tensor_tensor(c, x2, cos, ALU.mult))
        vlink(V.tensor_tensor(d, x1, sin, ALU.mult))
        vlink(V.tensor_tensor(x1, a, b, ALU.subtract))
        vlink(V.tensor_tensor(x2, c, d, ALU.add))

    def odd_vector(dve):
        vlink(V.memset(mask_chunk, 0.0))
        for i in (0, 2):
            vlink(V.memset(mask_chunk[0:64, i, 64:P], NEG))
        to_features_vector("od")
        vlink(V.tensor_copy(sel[0:FOX_H], over(ident[0:FOX_H, 0:FOX_H], 2, S)))
        for n, (name, _, _, cols) in enumerate(odd_pieces):
            full_wait(dve, "od", 1, n)
            b1 = psum[2 * (n % 3) + 1]
            b1c = b1.rearrange("p (c t) -> p c t", c=2)
            if name == "q":
                ins = V.tensor_scalar(fox_q[:, 2:4, :], b1c, HD ** -0.5, None, ALU.mult)
            elif name == "k":
                ins = V.tensor_copy(fox_k[:, 2:4, :], b1c)
            else:
                ins = V.tensor_copy({"c": c_tok, "v": fox_v, "f": f_x}[name][:, 1, :], b1[:, 0:cols])
            vlink(ins, sem("bank1_read"))
            if name == "c":
                read_wait(dve, "od", 0, n + 1)
                for i, (a, b) in enumerate(((0, Q_RANK), (Q_RANK, Q_RANK + KV_RANK))):
                    rms_scale(c_tok[:, :, a:b], q_cat[:, 0].rearrange("p h d -> p (h d)")[:, 0:b - a], b - a, c_rstd[:, i, :])
                    for j in range(T):
                        vlink(V.tensor_scalar(c_norm[:, j, a:b], c_tok[:, j, a:b], c_rstd[:, i, j:j + 1], None, ALU.mult),
                              *([sem("od_c_normed")] if i and j else []))
        read_wait(dve, "od", 0, len(odd_pieces))
        vlink(V.tensor_tensor(f_x, f_x, over(par["f_bias"], 1, T), ALU.add))
        vlink(V.tensor_scalar(f_x, f_x, -1.0, None, ALU.mult))
        vlink(minus_abs(f_e, f_x), sem("od_f_negabs"))
        dve.wait_ge(sem("od_c_turned"), 1)
        vlink(V.tensor_tensor(cT[:, 0:2, :], psum[6].rearrange("p (c t) -> p c t", c=2), over(par["q_norm"], 2, S), ALU.mult))
        vlink(V.tensor_scalar(cT[:, 2, :], psum[7][:, 0:S], par["kv_norm"], None, ALU.mult), sem("od_ct_ready"))
        tab = par["tables"]
        for j in range(T):
            pe_k = c_tok[:, j:j + 1, Q_RANK + KV_RANK:]
            cos, sin = (over(tab[:, j, 16 * i:16 * i + 16], 1, 1) for i in range(2))
            rope(pe_k[:, :, 0:16], pe_k[:, :, 16:32], cos, sin, [x[:, 0:1, :] for x in (rope_a, rope_b, rope_c, rope_d)])
        dve.wait_ge(sem("od_kvup"), 1)
        for j in range(T):
            for half in range(2):
                kv = psum[4 + 2 * j + half].rearrange("p (h d) -> p h d", h=4)
                vlink(V.tensor_copy(k_cat[:, j, 4 * half:4 * half + 4, 0:NOPE], kv[:, :, 0:NOPE]))
                vlink(V.tensor_copy(v_mla[:, j, 4 * half:4 * half + 4, :], kv[:, :, NOPE:]))
            vlink(V.tensor_copy(k_cat[:, j, :, NOPE:], over(c_tok[:, j, Q_RANK + KV_RANK:], 1, MLA_H)))
        dve.wait_ge(sem("od_qcat"), 1)
        for j in range(T):
            cos, sin = (over(tab[:, j, 16 * i:16 * i + 16], 1, MLA_H) for i in range(2))
            rope(q_cat[:, j, :, NOPE:NOPE + 16], q_cat[:, j, :, NOPE + 16:], cos, sin, (rope_a, rope_b, rope_c, rope_d))
        vlink(V.memset(at_sums, 0.0), sem("od_cat_ready"))
        for n in range(8):
            dve.wait_ge(sem("od_cat_turned"), n + 1)
            dst = (mla_qT, mla_kT)[n // 4]
            vlink(V.tensor_copy(dst[0:MLA_K, 2 * (n % 4):2 * (n % 4) + 2, :],
                                psum[6 + n % 2][0:MLA_K, :].rearrange("p (h t) -> p h t", h=2)), sem("od_cat_read"))
        dve.wait_ge(sem("od_f_ln"), 1)
        vlink(V.scalar_tensor_tensor(out=log_f, in0=f_x, scalar=0.0, in1=f_e, op0=ALU.max, op1=ALU.add))
        vlink(V.tensor_scalar(log_f, log_f, -1.0, None, ALU.mult), sem("od_logf"))

        def head_writer(off, width):
            def write(u, bank, scale, done):
                vlink(V.tensor_tensor(odd_mix[:, :, off + u * width:off + (u + 1) * width],
                                      bank[:, 0:T * width].rearrange("p (j d) -> p j d", j=T),
                                      over(scale, 2, width), ALU.mult), done)
            return write
        attention_vector("mla", MLA_H, MLA_K ** -0.5, lambda u: mask_chunk, at_masked, at_nbias, at_sums,
                         head_writer(0, V_DIM))
        dve.wait_ge(sem("od_fsum"), 1)
        vlink(V.tensor_copy(fox_sum[0:FOX_H], psum[6][0:FOX_H, 0:S]))
        vlink(V.tensor_scalar(fox_neg[0:FOX_H], fox_sum[0:FOX_H], -1.0, None, ALU.mult), sem("od_fsum_read"))

        def fox_mask(u):
            dve.wait_ge(sem("fox_term"), u + 1)
            vlink(V.tensor_tensor(fox_bias[:, u % 2], psum[6 + u % 2][:, 0:3 * P].rearrange("p (i s) -> p i s", i=3),
                                  mask_causal, ALU.add), sem("fox_biased"))
            return fox_bias[:, u % 2]
        attention_vector("fox", FOX_H, 1.0, fox_mask, at_masked, at_nbias[:, 8:], at_sums[:, 8:],
                         head_writer(MLA_H * V_DIM, HD))
        vlink(V.memset(at_nbias[:, 0, :], 0.0), sem("mix_ready"))
        out_vector("od", odd_mixT, 2, ALPHA)
        dve.wait_ge(sem("norm_landed"), 96)
        layer_norm()
        dve.sem_inc(sem("phase_done"), 1)

    ca = carver()
    ca(3 * D)
    sg_mix = ca(T, SG_W)
    sg_v = ca(T, SG_W)
    sg_mixT = ca(4, 4, S)
    spatialT = ca(SG_G, P)
    sg_junk = ca(SG_W)

    def sg_tensor(pe):
        t = "sg"
        pe.wait_ge(sem("phase_done"), 4)
        pe.wait_ge(sem("normed"), 1)
        to_features_tensor(pe, t, normed)
        project_tensor(pe, t, sg_pieces)
        read_wait(pe, "sg", 0, 8)
        read_wait(pe, "sg", 1, 8)
        piece_wait(pe, sg_spatial)
        wsp = piece_ap(sg_spatial)
        for g in range(SG_G):
            last = nc.tensor.transpose(psum[6 + g // 4][:, (g % 4) * P:(g % 4 + 1) * P], wsp[:, g, :], ident)
        last.then_inc(sem("sg_w_turned"), 1)
        pe.wait_ge(sem("sg_w_ready"), 1)
        pe.wait_ge(sem("sg_v_ready"), 1)
        for n in range(8):
            j, g = n // 4, 2 * (n % 4)
            if n >= 4:
                pe.wait_ge(sem("sg_gated"), n - 3)
            for i in range(2):
                last = nc.tensor.matmul(psum[n % 4][:, i * SG_C:(i + 1) * SG_C], spatialT[:, g + i, :],
                                        sg_v[:, j, (g + i) * SG_C:(g + i + 1) * SG_C], start=True, stop=True)
            last.then_inc(sem("sg_mixed"), 1)
        out_tensor(pe, t, sg_mix, sg_mixT, sg_out)

    def sg_scalar(act):
        rsqrt_scalar(act, sq, T)
        for n in range(8):
            dst = sg_mix if n < 4 else sg_v
            for half in range(2):
                full_wait(act, "sg", half, n)
                nc.scalar.activation(dst[:, half, (n % 4) * 512:(n % 4 + 1) * 512], psum[2 * (n % 3) + half],
                                     ACT.Gelu_apprx_tanh).then_inc(sem(f"bank{half}_read"), 1)
        rsqrt_scalar(act, sq, T)

    def sg_vector(dve):
        normed_vector("sg")
        to_features_vector("sg", par["l0_mix_norm_2"])
        dve.wait_ge(sem("sg_w_turned"), 1)
        for i in range(2):
            vlink(V.tensor_tensor(spatialT[:, 4 * i:4 * i + 4, :], psum[6 + i].rearrange("p (g t) -> p g t", g=4),
                                  over(upto, 1, 4), ALU.mult), *([sem("sg_w_ready")] if i else []))
        read_wait(dve, "sg", 1, 8)
        rms_scale(sg_v, sg_junk, SG_W, rstd)
        dve.wait_ge(sem("norm_landed"), 160)
        for j in range(T):
            vlink(V.scalar_tensor_tensor(out=sg_v[:, j, :], in0=sg_v[:, j, :], scalar=rstd[:, j:j + 1], in1=norm_vec,
                                         op0=ALU.mult, op1=ALU.mult), *([sem("sg_v_ready")] if j else []))
        for n in range(8):
            j, g = n // 4, 2 * (n % 4)
            dve.wait_ge(sem("sg_mixed"), n + 1)
            for i in range(2):
                u = sg_mix[:, j, (g + i) * SG_C:(g + i + 1) * SG_C]
                vlink(V.scalar_tensor_tensor(out=u, in0=psum[n % 4][:, i * SG_C:(i + 1) * SG_C],
                                             scalar=par["b_spatial"][:, g + i:g + i + 1], in1=u, op0=ALU.add, op1=ALU.mult),
                      *([sem("sg_gated")] if i else []), *([sem("mix_ready")] if i and n == 7 else []))
        out_vector("sg", sg_mixT, 4, 1.0)
        dve.sem_inc(sem("phase_done"), 1)

    def dense_vector(dve):
        normed_vector("ff")
        to_features_vector("ff", par["l0_ffn_norm_2"])
        ff_vector(dve, "ff", fixed=ones)
        dve.sem_inc(sem("phase_done"), 1)

    def moe_second_vector(dve):
        normed_vector("m2")
        to_features_vector("m2", par["l1_moe_norm_2"])
        route_vector(dve, "m2", None)
        ff_vector(dve, "m2")
        dve.sem_inc(sem("phase_done"), 1)

    ca = carver()
    ca(3 * D)
    MAPS = 2 * DA_H
    da_qk = ca(T, 2 * MAPS, HD)
    da_v = ca(T, D)
    da_qkT = ca(2 * DA_H, S)
    da_mix = ca(T, D)
    da_mixT = ca(2, 4, S)
    da_masked, da_probs, da_probsT = ca(2, 3, P), ca(2, 3, P), ca(2, 3, P)
    da_first = ca(T, P)
    da_tmps = [ca(2 * MAPS, 8) for _ in range(4)]
    da_sq = da_mixT.rearrange("p k c t -> p (k c t)").rearrange("p (m d) -> p m d", d=HD)
    da_ms = ca(T, 2 * MAPS)
    da_hs = ca(T, DA_H)
    da_ms_flat, da_hs_flat = da_ms.rearrange("p j m -> p (j m)"), da_hs.rearrange("p j h -> p (j h)")
    ang, turns, half_sin, cs_cos, cs_sin = (tiny(T, 8) for _ in range(5))
    posf = tiny(T)
    lam_tmp, lam_sum = ca(2, HD), tiny(2)
    neg_lam = tiny(1)

    def da_tensor(pe):
        t = "da"
        pe.wait_ge(sem("phase_done"), 6)
        pe.wait_ge(sem("normed"), 3)
        to_features_tensor(pe, t, normed)
        project_tensor(pe, t, da_pieces)
        pe.wait_ge(sem("da_rotated"), 1)
        for n in range(8):
            if n >= 2:
                pe.wait_ge(sem("da_qk_read"), n - 1)
            for i in range(4):
                c, j = 2 * n + i // 2, i % 2
                last = nc.tensor.transpose(psum[6 + n % 2][:, i * P:(i + 1) * P],
                                           da_qk[:, j, 2 * c:2 * c + 2, :].rearrange("p m d -> p (m d)"), ident)
            last.then_inc(sem("da_qk_turned"), 1)
        pe.wait_ge(sem("da_qk_read"), 8)
        read_wait(pe, "da", 0, 6)
        read_wait(pe, "da", 1, 6)

        def logits(u, bank):
            r = slice((u % 2) * 64, (u % 2) * 64 + 64)
            qq, kk = da_qkT[r, u // 2, :], da_qkT[r, DA_H + u // 2, :]
            nc.tensor.matmul(bank[:, 0:P], qq[:, 0:P], kk[:, 0:P], start=True, stop=True)
            return nc.tensor.matmul(bank[:, P:3 * P], qq[:, P:S], kk, start=True, stop=True)
        attention_tensor(pe, "dat", MAPS, logits, da_probs, da_probsT,
                         lambda u, s: da_v[:, s, (u // 2) * P:(u // 2 + 1) * P], P)
        out_tensor(pe, t, da_mix, da_mixT, da_out)

    def da_scalar(act):
        A = nc.scalar
        rsqrt_scalar(act, sq, T)
        for n in range(6):
            full_wait(act, "da", 0, n)
            dst = da_qk[:, 0].rearrange("p m d -> p (m d)")[:, n * 512:(n + 1) * 512] if n < 4 else \
                da_v[:, 0, (n - 4) * 512:(n - 3) * 512]
            A.copy(dst, psum[2 * (n % 3)]).then_inc(sem("bank0_read"), 1)
        act.wait_ge(sem("da_reduced"), 1)
        A.activation(cs_sin, ang, ACT.Sin)
        A.activation(half_sin, ang, ACT.Sin, scale=0.5).then_inc(sem("da_sines"), 1)
        act.wait_ge(sem("da_lam_sums"), 1)
        A.activation(lam_sum, lam_sum, ACT.Exp).then_inc(sem("da_lam_exp"), 1)
        rsqrt_scalar(act, da_ms_flat, T * 2 * MAPS)
        attention_scalar(act, "dat", MAPS, HD ** -0.5, da_masked, at_nbias, da_probs, at_sums, da_probsT)
        rsqrt_scalar(act, da_hs_flat, T * DA_H)

    def da_vector(dve):
        normed_vector("da")
        to_features_vector("da", par["l1_mix_norm_2"])
        two_pi = 2 * math.pi
        c1 = 6.28125
        c2 = float(np.float32(np.round((two_pi - c1) * 2 ** 22) / 2 ** 22))
        c3 = float(np.float32(two_pi - c1 - c2))
        magic = 12582912.0
        vlink(V.tensor_copy(posf, par["positions"]))
        vlink(V.tensor_tensor(ang, par["tables"][:, :, 32:40], over(posf, 2, 8), ALU.mult))
        vlink(V.tensor_scalar(turns, ang, 1.0 / two_pi, None, ALU.mult))
        vlink(V.tensor_scalar(turns, turns, magic, None, ALU.add))
        vlink(V.tensor_scalar(turns, turns, -magic, None, ALU.add))
        for c in (c1, c2, c3):
            vlink(V.scalar_tensor_tensor(out=ang, in0=turns, scalar=-c, in1=ang, op0=ALU.mult, op1=ALU.add))
        vlink(V.tensor_scalar(ang, ang, 3.1415925, -3.1415925, ALU.min, ALU.max), sem("da_reduced"))
        lam = par["lam"]
        for i in range(2):
            vlink(V.tensor_tensor_reduce(out=lam_tmp[:, i, :], in0=lam[:, 2 * i, :], in1=lam[:, 2 * i + 1, :], scale=1.0,
                                         scalar=0.0, op0=ALU.mult, op1=ALU.add, accum_out=lam_sum[:, i:i + 1]),
                  *([sem("da_lam_sums")] if i else []))
        for n in range(6):
            full_wait(dve, "da", 1, n)
            dst = da_qk[:, 1].rearrange("p m d -> p (m d)")[:, n * 512:(n + 1) * 512] if n < 4 else \
                da_v[:, 1, (n - 4) * 512:(n - 3) * 512]
            vlink(V.tensor_copy(dst, psum[2 * (n % 3) + 1]), sem("bank1_read"))
        read_wait(dve, "da", 0, 6)
        dve.wait_ge(sem("da_sines"), 1)
        vlink(V.tensor_tensor(cs_cos, half_sin, half_sin, ALU.mult))
        vlink(V.tensor_scalar(cs_cos, cs_cos, -2.0, 1.0, ALU.mult, ALU.add))
        dve.wait_ge(sem("da_lam_exp"), 1)
        vlink(V.tensor_tensor(neg_lam, lam_sum[:, 1:2], lam_sum[:, 0:1], ALU.subtract))
        vlink(V.tensor_scalar(neg_lam, neg_lam, -LAMBDA_INIT, None, ALU.add))
        for j in range(T):
            vlink(V.tensor_tensor(da_sq, da_qk[:, j], da_qk[:, j], ALU.mult))
            vlink(V.tensor_reduce(out=da_ms[:, j, :], in_=da_sq, axis=AX, op=ALU.add))
        vlink(V.tensor_scalar(da_ms, da_ms, 1.0 / HD, RMS_EPS, ALU.mult, ALU.add))
        rsqrt_vector(da_ms_flat, da_ms_flat, T * 2 * MAPS)
        for j in range(T):
            vlink(V.tensor_tensor(da_qk[:, j], da_qk[:, j], over(da_ms[:, j, :], 2, HD), ALU.mult))
            for i, gain in enumerate(("da_q_norm", "da_k_norm")):
                part = da_qk[:, j, i * MAPS:(i + 1) * MAPS, :]
                vlink(V.tensor_tensor(part, part, over(par[gain], 1, MAPS), ALU.mult))
            cos, sin = (over(x[:, j, :], 1, 2 * MAPS) for x in (cs_cos, cs_sin))
            rope(da_qk[:, j, :, 0:8], da_qk[:, j, :, 8:16], cos, sin, da_tmps)
        vlink(V.memset(at_sums, 0.0), sem("da_rotated"))
        for n in range(8):
            dve.wait_ge(sem("da_qk_turned"), n + 1)
            vlink(V.tensor_copy(da_qkT[:, 2 * n:2 * n + 2, :], psum[6 + n % 2].rearrange("p (c t) -> p c t", c=2)),
                  sem("da_qk_read"))

        def write(u, bank, scale, done):
            src = bank[:, 0:T * P].rearrange("p (j d) -> p j d", j=T)
            if u % 2 == 0:
                vlink(V.tensor_tensor(da_first, src, over(scale, 2, P), ALU.mult), done)
            else:
                dst = da_mix[:, :, (u // 2) * P:(u // 2 + 1) * P]
                vlink(V.tensor_tensor(dst, src, over(scale, 2, P), ALU.mult), done)
                vlink(V.scalar_tensor_tensor(out=dst, in0=dst, scalar=neg_lam, in1=da_first, op0=ALU.mult, op1=ALU.add))
        attention_vector("dat", MAPS, HD ** -0.5, lambda u: mask_causal, da_masked, at_nbias, at_sums, write)
        for j in range(T):
            y = da_mix[:, j, :].rearrange("p (h d) -> p h d", d=P)
            sqv = da_qk[:, 0].rearrange("p m d -> p (m d)")[:, 0:D].rearrange("p (h d) -> p h d", d=P)
            vlink(V.tensor_tensor(sqv, y, y, ALU.mult))
            vlink(V.tensor_reduce(out=da_hs[:, j, :], in_=sqv, axis=AX, op=ALU.add))
        vlink(V.tensor_scalar(da_hs, da_hs, 1.0 / P, RMS_EPS, ALU.mult, ALU.add))
        rsqrt_vector(da_hs_flat, da_hs_flat, T * DA_H)
        vlink(V.tensor_scalar(da_hs, da_hs, 1.0 - LAMBDA_INIT, None, ALU.mult))
        for j in range(T):
            y = da_mix[:, j, :].rearrange("p (h d) -> p h d", d=P)
            vlink(V.tensor_tensor(y, y, over(da_hs[:, j, :], 2, P), ALU.mult))
            vlink(V.tensor_tensor(y, y, over(par["subln"], 1, DA_H), ALU.mult), *([sem("mix_ready")] if j else []))
        out_vector("da", da_mixT, 2, 1.0)
        dve.sem_inc(sem("phase_done"), 1)

    block = nc.Block()
    with block as block:
        @block.sync
        def _(sp):
            sp.dma_start(h, w["x"][0].rearrange("(j p) d -> p j d", p=P)).then_inc(sem("x_landed"), 16)

            def load_pieces(a, b):
                for n in range(a, b):
                    if n >= PSLOTS:
                        name, count = released[n - PSLOTS]
                        sp.wait_ge(sem(name), count)
                    sp.dma_start(piece_ap(n), piece_list[n][0]).then_inc(sem(f"piece_landed{n % PSLOTS}"), 16)
            load_pieces(0, EVEN_END)
            ff_sync(sp, "m0", w["moe_w_gate"][0], w["moe_w_up"][0], w["moe_w_down"][0])
            load_pieces(EVEN_END, ODD_END)
            ff_sync(sp, "m1", w["moe_w_gate"][1], w["moe_w_up"][1], w["moe_w_down"][1])
            load_pieces(ODD_END, SG_END)
            ff_sync(sp, "ff", w["l0_ffn_w_gate_2"], w["l0_ffn_w_up_2"], w["l0_ffn_w_down_2"])
            load_pieces(SG_END, DA_END)
            ff_sync(sp, "m2", w["l1_moe_w_gate_2"], w["l1_moe_w_up_2"], w["l1_moe_w_down_2"])
            sp.wait_ge(sem("phase_done"), 8)
            sp.dma_start(out[0].rearrange("(j p) d -> p j d", p=P), h).then_inc(sem("out_written"), 16)
            sp.wait_ge(sem("out_written"), 16)

        @block.gpsimd
        def _(pool):
            setup_gpsimd(pool)
            norm_loads_gpsimd(pool)

        @block.tensor
        def _(pe):
            free_slots_tensor(pe)
            even_tensor(pe)
            ff_tensor(pe, "m0", 1, par["route_w0"])
            odd_tensor(pe)
            ff_tensor(pe, "m1", 3, par["route_w1"])
            sg_tensor(pe)
            ff_tensor(pe, "ff", 5, None)
            da_tensor(pe)
            ff_tensor(pe, "m2", 7, par["route_w2"])

        @block.scalar
        def _(act):
            even_scalar(act)
            ff_scalar(act, "m0")
            odd_scalar(act)
            ff_scalar(act, "m1")
            sg_scalar(act)
            ff_scalar(act, "ff")
            da_scalar(act)
            ff_scalar(act, "m2")

        @block.vector
        def _(dve):
            for i in range(8):
                vlink(V.memset(rank[:, i:i + 1], float(8 - i)))
            dve.wait_ge(sem("const_ready"), 1)
            even_vector(dve)
            moe_first_vector(dve, "m0", 0)
            odd_vector(dve)
            moe_first_vector(dve, "m1", 1)
            sg_vector(dve)
            dense_vector(dve)
            da_vector(dve)
            moe_second_vector(dve)


INPUTS = [
    "x", "ev_w_in", "ev_conv_w", "ev_conv_b", "ev_dt_bias", "ev_a_log", "ev_d_skip", "ev_norm_g", "ev_w_out",
    "od_w_in", "od_q_norm_g", "od_w_q_up", "od_kv_norm_g", "od_w_kv_up", "od_f_bias", "od_w_out", "ln1_g",
    "ln1_b", "ln2_g", "ln2_b", "moe_w_group", "moe_b_group", "moe_w_expert", "moe_b_expert", "moe_w_gate",
    "moe_w_up", "moe_w_down", "positions_2", "l0_mix_norm_2", "l0_sg_w_in_2", "l0_sg_v_norm_2",
    "l0_sg_w_spatial_2", "l0_sg_b_spatial_2", "l0_sg_w_out_2", "l0_ffn_norm_2", "l0_ffn_w_gate_2",
    "l0_ffn_w_up_2", "l0_ffn_w_down_2", "l1_mix_norm_2", "l1_da_w_qkv_2", "l1_da_q_norm_2",
    "l1_da_k_norm_2", "l1_da_lambda_q1_2", "l1_da_lambda_k1_2", "l1_da_lambda_q2_2", "l1_da_lambda_k2_2",
    "l1_da_subln_2", "l1_da_w_out_2", "l1_moe_norm_2", "l1_moe_w_router_2", "l1_moe_w_gate_2",
    "l1_moe_w_up_2", "l1_moe_w_down_2",
]


def kernel(**inputs):
    import numpy as _np
    import concourse.bacc as _bacc
    from concourse import mybir as _mybir
    from concourse.bass_utils import run_bass_kernel_spmd as _run

    nc = _bacc.Bacc("TRN2", target_bir_lowering=False, num_devices=1)
    arrays, w = {}, {}
    for name in INPUTS:
        a = _np.ascontiguousarray(inputs[name])
        arrays[f"in_{name}"] = a
        w[name] = nc.dram_tensor(f"in_{name}", a.shape, _mybir.dt.from_np(a.dtype), kind="ExternalInput").ap()
    tables = shape_tables()
    arrays["in_tables"] = tables
    w["tables"] = nc.dram_tensor("in_tables", tables.shape, _mybir.dt.float32, kind="ExternalInput").ap()
    out = nc.dram_tensor("out", (1, S, D), _mybir.dt.float32, kind="ExternalOutput").ap()
    build(nc, w, out)
    r = _run(nc, [arrays], core_ids=[0])
    return r.results[0]["out"]
```

```python
import math

import numpy as np

import concourse.bass as bass
from concourse import mybir

F32 = mybir.dt.float32
I32 = mybir.dt.int32
ALU = mybir.AluOpType
ACT = mybir.ActivationFunctionType
AX = mybir.AxisListType.X

P = 128
D = 1024
S = 256
T = S // P
DC = D // P
SSD_H, SSD_P, SSD_G, SSD_N = 16, 64, 2, 128
SSD_INNER = SSD_H * SSD_P
CONV_K = 4
CONV_DIM = SSD_INNER + 2 * SSD_G * SSD_N
CONV_C = CONV_DIM // P
SB_H = 8
HD = 64
SB_W = SB_H * HD
Q_RANK, KV_RANK, NOPE, ROPE, V_DIM = 256, 128, 64, 32, 64
MLA_H = 8
MLA_K = NOPE + ROPE
FOX_H = 8
FOX_W = FOX_H * HD
SG_W = 2 * D
SG_G = 8
SG_C = SG_W // SG_G
DA_H = 8
ROT = 16
BLK = 256
MOE_E, MOE_GRP = 16, 4
MOE2_E, MOE2_FF = 8, 3584
DENSE_FF = 2816
ALPHA = 4.0 ** 0.25
LN_EPS, RMS_EPS = 1e-5, 1e-6
LAMBDA_INIT = 0.8 - 0.6 * math.exp(-0.3)
NEG = -1.0e30
PW = 4096
PSLOTS = 2
ROPE_THETA, ROPE_THETA_2 = 10000.0, 500000.0


def shape_tables():
    inv = (np.float32(ROPE_THETA) ** (-(np.arange(0, ROPE, 2, dtype=np.float32) / np.float32(ROPE)))).astype(np.float32)
    ang = (np.arange(S, dtype=np.float32)[:, None] * inv[None, :]).astype(np.float32)
    inv2 = (np.float32(1.0) / (np.float32(ROPE_THETA_2) ** (np.arange(0, ROT, 2, dtype=np.float32) / np.float32(ROT)))).astype(np.float32)
    return np.concatenate([np.cos(ang), np.sin(ang), np.tile(inv2[None, :], (S, 1))], axis=1).astype(np.float32)


def build(nc, w, out):
    sems = {}

    def sem(name):
        if name not in sems:
            sems[name] = nc.alloc_semaphore(name)
        return sems[name]

    def sb(name, shape, dt=F32):
        return nc.alloc_sbuf_tensor(name, shape, dt).ap()

    h = sb("h", [P, T, D])
    xT = sb("xT", [P, DC, S])
    ffw_gu = sb("ffw_gu", [P, 2, DC, 2 * BLK])
    ffw_d = sb("ffw_d", [P, 2, BLK // P, D])
    pieces = sb("pieces", [P, PSLOTS, PW])
    norm_vec = sb("norm_vec", [P, 2 * D])
    row_index = sb("row_index", [P, P])
    ident = sb("ident", [P, P])
    ones = sb("ones", [P, P])
    upto = sb("upto", [P, P])
    above = sb("above", [P, P])
    atleast = sb("atleast", [P, P])
    mask_causal = sb("mask_causal", [P, 3, P])
    mask_strict = sb("mask_strict", [P, 3, P])
    keep_strict = sb("keep_strict", [P, 3, P])
    ARENA = 22312
    SMALL = 896
    arena = sb("arena", [P, ARENA])
    small = sb("small", [P, SMALL])

    psum = [nc.alloc_psum_tensor(f"bank{i}", [P, 512], F32).ap() for i in range(8)]

    par = {}
    par_loads = []

    def param(name, shape, src, dt=F32):
        par[name] = sb("par_" + name, shape, dt)
        par_loads.append((par[name], src))

    def bcast(v):
        return v.partition_broadcast(P)

    param("conv_w", [P, CONV_K, CONV_C], w["ev_conv_w"][0].rearrange("k (c p) -> p k c", p=P))
    param("conv_b", [P, CONV_C], w["ev_conv_b"][0].rearrange("(c p) -> p c", p=P))
    param("dt_bias", [P, SSD_H], bcast(w["ev_dt_bias"][0]))
    param("a_log", [P, SSD_H], bcast(w["ev_a_log"][0]))
    param("d_skip", [P, SSD_H], bcast(w["ev_d_skip"][0]))
    param("ssd_norm", [P, 2, 4], w["ev_norm_g"][0].rearrange("(k p c) -> p k c", k=2, c=4))
    param("q_norm", [P, 2], w["od_q_norm_g"][0].rearrange("(c p) -> p c", p=P))
    param("kv_norm", [P, 1], w["od_kv_norm_g"][0].rearrange("(c p) -> p c", p=P))
    param("f_bias", [P, FOX_H], bcast(w["od_f_bias"][0]))
    for i in range(2):
        param(f"route_b{i}", [P, 20], None)
        par_loads.pop()
        par_loads.append((par[f"route_b{i}"][:, 0:4], bcast(w["moe_b_group"][i])))
        par_loads.append((par[f"route_b{i}"][:, 4:20], bcast(w["moe_b_expert"][i])))
        param(f"route_w{i}", [P, DC, 20], None)
        par_loads.pop()
        par_loads.append((par[f"route_w{i}"][:, :, 0:4], w["moe_w_group"][i].rearrange("(p c) n -> p c n", c=DC)))
        par_loads.append((par[f"route_w{i}"][:, :, 4:20], w["moe_w_expert"][i].rearrange("(p c) n -> p c n", c=DC)))
    param("route_w2", [P, DC, MOE2_E], w["l1_moe_w_router_2"].rearrange("(p c) n -> p c n", c=DC))
    for name in ("l0_mix_norm_2", "l0_ffn_norm_2", "l1_mix_norm_2", "l1_moe_norm_2"):
        param(name, [P, DC], w[name].rearrange("(p c) -> p c", c=DC))
    param("b_spatial", [P, SG_G], w["l0_sg_b_spatial_2"].rearrange("g t -> t g"))
    param("da_q_norm", [P, HD], bcast(w["l1_da_q_norm_2"]))
    param("da_k_norm", [P, HD], bcast(w["l1_da_k_norm_2"]))
    param("lam", [P, 4, HD], None)
    par_loads.pop()
    for i, name in enumerate(("q1", "k1", "q2", "k2")):
        par_loads.append((par["lam"][:, i, :], bcast(w[f"l1_da_lambda_{name}_2"])))
    param("subln", [P, P], bcast(w["l1_da_subln_2"]))
    param("tables", [P, T, 40], w["tables"].rearrange("(j p) n -> p j n", p=P))
    param("positions", [P, T], w["positions_2"].rearrange("a (j p) -> p (a j)", p=P), I32)

    piece_list = []

    def piece(src, shape):
        piece_list.append((src, shape))
        return len(piece_list) - 1

    def piece_ap(n):
        shape = piece_list[n][1]
        size = int(np.prod(shape[1:]))
        flat = pieces[:, n % PSLOTS, 0:size]
        if len(shape) == 2:
            return flat
        return flat.rearrange("p (a b) -> p a b", a=shape[1])

    def columns(mat, c0, c1):
        return piece(mat[:, c0:c1].rearrange("(p c) n -> p c n", c=DC), [P, DC, c1 - c0])

    def rows(mat, k):
        return piece(mat[512 * k:512 * (k + 1), :].rearrange("(p c) n -> p c n", c=4), [P, 4, D])

    ev = w["ev_w_in"][0]
    o = SSD_INNER
    even_pieces = [("z", "tok", columns(ev, 0, 512), 512), ("z", "tok", columns(ev, 512, 1024), 512)]
    even_pieces += [("xbc", "feat", columns(ev, o + 512 * i, o + 512 * (i + 1)), 512) for i in range(3)]
    o += CONV_DIM
    even_pieces += [("dt", "tok", columns(ev, o, o + SSD_H), SSD_H)]
    o += SSD_H
    even_pieces += [("q", "feat", columns(ev, o, o + 512), 512), ("k", "feat", columns(ev, o + 512, o + 1024), 512),
                    ("v", "tok", columns(ev, o + 1024, o + 1536), 512)]
    even_out = [rows(w["ev_w_out"][0], k) for k in range(3)]
    EVEN_END = len(piece_list)
    od = w["od_w_in"][0]
    o = Q_RANK + KV_RANK + ROPE
    odd_pieces = [("c", "tok", columns(od, 0, o), o), ("q", "feat", columns(od, o, o + 512), 512),
                  ("k", "feat", columns(od, o + 512, o + 1024), 512),
                  ("v", "tok", columns(od, o + 1024, o + 1536), 512),
                  ("f", "tok", columns(od, o + 1536, o + 1536 + FOX_H), FOX_H)]
    odd_qup = piece(w["od_w_q_up"][0].rearrange("(c p) n -> p c n", p=P), [P, 2, MLA_H * MLA_K])
    odd_kvup = piece(w["od_w_kv_up"][0], [P, MLA_H * (NOPE + V_DIM)])
    odd_out = [rows(w["od_w_out"][0], k) for k in range(2)]
    ODD_END = len(piece_list)
    sg_in = w["l0_sg_w_in_2"]
    sg_pieces = [("z", "tok", columns(sg_in, 512 * i, 512 * (i + 1)), 512) for i in range(8)]
    sg_spatial = piece(w["l0_sg_w_spatial_2"].rearrange("g t s -> t g s"), [P, SG_G, P])
    sg_out = [rows(w["l0_sg_w_out_2"], k) for k in range(4)]
    SG_END = len(piece_list)
    qkv = w["l1_da_w_qkv_2"]
    da_pieces = [("qkv", "tok", columns(qkv, 512 * i, 512 * (i + 1)), 512) for i in range(6)]
    da_out = [rows(w["l1_da_w_out_2"], k) for k in range(2)]
    DA_END = len(piece_list)

    FIRST_P, FIRST_O, PHASE, MIXER = {}, {}, {}, {}
    at_p = at_o = 0
    for k, (t, plan, outs) in enumerate((("ev", even_pieces, even_out), ("od", odd_pieces, odd_out),
                                         ("sg", sg_pieces, sg_out), ("da", da_pieces, da_out))):
        FIRST_P[t], FIRST_O[t], MIXER[t] = at_p, at_o, k
        at_p, at_o = at_p + len(plan), at_o + len(outs)
    for k, t in enumerate(("ev", "m0", "od", "m1", "sg", "ff", "da", "m2")):
        PHASE[t] = k
    FIRST_U = {"mla": 0, "fox": MLA_H, "dat": MLA_H + FOX_H}
    ROUTER = {"m0": 0, "m1": 1, "m2": 2}

    def full_wait(eng, t, half, n):
        eng.wait_ge(sem(f"bank{half}_full"), FIRST_P[t] + n + 1)

    def read_wait(eng, t, half, n):
        eng.wait_ge(sem(f"bank{half}_read"), FIRST_P[t] + n)

    released = {}
    for t, plan, outs in (("ev", even_pieces, even_out), ("od", odd_pieces, odd_out), ("sg", sg_pieces, sg_out),
                          ("da", da_pieces, da_out)):
        for k, (_, _, n, _) in enumerate(plan):
            released[n] = ("bank1_full", FIRST_P[t] + k + 1)
        for k, n in enumerate(outs):
            released[n] = ("out_piece", FIRST_O[t] + k + 1)
    released[odd_qup], released[odd_kvup] = ("od_qup", 1), ("od_kvup", 1)
    released[sg_spatial] = ("sg_w_turned", 1)

    def piece_wait(eng, n):
        eng.wait_ge(sem(f"piece_landed{n % PSLOTS}"), 16 * (n // PSLOTS + 1))

    counts = {"dve": 0, "act": 0}

    def vlink(ins, *also):
        counts["dve"] += 1
        ins.then_inc(sem("vector_step"), 1)
        nc.vector.wait_ge(sem("vector_step"), counts["dve"])
        for s in also:
            nc.vector.sem_inc(s, 1)

    V = nc.vector

    arena_used = []

    def minus_abs(dst, x):
        return V.scalar_tensor_tensor(out=dst, in0=x, scalar=-1.0, in1=x, op0=ALU.mult, op1=ALU.min)

    def carver():
        used = [0]

        def carve(*shape):
            size = int(np.prod(shape))
            at = used[0]
            used[0] += size
            assert used[0] <= ARENA, used[0]
            arena_used.append(used[0])
            flat = arena[:, at:at + size]
            if len(shape) == 1:
                return flat
            names = "abcd"[:len(shape)]
            return flat.rearrange(f"p ({' '.join(names)}) -> p {' '.join(names)}",
                                  **{n: s for n, s in zip(names, shape)})
        return carve

    small_at = [0]

    def tiny(*shape):
        size = int(np.prod(shape))
        at = small_at[0]
        small_at[0] += size
        assert small_at[0] <= SMALL, small_at[0]
        flat = small[:, at:at + size]
        if len(shape) == 1:
            return flat
        names = "abcd"[:len(shape)]
        return flat.rearrange(f"p ({' '.join(names)}) -> p {' '.join(names)}",
                              **{n: s for n, s in zip(names, shape)})

    def over(ap, axis, n):
        a = ap.unsqueeze(axis)
        shape = list(a.shape)
        shape[axis] = n
        return a.to_broadcast(shape)

    stats, moments = tiny(T, 2, 6), tiny(T, 2)
    sq, rstd = tiny(T), tiny(T)
    root_y, root_t = tiny(T * 2 * 16), tiny(T * 2 * 16)
    roots = {"asked": 0, "answered": 0}

    def rsqrt_scalar(act, x, n):
        roots["answered"] += 1
        act.wait_ge(sem("root_asked"), roots["answered"])
        nc.scalar.activation(root_y[:, 0:n], x, ACT.Ln).then_inc(sem("root_ln"), 1)
        act.wait_ge(sem("root_ln"), roots["answered"])
        nc.scalar.activation(root_y[:, 0:n], root_y[:, 0:n], ACT.Exp, scale=-0.5).then_inc(sem("root_found"), 1)

    def rsqrt_vector(x, dst, n):
        roots["asked"] += 1
        V.sem_inc(sem("root_asked"), 1)
        V.wait_ge(sem("root_found"), roots["asked"])
        y, u = root_y[:, 0:n], root_t[:, 0:n]
        vlink(V.tensor_tensor(u, y, y, ALU.mult))
        vlink(V.tensor_tensor(u, u, x, ALU.mult))
        vlink(V.tensor_scalar(u, u, -0.5, 1.5, ALU.mult, ALU.add))
        vlink(V.tensor_tensor(dst, u, y, ALU.mult))

    def layer_norm():
        for j in range(T):
            for k in range(2):
                vlink(V.bn_stats(out=stats[:, j, k, :], in_=h[:, j, 512 * k:512 * (k + 1)]))
            vlink(V.bn_aggr(out=moments[:, j, :], in_=stats[:, j]))
        vlink(V.tensor_scalar(sq, moments[:, :, 1], LN_EPS, None, ALU.add))
        rsqrt_vector(sq, rstd, T)
        for j in range(T):
            vlink(V.tensor_scalar(h[:, j, :], h[:, j, :], moments[:, j, 0:1], rstd[:, j:j + 1], ALU.subtract, ALU.mult))
            vlink(V.tensor_tensor(h[:, j, :], h[:, j, :], norm_vec[:, 0:D], ALU.mult))
            vlink(V.tensor_tensor(h[:, j, :], h[:, j, :], norm_vec[:, D:2 * D], ALU.add))

    def rms_scale(src, junk, n, scale_out):
        for j in range(T):
            vlink(V.tensor_tensor_reduce(out=junk, in0=src[:, j, :], in1=src[:, j, :], scale=1.0, scalar=0.0,
                                         op0=ALU.mult, op1=ALU.add, accum_out=sq[:, j:j + 1]))
        vlink(V.tensor_scalar(sq, sq, 1.0 / n, RMS_EPS, ALU.mult, ALU.add))
        rsqrt_vector(sq, scale_out, T)

    def to_features_tensor(pe, t, src):
        for c in range(DC):
            for j in range(T):
                bank = psum[c // 2]
                last = nc.tensor.transpose(bank[:, (c % 2) * S + j * P:(c % 2) * S + (j + 1) * P],
                                           src[:, j, :].rearrange("t (p c) -> t c p", c=DC)[:, c, :], ident)
            if c % 2:
                last.then_inc(sem("xt_turned"), 1)

    def to_features_vector(t, gain=None):
        for b in range(DC // 2):
            V.wait_ge(sem("xt_turned"), DC // 2 * PHASE[t] + b + 1)
            src = psum[b].rearrange("p (c t) -> p c t", c=2)
            if gain is None:
                ins = V.tensor_copy(xT[:, 2 * b:2 * b + 2, :], src)
            else:
                ins = V.tensor_tensor(xT[:, 2 * b:2 * b + 2, :], src, over(gain[:, 2 * b:2 * b + 2], 2, S), ALU.mult)
            vlink(ins, *([sem("xt_ready")] if b == DC // 2 - 1 else []))

    def project_tensor(pe, t, plan):
        pe.wait_ge(sem("xt_ready"), PHASE[t] + 1)
        for n, (_, kind, g, cols) in enumerate(plan):
            piece_wait(pe, g)
            if n >= 3:
                read_wait(pe, t, 0, n - 2)
                read_wait(pe, t, 1, n - 2)
            wt = piece_ap(g)
            for half in range(2):
                bank = psum[2 * (n % 3) + half]
                if kind == "tok":
                    for c in range(DC):
                        last = nc.tensor.matmul(bank[:, 0:cols], xT[:, c, half * P:(half + 1) * P], wt[:, c, :],
                                                start=(c == 0), stop=(c == DC - 1))
                else:
                    for m in range(2):
                        m0 = (2 * half + m) * P
                        for c in range(DC):
                            last = nc.tensor.matmul(bank[:, m * S:(m + 1) * S], wt[:, c, m0:m0 + P], xT[:, c, :],
                                                    start=(c == 0), stop=(c == DC - 1))
                last.then_inc(sem(f"bank{half}_full"), 1)

    def out_tensor(pe, t, mix, mixT, plan):
        pe.wait_ge(sem("mix_ready"), MIXER[t] + 1)
        g = 0
        for k in range(len(plan)):
            for c in range(4):
                for j in range(T):
                    b = 4 + g // 4 % 2
                    if g % 4 == 0 and g >= 8:
                        pe.wait_ge(sem("mixt_read"), 2 * FIRST_O[t] + g // 4 - 1)
                    last = nc.tensor.transpose(psum[b][:, (g % 4) * P:(g % 4 + 1) * P],
                                               mix[:, j, 512 * k:512 * (k + 1)].rearrange("t (p c) -> t c p", c=4)[:, c, :],
                                               ident)
                    g += 1
                    if g % 4 == 0:
                        last.then_inc(sem("mixt_turned"), 1)
        for k, n in enumerate(plan):
            piece_wait(pe, n)
            pe.wait_ge(sem("mixt_read"), 2 * FIRST_O[t] + 2 * k + 2)
            wt = piece_ap(n)
            for j in range(T):
                for half in range(2):
                    for c in range(4):
                        last = nc.tensor.matmul(psum[2 * j + half], mixT[:, k, c, j * P:(j + 1) * P],
                                                wt[:, c, half * 512:(half + 1) * 512],
                                                start=(k == 0 and c == 0), stop=(k == len(plan) - 1 and c == 3))
            last.then_inc(sem("out_piece"), 1)

    def out_vector(t, mixT, n_pieces, scale, gain=None):
        for g in range(2 * n_pieces):
            V.wait_ge(sem("mixt_turned"), 2 * FIRST_O[t] + g + 1)
            k, c0 = g // 2, 2 * (g % 2)
            src = psum[4 + g % 2].rearrange("p (c t) -> p c t", c=2)
            dst = mixT[:, k, c0:c0 + 2, :]
            if gain is not None and k < gain.shape[1]:
                ins = V.tensor_tensor(dst, src, over(gain[:, k, c0:c0 + 2], 2, S), ALU.mult)
            else:
                ins = V.tensor_copy(dst, src)
            ins.then_inc(sem("mixt_read"), 1)
        V.wait_ge(sem("out_piece"), FIRST_O[t] + n_pieces)
        for j in range(T):
            for half in range(2):
                hv = h[:, j, half * 512:(half + 1) * 512]
                vlink(V.scalar_tensor_tensor(out=hv, in0=hv, scalar=scale, in1=psum[2 * j + half],
                                             op0=ALU.mult, op1=ALU.add))

    TRI = [(0, 0), (1, 0), (1, 1)]

    def attention_tensor(pe, t, units, logits, probs, probsT, value, dv):
        U0 = FIRST_U[t]
        for u in range(units + 2):
            if u < units:
                if u >= 2:
                    pe.wait_ge(sem("at_masked"), U0 + u - 1)
                logits(u, psum[u % 2]).then_inc(sem("at_logits"), 1)
            if 1 <= u <= units:
                v = u - 1
                pe.wait_ge(sem("at_probs"), U0 + v + 1)
                if v >= 2:
                    pe.wait_ge(sem("at_probst"), U0 + v - 1)
                for i in range(3):
                    last = nc.tensor.transpose(psum[2 + v % 2][:, i * P:(i + 1) * P], probs[:, v % 2, i, :], ident)
                last.then_inc(sem("at_turned"), 1)
            if u >= 2:
                v = u - 2
                pe.wait_ge(sem("at_probst"), U0 + v + 1)
                if v >= 2:
                    pe.wait_ge(sem("at_written"), U0 + v - 1)
                for i, (j, s) in enumerate(TRI):
                    last = nc.tensor.matmul(psum[4 + v % 2][:, j * dv:(j + 1) * dv], probsT[:, v % 2, i, :], value(v, s),
                                            start=(s == 0), stop=(s == j))
                last.then_inc(sem("at_outputs"), 1)

    def attention_scalar(act, t, units, scale, masked, nbias, probs, sums, probsT):
        U0 = FIRST_U[t]
        for u in range(units + 1):
            if u < units:
                act.wait_ge(sem("at_masked"), U0 + u + 1)
                if u >= 2:
                    act.wait_ge(sem("at_turned"), U0 + u - 1)
                for j, (a, b) in enumerate(((0, 1), (1, 3))):
                    ins = nc.scalar.activation(probs[:, u % 2, a:b, :], masked[:, u % 2, a:b, :], ACT.Exp,
                                               bias=nbias[:, u, j:j + 1], scale=scale, accum_out=sums[:, u, j:j + 1])
                ins.then_inc(sem("at_probs"), 1)
            if u >= 1:
                v = u - 1
                act.wait_ge(sem("at_turned"), U0 + v + 1)
                if v >= 2:
                    act.wait_ge(sem("at_outputs"), U0 + v - 1)
                nc.scalar.copy(probsT[:, v % 2, :, :], psum[2 + v % 2][:, 0:3 * P].rearrange("p (i t) -> p i t", i=3))\
                    .then_inc(sem("at_probst"), 1)

    def attention_vector(t, units, scale, mask_of, masked, nbias, sums, write):
        U0 = FIRST_U[t]
        for u in range(units + 1):
            if u < units:
                V.wait_ge(sem("at_logits"), U0 + u + 1)
                if u >= 2:
                    V.wait_ge(sem("at_probs"), U0 + u - 1)
                z = psum[u % 2][:, 0:3 * P].rearrange("p (i s) -> p i s", i=3)
                mask = mask_of(u)
                for j, (a, b) in enumerate(((0, 1), (1, 3))):
                    vlink(V.tensor_tensor_reduce(out=masked[:, u % 2, a:b, :], in0=z[:, a:b, :], in1=mask[:, a:b, :],
                                                 scale=1.0, scalar=-3.0e38, op0=ALU.add, op1=ALU.max,
                                                 accum_out=nbias[:, u, j:j + 1]))
                vlink(V.tensor_scalar(nbias[:, u, :], nbias[:, u, :], -scale, None, ALU.mult), sem("at_masked"))
            if u >= 1:
                v = u - 1
                V.wait_ge(sem("at_outputs"), U0 + v + 1)
                vlink(V.reciprocal(sums[:, v, :], sums[:, v, :]))
                write(v, psum[4 + v % 2], sums[:, v, :], sem("at_written"))

    def setup_gpsimd(pool):
        for ap, src in par_loads:
            pool.dma_start(ap, src, allow_slow_non_contiguous=True).then_inc(sem("params_landed"), 16)
        g = nc.gpsimd
        for m, v in ((ident, 0.0), (ones, 1.0), (upto, 1.0), (above, 1.0), (atleast, 1.0), (mask_causal, 0.0),
                     (mask_strict, 0.0), (keep_strict, 1.0)):
            last = g.memset(m, v)
        last.then_inc(sem("const_filled"), 1)
        pool.wait_ge(sem("const_filled"), 1)

        g.iota(row_index, [[1, P]], base=0, channel_multiplier=0, allow_small_or_imprecise_dtypes=True)\
            .then_inc(sem("index_ready"), 1)

        def select(m, op, fill, cm, step, base=0):
            return g.affine_select(out=m, in_=m, compare_op=op, fill=fill, base=base, pattern=[[step, P]],
                                   channel_multiplier=cm)
        select(ident, ALU.not_equal, 1.0, 1, -1)
        select(upto, ALU.is_ge, 0.0, -1, 1)
        select(above, ALU.is_gt, 0.0, 1, -1)
        select(atleast, ALU.is_ge, 0.0, 1, -1)
        for i in (0, 2):
            select(mask_causal[:, i, :], ALU.is_ge, NEG, 1, -1)
            select(mask_strict[:, i, :], ALU.is_gt, NEG, -1, 1)
            last = select(keep_strict[:, i, :], ALU.is_gt, 0.0, -1, 1)
        last.then_inc(sem("const_ready"), 1)

    def phases_gpsimd(pool):
        plan = [(0, w["ln1_g"][0], w["ln1_b"][0], None), (1, w["ln2_g"][0], w["ln2_b"][0], "m0"),
                (2, w["ln1_g"][1], w["ln1_b"][1], None), (3, w["ln2_g"][1], w["ln2_b"][1], "m1"),
                (4, w["l0_sg_v_norm_2"][0:D], w["l0_sg_v_norm_2"][D:2 * D], None), (7, None, None, "m2")]
        for phase, a, b, t in plan:
            if phase:
                pool.wait_ge(sem("phase_done"), phase)
            if a is not None:
                pool.dma_start(norm_vec[:, 0:D], bcast(a)).then_inc(sem("norm_landed"), 16)
                pool.dma_start(norm_vec[:, D:2 * D], bcast(b)).then_inc(sem("norm_landed"), 16)
            if t is not None:
                zero_gpsimd(pool, t)

    ca = carver()
    zs = ca(T, SSD_INNER)
    xp_flat = ca(CONV_C * (S + CONV_K - 1))
    xp = xp_flat.rearrange("p (c t) -> p c t", c=CONV_C)
    xc = ca(CONV_C, S)
    sbq, sbk, sbv = ca(4, S), ca(4, S), ca(T, SB_W)
    xs_tok, xdt = ca(T, SSD_INNER), ca(T, SSD_INNER)
    ev_mix = ca(T, SSD_INNER + SB_W)
    b_tok = ca(T, SSD_G, P)
    cbm = ca(T, SSD_G, P)
    steps = ca(2, 4, P)
    decay = ca(2, 4, P)
    sb_w = ca(2, 3, P)
    sb_e = xc[:, 0:3, :].rearrange("p c t -> p (c t)").rearrange("p (b i t) -> p b i t", b=2, i=3)
    sb_l = xc[:, 3:6, :].rearrange("p c t -> p (c t)").rearrange("p (b i t) -> p b i t", b=2, i=3)
    ev_mixT = xp_flat[:, 0:3 * 4 * S].rearrange("p (k c t) -> p k c t", k=3, c=4)
    xdd = xT[:, 0:4, :].rearrange("p c t -> p (c t)")
    state = xT[:, 4:8, :].rearrange("p c t -> p (c t)")
    dt_raw, dt, dt_e, da = tiny(T, SSD_H), tiny(T, SSD_H), tiny(T, SSD_H), tiny(T, SSD_H)
    a_neg = tiny(SSD_H)
    carry = tiny(2, T, SSD_H)
    y_bank = {(0, 0): 2, (0, 1): 3, (1, 0): 0, (1, 1): 1}

    def even_tensor(pe):
        t = "ev"
        pe.wait_ge(sem("const_ready"), 1)
        pe.wait_ge(sem("x_landed"), 16)
        to_features_tensor(pe, t, h)
        project_tensor(pe, t, even_pieces)
        groups = [[(j, 4 * k + c) for c in range(4)] for k in range(2) for j in range(T)]
        groups.append([(j, 8 + g) for j in range(T) for g in range(SSD_G)])
        pe.wait_ge(sem("ev_conv_out"), CONV_C)
        for n, group in enumerate(groups):
            if n >= 2:
                pe.wait_ge(sem("ev_tok_read"), n - 1)
            for i, (j, c) in enumerate(group):
                last = nc.tensor.transpose(psum[6 + n % 2][:, i * P:(i + 1) * P], xc[:, c, j * P:(j + 1) * P], ident)
            last.then_inc(sem("ev_tok_turned"), 1)
        read_wait(pe, "ev", 0, len(even_pieces))
        read_wait(pe, "ev", 1, len(even_pieces))
        for j in range(T):
            for g in range(SSD_G):
                i = j * SSD_G + g
                last = nc.tensor.matmul(psum[4][:, i * P:(i + 1) * P], xc[:, 8 + g, j * P:(j + 1) * P],
                                        xc[:, 10 + g, j * P:(j + 1) * P], start=True, stop=True)
        last.then_inc(sem("ev_cb"), 1)
        pe.wait_ge(sem("ev_da_ready"), 1)
        dav = da.rearrange("p j h -> p (j h)")
        nc.tensor.matmul(psum[5][:, 0:32], upto, dav, start=True, stop=True)
        nc.tensor.matmul(psum[5][:, 32:64], above, dav, start=True, stop=True).then_inc(sem("ev_sums"), 1)
        pe.wait_ge(sem("ev_xdd_ready"), 1)
        for g in range(SSD_G):
            last = nc.tensor.matmul(psum[g], b_tok[:, 0, g, :], xdd[:, g * 512:(g + 1) * 512], start=True, stop=True)
        last.then_inc(sem("ev_state_full"), 1)
        for s in range(9):
            if s < 8:
                j, q = divmod(s, 4)
                pe.wait_ge(sem("ev_steps"), s + 1)
                if s >= 2:
                    pe.wait_ge(sem("ev_decay"), s - 1)
                for i in range(4):
                    last = nc.tensor.matmul(psum[6 + s % 2][:, i * P:(i + 1) * P], steps[:, s % 2, i, :], upto,
                                            start=True, stop=True)
                last.then_inc(sem("ev_seg"), 1)
            if s >= 1:
                j, q = divmod(s - 1, 4)
                pe.wait_ge(sem("ev_weights"), s)
                if s - 1 == 4:
                    pe.wait_ge(sem("ev_state"), 1)
                for i in range(4):
                    head = 4 * q + i
                    b = psum[y_bank[j, q // 2]]
                    last = nc.tensor.matmul(b[:, (q % 2) * 256 + i * 64:(q % 2) * 256 + (i + 1) * 64],
                                            decay[:, (s - 1) % 2, i, :], xdt[:, j, head * 64:(head + 1) * 64],
                                            start=True, stop=True)
                last.then_inc(sem("ev_diag"), 1)
        for g in range(SSD_G):
            last = nc.tensor.matmul(psum[4 + g], xc[:, 10 + g, P:S], state[:, g * 512:(g + 1) * 512], start=True, stop=True)
        last.then_inc(sem("ev_off"), 1)
        pe.wait_ge(sem("ev_ssd_read"), 1)
        for s in range(SB_H + 2):
            if s < SB_H:
                if s >= 2:
                    pe.wait_ge(sem("ev_sb_expo"), s - 1)
                r = slice((s % 2) * 64, (s % 2) * 64 + 64)
                kk, qq = sbk[r, s // 2, :], sbq[r, s // 2, :]
                nc.tensor.matmul(psum[s % 2][:, 0:S], kk[:, 0:P], qq, start=True, stop=True)
                nc.tensor.matmul(psum[s % 2][:, S:3 * P], kk[:, P:S], qq[:, P:S], start=True, stop=True)\
                    .then_inc(sem("ev_sb_z"), 1)
            if 1 <= s <= SB_H:
                v = s - 1
                pe.wait_ge(sem("ev_sb_l"), v + 1)
                lv = sb_l[:, v % 2].rearrange("p i t -> p (i t)")
                cum = psum[2 + v % 2]
                nc.tensor.matmul(cum[:, 0:P], atleast, lv[:, 0:P], start=True, stop=True)
                nc.tensor.matmul(cum[:, P:S], atleast, lv[:, P:S], start=True, stop=False)
                nc.tensor.matmul(cum[:, P:S], ones, lv[:, S:3 * P], start=False, stop=True)
                nc.tensor.matmul(cum[:, S:3 * P], atleast, lv[:, S:3 * P], start=True, stop=True)\
                    .then_inc(sem("ev_sb_cum"), 1)
            if s >= 2:
                v = s - 2
                pe.wait_ge(sem("ev_sb_w"), v + 1)
                vc = slice(v * 64, (v + 1) * 64)
                nc.tensor.matmul(psum[4][:, vc], sb_w[:, v % 2, 0, :], sbv[:, 0, vc], start=True, stop=True)
                nc.tensor.matmul(psum[5][:, vc], sb_w[:, v % 2, 1, :], sbv[:, 0, vc], start=True, stop=False)
                nc.tensor.matmul(psum[5][:, vc], sb_w[:, v % 2, 2, :], sbv[:, 1, vc], start=False, stop=True)\
                    .then_inc(sem("ev_sb_out"), 1)
        out_tensor(pe, t, ev_mix, ev_mixT, even_out)

    def even_scalar(act):
        A = nc.scalar
        n = 0
        for n, (name, _, _, _) in enumerate(even_pieces):
            full_wait(act, "ev", 0, n)
            b0 = psum[2 * (n % 3)]
            if name == "z":
                A.activation(zs[:, 0, n * 512:(n + 1) * 512], b0, ACT.Silu).then_inc(sem("bank0_read"), 1)
            elif name == "xbc":
                c = 4 * (n - 2)
                A.copy(xp[:, c:c + 2, 3:], b0.rearrange("p (c t) -> p c t", c=2)).then_inc(sem("bank0_read"), 1)
            elif name == "dt":
                A.copy(dt_raw[:, 0, :], b0[:, 0:SSD_H]).then_inc(sem("bank0_read"), 1)
            elif name == "q":
                A.mul(sbq[:, 0:2, :], b0.rearrange("p (c t) -> p c t", c=2), HD ** -0.5)\
                    .then_inc(sem("bank0_read"), 1)
            elif name == "k":
                A.copy(sbk[:, 0:2, :], b0.rearrange("p (c t) -> p c t", c=2)).then_inc(sem("bank0_read"), 1)
            else:
                A.copy(sbv[:, 0, :], b0).then_inc(sem("bank0_read"), 1)
        read_wait(act, "ev", 1, 2)
        A.activation(zs[:, 1, :], zs[:, 1, :], ACT.Silu).then_inc(sem("ev_z_ready"), 1)
        for c in range(CONV_C):
            act.wait_ge(sem("ev_conv_sum"), c + 1)
            A.activation(xc[:, c, :], xc[:, c, :], ACT.Silu, bias=par["conv_b"][:, c:c + 1])\
                .then_inc(sem("ev_conv_out"), 1)
        act.wait_ge(sem("ev_dt_negabs"), 1)
        A.activation(dt_e, dt_e, ACT.Exp).then_inc(sem("ev_dt_exp"), 1)
        act.wait_ge(sem("ev_dt_exp"), 1)
        A.activation(dt_e, dt_e, ACT.Ln, bias=1.0).then_inc(sem("ev_dt_ln"), 1)
        A.activation(a_neg, par["a_log"], ACT.Exp).then_inc(sem("ev_a_exp"), 1)
        act.wait_ge(sem("ev_sums"), 1)
        A.activation(carry.rearrange("p a j h -> p (a j h)"), psum[5][:, 0:64], ACT.Exp).then_inc(sem("ev_carry"), 1)
        act.wait_ge(sem("ev_state_full"), 1)
        A.copy(state[:, 0:512], psum[0])
        A.copy(state[:, 512:1024], psum[1]).then_inc(sem("ev_state"), 1)
        for s in range(8):
            act.wait_ge(sem("ev_seg"), s + 1)
            if s >= 2:
                act.wait_ge(sem("ev_diag"), s - 1)
            A.activation(decay[:, s % 2], psum[6 + s % 2].rearrange("p (i l) -> p i l", i=4), ACT.Exp)\
                .then_inc(sem("ev_decay"), 1)
        for s in range(SB_H + 2):
            if s >= 2:
                v = s - 2
                act.wait_ge(sem("ev_sb_expo"), v + 1)
                A.activation(sb_w[:, v % 2], sb_w[:, v % 2], ACT.Exp).then_inc(sem("ev_sb_w"), 1)
            if s < SB_H:
                act.wait_ge(sem("ev_sb_z"), s + 1)
                if s >= 2:
                    act.wait_ge(sem("ev_sb_l"), s - 1)
                A.activation(sb_e[:, s % 2], psum[s % 2][:, 0:3 * P].rearrange("p (i t) -> p i t", i=3), ACT.Abs)\
                    .then_inc(sem("ev_sb_abs"), 1)
                act.wait_ge(sem("ev_sb_abs"), s + 1)
                A.activation(sb_e[:, s % 2], sb_e[:, s % 2], ACT.Exp, scale=-1.0).then_inc(sem("ev_sb_exp"), 1)
                act.wait_ge(sem("ev_sb_exp"), s + 1)
                A.activation(sb_e[:, s % 2], sb_e[:, s % 2], ACT.Ln, bias=1.0).then_inc(sem("ev_sb_ln"), 1)
        rsqrt_scalar(act, sq, T)
        rsqrt_scalar(act, sq, T)

    def even_vector(dve):
        V.memset(xp[:, :, 0:3], 0.0).then_inc(sem("ev_pad"), 1)
        dve.wait_ge(sem("ev_pad"), 1)
        to_features_vector("ev")
        dve.wait_ge(sem("params_landed"), 16 * len(par_loads))
        for n, (name, _, _, _) in enumerate(even_pieces):
            full_wait(dve, "ev", 1, n)
            b1 = psum[2 * (n % 3) + 1]
            b1c = b1.rearrange("p (c t) -> p c t", c=2)
            read = sem("bank1_read")
            if name == "z":
                vlink(V.tensor_copy(zs[:, 1, n * 512:(n + 1) * 512], b1), read)
            elif name == "xbc":
                c = 4 * (n - 2)
                vlink(V.tensor_copy(xp[:, c + 2:c + 4, 3:], b1c), read)
                read_wait(dve, "ev", 0, n + 1)
                for c in range(c, c + 4):
                    vlink(V.tensor_scalar(xc[:, c, :], xp[:, c, 0:S], par["conv_w"][:, 0, c:c + 1], None, ALU.mult))
                    for k in range(1, CONV_K):
                        vlink(V.scalar_tensor_tensor(out=xc[:, c, :], in0=xp[:, c, k:k + S],
                                                     scalar=par["conv_w"][:, k, c:c + 1], in1=xc[:, c, :],
                                                     op0=ALU.mult, op1=ALU.add),
                              *([sem("ev_conv_sum")] if k == CONV_K - 1 else []))
            elif name == "dt":
                vlink(V.tensor_copy(dt_raw[:, 1, :], b1[:, 0:SSD_H]), read)
            elif name == "q":
                vlink(V.tensor_scalar(sbq[:, 2:4, :], b1c, HD ** -0.5, None, ALU.mult), read)
            elif name == "k":
                vlink(V.tensor_copy(sbk[:, 2:4, :], b1c), read)
            else:
                vlink(V.tensor_copy(sbv[:, 1, :], b1), read)
        read_wait(dve, "ev", 0, 6)
        vlink(V.tensor_tensor(dt_raw, dt_raw, over(par["dt_bias"], 1, T), ALU.add))
        vlink(minus_abs(dt_e, dt_raw), sem("ev_dt_negabs"))
        dve.wait_ge(sem("ev_dt_ln"), 1)
        vlink(V.scalar_tensor_tensor(out=dt, in0=dt_raw, scalar=0.0, in1=dt_e, op0=ALU.max, op1=ALU.add))
        dve.wait_ge(sem("ev_a_exp"), 1)
        vlink(V.scalar_tensor_tensor(out=da, in0=dt, scalar=-1.0, in1=over(a_neg, 1, T), op0=ALU.mult, op1=ALU.mult),
              sem("ev_da_ready"))
        for n in range(5):
            dve.wait_ge(sem("ev_tok_turned"), n + 1)
            if n < 4:
                k, j = divmod(n, 2)
                vlink(V.tensor_copy(xs_tok[:, j, k * 512:(k + 1) * 512], psum[6 + n % 2]), sem("ev_tok_read"))
            else:
                vlink(V.tensor_copy(b_tok, psum[6].rearrange("p (j g n) -> p j g n", j=T, g=SSD_G)), sem("ev_tok_read"))
        dve.wait_ge(sem("ev_cb"), 1)
        vlink(V.tensor_tensor(cbm.rearrange("p j g l -> p (j g) l"), psum[4].rearrange("p (i l) -> p i l", i=4),
                              over(upto, 1, 4), ALU.mult))
        for j in range(T):
            vlink(V.tensor_tensor(xdt[:, j, :].rearrange("p (h d) -> p h d", d=SSD_P),
                                  xs_tok[:, j, :].rearrange("p (h d) -> p h d", d=SSD_P),
                                  over(dt[:, j, :], 2, SSD_P), ALU.mult))
        dve.wait_ge(sem("ev_carry"), 1)
        vlink(V.tensor_tensor(xdd.rearrange("p (h d) -> p h d", d=SSD_P),
                              xdt[:, 0, :].rearrange("p (h d) -> p h d", d=SSD_P),
                              over(carry[:, 1, 0, :], 2, SSD_P), ALU.mult), sem("ev_xdd_ready"))
        for s in range(9):
            if s < 8:
                j, q = divmod(s, 4)
                if s >= 2:
                    dve.wait_ge(sem("ev_seg"), s - 1)
                vlink(V.tensor_tensor(steps[:, s % 2], over(above, 1, 4), over(da[:, j, 4 * q:4 * q + 4], 2, P), ALU.mult),
                      sem("ev_steps"))
            if s >= 1:
                j, q = divmod(s - 1, 4)
                dve.wait_ge(sem("ev_decay"), s)
                vlink(V.tensor_tensor(decay[:, (s - 1) % 2], decay[:, (s - 1) % 2], over(cbm[:, j, q // 2, :], 1, 4),
                                      ALU.mult), sem("ev_weights"))
        dve.wait_ge(sem("ev_diag"), 8)
        dve.wait_ge(sem("ev_off"), 1)
        dve.wait_ge(sem("ev_z_ready"), 1)
        for j in range(T):
            for half in range(2):
                heads = slice(8 * half, 8 * half + 8)
                cols = slice(512 * half, 512 * half + 512)

                def by_head(ap):
                    return ap.rearrange("p (h d) -> p h d", d=SSD_P)
                y = ev_mix[:, j, cols]
                vlink(V.tensor_tensor(by_head(y), by_head(xs_tok[:, j, cols]), over(par["d_skip"][:, heads], 2, SSD_P),
                                      ALU.mult))
                vlink(V.tensor_tensor(y, y, psum[y_bank[j, half]], ALU.add))
                if j == 1:
                    off = xdt[:, 0, cols]
                    vlink(V.tensor_tensor(by_head(off), by_head(psum[4 + half]), over(carry[:, 0, 1, heads], 2, SSD_P),
                                          ALU.mult))
                    vlink(V.tensor_tensor(y, y, off, ALU.add))
                vlink(V.tensor_tensor(y, y, zs[:, j, cols], ALU.mult),
                      *([sem("ev_ssd_read")] if (j, half) == (1, 1) else []))
        for s in range(SB_H + 2):
            if s >= 2:
                v = s - 2
                dve.wait_ge(sem("ev_sb_cum"), v + 1)
                if v >= 2:
                    dve.wait_ge(sem("ev_sb_out"), v - 1)
                zv = psum[v % 2][:, 0:3 * P].rearrange("p (i t) -> p i t", i=3)
                cv = psum[2 + v % 2][:, 0:3 * P].rearrange("p (i t) -> p i t", i=3)
                vlink(V.tensor_copy(sb_w[:, v % 2], zv))
                vlink(V.tensor_tensor(sb_w[:, v % 2], sb_w[:, v % 2], cv, ALU.subtract))
                vlink(V.tensor_tensor(sb_w[:, v % 2], sb_w[:, v % 2], mask_strict, ALU.add), sem("ev_sb_expo"))
            if 1 <= s <= SB_H:
                v = s - 1
                dve.wait_ge(sem("ev_sb_ln"), v + 1)
                if v >= 2:
                    dve.wait_ge(sem("ev_sb_cum"), v - 1)
                zv = psum[v % 2][:, 0:3 * P].rearrange("p (i t) -> p i t", i=3)
                vlink(V.scalar_tensor_tensor(out=sb_l[:, v % 2], in0=zv, scalar=0.0, in1=sb_e[:, v % 2],
                                             op0=ALU.max, op1=ALU.add))
                vlink(V.tensor_tensor(sb_l[:, v % 2], sb_l[:, v % 2], keep_strict, ALU.mult), sem("ev_sb_l"))
        rms_scale(ev_mix[:, :, 0:SSD_INNER], xdt[:, 1, :], SSD_INNER, rstd)
        for j in range(T):
            vlink(V.tensor_scalar(ev_mix[:, j, 0:SSD_INNER], ev_mix[:, j, 0:SSD_INNER], rstd[:, j:j + 1], None, ALU.mult))
        dve.wait_ge(sem("ev_sb_out"), SB_H)
        for j in range(T):
            vlink(V.tensor_copy(ev_mix[:, j, SSD_INNER:], psum[4 + j]), *([sem("mix_ready")] if j else []))
        out_vector("ev", ev_mixT, 3, ALPHA, par["ssd_norm"])
        dve.wait_ge(sem("norm_landed"), 32)
        layer_norm()
        dve.sem_inc(sem("phase_done"), 1)

    ca = carver()
    normed_flat = ca(T * D)
    ca(D)
    silu_buf = ca(2, BLK)
    hid = ca(2, BLK)
    hidT = ca(2, 2, P)
    xg = ca(DC, P)
    pick_t = ca(T, P)
    pick_r = ca(T, P)
    yg = ca(D)
    normed = normed_flat.rearrange("p (j d) -> p j d", j=T)
    junk_row = arena[:, T * D:T * D + D]
    gates = tiny(T, MOE_E)
    member = tiny(T, 8)
    row_of = tiny(T, 8)
    unit_row, unit_gate = tiny(T), tiny(T, 4)
    row_gate = tiny(4)
    SLOTS = P

    FFS = {"m0": (0, 0, 0, MOE_GRP, 4), "m1": (16, 16, 4, MOE_GRP, 4), "ff": (32, 32, 8, 1, DENSE_FF // BLK),
           "m2": (43, 54, 8, MOE2_E, MOE2_FF // BLK)}
    CREDIT = 2
    DOWN_CREDIT = 4

    def credits_tensor(pe):
        for name in ("gu_done", "hid_done", "down_read", "scattered", "scatter_read"):
            pe.sem_inc(sem(name), CREDIT)
        pe.sem_inc(sem("down_done"), DOWN_CREDIT)

    def make_step(t, u, i, c):
        b0, s0, _, _, nb = FFS[t]
        if t == "ff":
            blk = b0 + c // 2
            return {"s": s0 + 4 * i + c, "slot": blk % 2, "uses": blk // 2 + i + 1, "par": c % 2, "col": None}
        return {"s": s0 + nb * u + 2 * i + c, "slot": (b0 + c) % 2, "uses": (b0 + c) // 2 + nb // 2 * u + i + 1,
                "par": c % 2, "col": (2 * i + c if nb == 4 else 0)}

    def middle(eng, t, u, fn):
        nb = FFS[t][4]
        period, n = (4, 2 * nb) if t == "ff" else (2, nb)
        loops = (n - 2) // period

        def run(i):
            for c in range(1, period + 1):
                fn(make_step(t, u, i, c), make_step(t, u, i, c - 1))
        if loops == 1:
            run(0)
        else:
            with eng.Fori(0, loops) as i:
                run(i)
        last = make_step(t, u, loops, 1)
        fn(last, make_step(t, u, loops, 0))
        return last

    def units(eng, t, unit):
        n = FFS[t][3]
        with eng.Fori(0, n - 1) as u:
            unit(u, False)
        unit(n - 1, True)

    def gate_up_tensor(pe, st, x, part):
        if part == 0:
            pe.wait_ge(sem(f"gu_landed{st['slot']}"), 32 * st["uses"])
            pe.wait_ge(sem("hid_done"), st["s"] - 1 + CREDIT)
        for c in range(4 * part, 4 * part + 4):
            last = nc.tensor.matmul(psum[st["par"]], x[:, c, :], ffw_gu[:, st["slot"], c, :],
                                    start=(c == 0), stop=(c == DC - 1))
        if part:
            last.then_inc(sem("gu_done"), 1)

    def turn_tensor(pe, st):
        pe.wait_ge(sem("hid_done"), st["s"] + 1 + CREDIT)
        for f in range(2):
            at = st["par"] * BLK + f * P
            last = nc.tensor.transpose(psum[2][:, at:at + P], hid[:, st["par"], f * P:(f + 1) * P], ident)
        last.then_inc(sem("hid_turned"), 1)

    def down_tensor(pe, st):
        pe.wait_ge(sem(f"down_landed{st['slot']}"), 16 * st["uses"])
        pe.wait_ge(sem("hidt_done"), st["s"] + 1)
        for half in range(2):
            pe.wait_ge(sem("down_read"), 2 * (st["s"] - 1) + half + 1 + CREDIT)
            for f in range(2):
                last = nc.tensor.matmul(psum[3 + half], hidT[:, st["par"], f, :],
                                        ffw_d[:, st["slot"], f, half * 512:(half + 1) * 512], start=(f == 0), stop=(f == 1))
            last.then_inc(sem("down_done"), 1)

    def gather_tensor(pe, q, src):
        pe.wait_ge(sem("pick_ready"), q + 1)
        if not (isinstance(q, int) and q == 0):
            pe.wait_ge(sem("scatter_read"), 4 * (q - 1) + CREDIT)
        for c in range(DC):
            for j in range(T):
                last = nc.tensor.matmul(psum[5 + c // 4][:, (c % 4) * P:(c % 4 + 1) * P],
                                        src[:, j, :].rearrange("t (p c) -> t c p", c=DC)[:, c, :], pick_t[:, j, :],
                                        start=(j == 0), stop=(j == T - 1))
            if c % 4 == 3:
                last.then_inc(sem("gathered"), 1)

    def permute_tensor(pe, signal):
        for j in range(T):
            nc.tensor.transpose(psum[7][:, j * P:(j + 1) * P], pick_t[:, j, :], ident)
        for j in range(T):
            last = nc.tensor.matmul(psum[7][:, 256:260], pick_t[:, j, :], unit_gate[:, j, :],
                                    start=(j == 0), stop=(j == T - 1))
        last.then_inc(signal, 1)

    def scatter_tensor(pe, q, s_end):
        pe.wait_ge(sem("pickr_ready"), q + 1)
        pe.wait_ge(sem("down_read"), 2 * s_end + CREDIT)
        pe.wait_ge(sem("scatter_read"), 4 * q + CREDIT)
        for k in range(4):
            j, half = divmod(k, 2)
            if k >= 2:
                pe.wait_ge(sem("scatter_read"), 4 * q + k - 1 + CREDIT)
            nc.tensor.matmul(psum[5 + k % 2], pick_r[:, j, :], yg[:, half * 512:(half + 1) * 512], start=True, stop=True)\
                .then_inc(sem("scattered"), 1)

    def ff_begin_tensor(pe, t, phase, route):
        pe.wait_ge(sem("phase_done"), phase)
        src = h
        if t in ("ff", "m2"):
            pe.wait_ge(sem("normed"), PHASE[t] - 3)
            src = normed
        to_features_tensor(pe, t, src)
        pe.wait_ge(sem("xt_ready"), PHASE[t] + 1)
        if route is not None:
            n = route.shape[2]
            for j in range(T):
                for c in range(DC):
                    last = nc.tensor.matmul(psum[4][:, 32 * j:32 * j + n], xT[:, c, j * P:(j + 1) * P], route[:, c, :],
                                            start=(c == 0), stop=(c == DC - 1))
            last.then_inc(sem("route_logits"), 1)
            pe.wait_ge(sem("route_member"), ROUTER[t] + 1)
            before = keep_strict[:, 0, :]
            nc.tensor.matmul(psum[7][:, 0:8], before, member[:, 0, :], start=True, stop=True)
            nc.tensor.matmul(psum[7][:, 8:16], ones, member[:, 0, :], start=True, stop=False)
            nc.tensor.matmul(psum[7][:, 8:16], before, member[:, 1, :], start=False, stop=True)
            nc.tensor.matmul(psum[7][:, 16:24], ones, member[:, 0, :], start=True, stop=False)
            nc.tensor.matmul(psum[7][:, 16:24], ones, member[:, 1, :], start=False, stop=True)\
                .then_inc(sem("route_rows"), 1)

    def dense_tensor(pe):
        ff_begin_tensor(pe, "ff", 5, None)

        def x(st):
            return xT[:, :, st["par"] * P:(st["par"] + 1) * P]

        def step(st, prev):
            gate_up_tensor(pe, st, x(st), 0)
            turn_tensor(pe, prev)
            gate_up_tensor(pe, st, x(st), 1)
            down_tensor(pe, prev)
        first = make_step("ff", 0, 0, 0)
        gate_up_tensor(pe, first, x(first), 0)
        gate_up_tensor(pe, first, x(first), 1)
        last = middle(pe, "ff", 0, step)
        turn_tensor(pe, last)
        down_tensor(pe, last)

    def moe_tensor(pe, t, phase, route):
        ff_begin_tensor(pe, t, phase, route)
        b0, s0, q0, n_units, nb = FFS[t]

        def first_step(u, q):
            pe.wait_ge(sem("xga_ready"), q + 1)
            pe.wait_ge(sem("xgd_ready"), q + 1)
            st = make_step(t, u, 0, 0)
            gate_up_tensor(pe, st, xg, 0)
            gate_up_tensor(pe, st, xg, 1)

        def step(st, prev):
            gate_up_tensor(pe, st, xg, 0)
            turn_tensor(pe, prev)
            gate_up_tensor(pe, st, xg, 1)
            down_tensor(pe, prev)

        def unit(u, final):
            q = q0 + u
            last = middle(pe, t, u, step)
            if not final:
                gather_tensor(pe, q + 1, normed)
            turn_tensor(pe, last)
            down_tensor(pe, last)
            if not final:
                first_step(u + 1, q + 1)
            scatter_tensor(pe, q, s0 + nb * (u + 1))
            if not final:
                permute_tensor(pe, sem("permuted"))
        gather_tensor(pe, q0, normed)
        permute_tensor(pe, sem("permuted"))
        first_step(0, q0)
        units(pe, t, unit)
        overflow_tensor(pe, t)

    def silu_scalar(act, st):
        act.wait_ge(sem("gu_done"), st["s"] + 1 + CREDIT)
        act.wait_ge(sem("hid_done"), st["s"] - 1 + CREDIT)
        nc.scalar.activation(silu_buf[:, st["par"], :], psum[st["par"]][:, 0:BLK], ACT.Silu).then_inc(sem("silu_done"), 1)

    def hidt_scalar(act, st):
        act.wait_ge(sem("hid_turned"), st["s"] + 1)
        act.wait_ge(sem("down_done"), 2 * (st["s"] - 1) + DOWN_CREDIT)
        nc.scalar.copy(hidT[:, st["par"]].rearrange("p f t -> p (f t)"),
                       psum[2][:, st["par"] * BLK:(st["par"] + 1) * BLK]).then_inc(sem("hidt_done"), 1)

    def rows_scalar(act, t, q):
        act.wait_ge(sem("gathered"), 2 * q + 1)
        if t == "m2":
            for c in range(4):
                ins = nc.scalar.activation(xg[:, c, :], psum[5][:, c * P:(c + 1) * P], ACT.Copy,
                                           scale=par["l1_moe_norm_2"][:, c:c + 1])
        else:
            ins = nc.scalar.copy(xg[:, 0:4, :].rearrange("p c t -> p (c t)"), psum[5])
        ins.then_inc(sem("xga_ready"), 1)

    def ff_scalar(act, t):
        if t in ("ff", "m2"):
            rsqrt_scalar(act, sq, T)

        def step(st, prev):
            hidt_scalar(act, prev)
            silu_scalar(act, st)
        if t == "ff":
            silu_scalar(act, make_step(t, 0, 0, 0))
            hidt_scalar(act, middle(act, t, 0, step))
            return
        act.wait_ge(sem("route_masked"), ROUTER[t] + 1)
        nc.scalar.activation(r_e, r_e, ACT.Exp).then_inc(sem("route_exp"), 1)
        q0 = FFS[t][2]

        def unit(u, final):
            last = middle(act, t, u, step)
            if not final:
                rows_scalar(act, t, q0 + u + 1)
            hidt_scalar(act, last)
            if not final:
                silu_scalar(act, make_step(t, u + 1, 0, 0))
        rows_scalar(act, t, q0)
        silu_scalar(act, make_step(t, 0, 0, 0))
        units(act, t, unit)
        overflow_scalar(act, t)
        if t in ("m0", "m1"):
            rsqrt_scalar(act, sq, T)

    def zero_gpsimd(pool, t):
        q0, n = FFS[t][2], FFS[t][3]
        for q in range(q0, q0 + n):
            pool.wait_ge(sem("scattered"), 4 * q + CREDIT)
            nc.gpsimd.memset(yg, 0.0).then_inc(sem("yg_zeroed"), 1)

    def hidden_vector(dve, st):
        dve.wait_ge(sem("silu_done"), st["s"] + 1)
        V.tensor_tensor(hid[:, st["par"], :], silu_buf[:, st["par"], :], psum[st["par"]][:, BLK:2 * BLK], ALU.mult)\
            .then_inc(sem("hid_done"), 1)

    def add_vector(dve, st, q=None):
        if q is not None:
            dve.wait_ge(sem("yg_zeroed"), q + 1)
            dve.wait_ge(sem("rowgate_ready"), q + 1)
        for half in range(2):
            dve.wait_ge(sem("down_done"), 2 * st["s"] + half + 1 + DOWN_CREDIT)
            cols = slice(half * 512, (half + 1) * 512)
            if q is None:
                dst = h[:, st["par"], cols]
                ins = V.tensor_tensor(dst, psum[3 + half], dst, ALU.add)
            else:
                ins = V.scalar_tensor_tensor(out=yg[:, cols], in0=psum[3 + half], scalar=row_gate[:, st["col"]:st["col"] + 1],
                                             in1=yg[:, cols], op0=ALU.mult, op1=ALU.add)
            ins.then_inc(sem("down_read"), 1)

    def pick_vector(dve, t, u, q):
        if not (isinstance(q, int) and q == 0):
            dve.wait_ge(sem("pick_ready"), q)
        V.tensor_copy(unit_row, row_of[:, :, bass.ds(u, 1)].rearrange("p j a -> p (j a)")).then_inc(sem("unit_picked"), 1)
        cols = gates[:, :, bass.ds(4 * u, 4)] if t != "m2" else gates[:, :, bass.ds(u, 4)]
        V.tensor_copy(unit_gate, cols).then_inc(sem("unit_picked"), 1)
        dve.wait_ge(sem("unit_picked"), 2 * q + 2)
        for j in range(T):
            ins = V.tensor_scalar(pick_t[:, j, :], row_index, unit_row[:, j:j + 1], None, ALU.is_equal)
        ins.then_inc(sem("pick_ready"), 1)

    def rows_vector(dve, t, q):
        dve.wait_ge(sem("gathered"), 2 * q + 2)
        src = psum[6].rearrange("p (c t) -> p c t", c=4)
        if t == "m2":
            ins = V.tensor_tensor(xg[:, 4:8, :], src, over(par["l1_moe_norm_2"][:, 4:8], 2, P), ALU.mult)
        else:
            ins = V.tensor_copy(xg[:, 4:8, :], src)
        ins.then_inc(sem("xgd_ready"), 1)

    def permuted_vector(dve, q, s):
        dve.wait_ge(sem("permuted"), q + 1)
        V.tensor_copy(pick_r.rearrange("p j t -> p (j t)"), psum[7][:, 0:2 * P]).then_inc(sem("pickr_ready"), 1)
        dve.wait_ge(sem("down_read"), 2 * s + CREDIT)
        V.tensor_copy(row_gate, psum[7][:, 256:260]).then_inc(sem("rowgate_ready"), 1)

    def scatter_vector(dve, q):
        for k in range(4):
            j, half = divmod(k, 2)
            dve.wait_ge(sem("scattered"), 4 * q + k + 1 + CREDIT)
            hv = h[:, j, half * 512:(half + 1) * 512]
            V.tensor_tensor(hv, psum[5 + k % 2], hv, ALU.add).then_inc(sem("scatter_read"), 1)

    def ff_vector(dve, t):
        b0, s0, q0, n_units, nb = FFS[t]
        if t == "ff":
            def step(st, prev):
                hidden_vector(dve, st)
                add_vector(dve, prev)
            hidden_vector(dve, make_step(t, 0, 0, 0))
            add_vector(dve, middle(dve, t, 0, step))
            dve.wait_ge(sem("down_read"), 2 * (s0 + 2 * nb) + CREDIT)
            return

        def unit(u, final):
            q = q0 + u
            if not final:
                pick_vector(dve, t, u + 1, q + 1)

            def step(st, prev):
                hidden_vector(dve, st)
                add_vector(dve, prev, q)
            last = middle(dve, t, u, step)
            if not final:
                rows_vector(dve, t, q + 1)
            add_vector(dve, last, q)
            if not final:
                hidden_vector(dve, make_step(t, u + 1, 0, 0))
            scatter_vector(dve, q)
            if not final:
                permuted_vector(dve, q + 1, s0 + nb * (u + 1))
        pick_vector(dve, t, 0, q0)
        rows_vector(dve, t, q0)
        permuted_vector(dve, q0, s0)
        hidden_vector(dve, make_step(t, 0, 0, 0))
        units(dve, t, unit)
        dve.wait_ge(sem("scatter_read"), 4 * (q0 + n_units) + CREDIT)
        overflow_vector(dve, t)

    def load_block(sp, wg, wu, wd, e, b, slot, gu_sem, down_sem, wait_gu, wait_down):
        def part(m, axis):
            m = m.unsqueeze(0) if e is None else m[bass.ds(e, 1)]
            if b is None:
                return m
            return m[:, :, bass.ds(b * BLK, BLK)] if axis else m[:, bass.ds(b * BLK, BLK), :]
        wait_gu()
        for k, m in enumerate((wg, wu)):
            sp.dma_start(ffw_gu[:, slot, :, k * BLK:(k + 1) * BLK],
                         part(m, 1).rearrange("a (p c) n -> p (a c) n", c=DC)).then_inc(gu_sem, 16)
        wait_down()
        sp.dma_start(ffw_d[:, slot], part(wd, 0).rearrange("a (f p) n -> p (a f) n", p=P)).then_inc(down_sem, 16)

    def steps_before(t, n):
        if t == "ff":
            return 31 if isinstance(n, int) and n == 0 else 30 + 2 * n
        if t == "m2":
            return 53 + n
        return FFS[t][1] - 1 + n

    def ff_sync(sp, t, wg, wu, wd):
        b0, _, q0, n_units, nb = FFS[t]

        def load(e, b, n, slot):
            done = steps_before(t, n)
            load_block(sp, wg, wu, wd, e, b, slot, sem(f"gu_landed{slot}"), sem(f"down_landed{slot}"),
                       lambda: sp.wait_ge(sem("gu_done"), done + CREDIT),
                       lambda: sp.wait_ge(sem("down_done"), 2 * done + DOWN_CREDIT))
        if t == "ff":
            for c in range(2):
                load(None, c, c, c)
            with sp.Fori(1, nb // 2) as i:
                for c in range(2):
                    load(None, 2 * i + c, 2 * i + c, c)
            load(None, nb - 1, nb - 1, (nb - 1) % 2)
        elif nb == 4:
            with sp.Fori(0, n_units * nb // 2) as i:
                for c in range(2):
                    load(2 * i + c, None, 2 * i + c, (b0 + c) % 2)
        else:
            with sp.Fori(0, n_units) as u:
                with sp.Fori(0, nb // 2) as i:
                    for c in range(2):
                        load(u, 2 * i + c, nb * u + 2 * i + c, (b0 + c) % 2)
        if t != "ff":
            overflow_sync(sp, t, wg, wu, wd)

    OV_UNIT = {"pe": 3, "dve": 12, "act": 0}
    OV_BLOCK = {"pe": 3, "dve": 4, "act": 1}

    def ov_at(eng, t, u, b, k):
        nb = FFS[t][4]
        return (OV_UNIT[eng] + nb * OV_BLOCK[eng]) * u + OV_BLOCK[eng] * b + k

    def ov_begin(eng, t):
        eng.wait_ge(sem("route_flag"), ROUTER[t] + 1)
        return eng.value_load(flags[0:1, ROUTER[t]:ROUTER[t] + 1], min_val=0, max_val=1)

    def ov_blocks(eng, t, fn):
        nb = FFS[t][4]
        if nb == 4:
            for b in range(nb):
                fn(b)
        else:
            with eng.Fori(0, nb) as b:
                fn(b)

    def overflow_sync(sp, t, wg, wu, wd):
        flag = ov_begin(sp, t)
        b0, s0, q0, n_units, nb = FFS[t]
        with sp.If(flag > 0):
            sp.wait_ge(sem("gu_done"), s0 + nb * n_units + CREDIT)
            sp.wait_ge(sem("down_done"), 2 * (s0 + nb * n_units) + DOWN_CREDIT)
            with sp.Fori(0, n_units) as u:
                def load(b):
                    wait = (lambda: sp.wait_ge(sem(f"ov_dve_{t}"), ov_at("dve", t, u, b, 8)))
                    e, col = (4 * u + b, None) if nb == 4 else (u, b)
                    load_block(sp, wg, wu, wd, e, col, 0, sem(f"ov_load_{t}"), sem(f"ov_load_{t}"), wait, lambda: None)
                ov_blocks(sp, t, load)
            sp.wait_ge(sem(f"ov_pe_{t}"), ov_at("pe", t, n_units, 0, 0))

    def overflow_tensor(pe, t):
        flag = ov_begin(pe, t)
        n_units, nb = FFS[t][3], FFS[t][4]
        done, dve, act = sem(f"ov_pe_{t}"), sem(f"ov_dve_{t}"), sem(f"ov_act_{t}")
        with pe.If(flag > 0):
            with pe.Fori(0, n_units) as u:
                pe.wait_ge(dve, ov_at("dve", t, u, 0, 4))
                for c in range(DC):
                    for j in range(T):
                        last = nc.tensor.matmul(psum[5 + c // 4][:, (c % 4) * P:(c % 4 + 1) * P],
                                                normed[:, j, :].rearrange("t (p c) -> t c p", c=DC)[:, c, :],
                                                pick_t[:, j, :], start=(j == 0), stop=(j == T - 1))
                last.then_inc(done, 1)
                permute_tensor(pe, done)

                def block_of(b):
                    pe.wait_ge(dve, ov_at("dve", t, u, b, 8))
                    pe.wait_ge(sem(f"ov_load_{t}"), 48 * (nb * u + b + 1))
                    for c in range(DC):
                        last = nc.tensor.matmul(psum[0], xg[:, c, :], ffw_gu[:, 0, c, :], start=(c == 0), stop=(c == DC - 1))
                    last.then_inc(done, 1)
                    pe.wait_ge(dve, ov_at("dve", t, u, b, 9))
                    for f in range(2):
                        last = nc.tensor.transpose(psum[2][:, f * P:(f + 1) * P], hid[:, 0, f * P:(f + 1) * P], ident)
                    last.then_inc(done, 1)
                    pe.wait_ge(dve, ov_at("dve", t, u, b, 10))
                    for half in range(2):
                        for f in range(2):
                            last = nc.tensor.matmul(psum[3 + half], hidT[:, 0, f, :],
                                                    ffw_d[:, 0, f, half * 512:(half + 1) * 512], start=(f == 0), stop=(f == 1))
                    last.then_inc(done, 1)
                ov_blocks(pe, t, block_of)
                pe.wait_ge(dve, ov_at("dve", t, u, nb, 8))
                for k in range(4):
                    last = nc.tensor.matmul(psum[(3, 4, 5, 6)[k]], pick_r[:, k // 2, :],
                                            yg[:, (k % 2) * 512:(k % 2 + 1) * 512], start=True, stop=True)
                last.then_inc(done, 1)

    def overflow_scalar(act, t):
        flag = ov_begin(act, t)
        with act.If(flag > 0):
            with act.Fori(0, FFS[t][3]) as u:
                def block_of(b):
                    act.wait_ge(sem(f"ov_pe_{t}"), ov_at("pe", t, u, b, 3))
                    nc.scalar.activation(silu_buf[:, 0, :], psum[0][:, 0:BLK], ACT.Silu).then_inc(sem(f"ov_act_{t}"), 1)
                ov_blocks(act, t, block_of)

    def overflow_vector(dve, t):
        flag = ov_begin(dve, t)
        n_units, nb = FFS[t][3], FFS[t][4]
        done, pe = sem(f"ov_dve_{t}"), sem(f"ov_pe_{t}")
        with dve.If(flag > 0):
            with dve.Fori(0, n_units) as u:
                def step(ins, b, k):
                    ins.then_inc(done, 1)
                    dve.wait_ge(done, ov_at("dve", t, u, b, k))
                rows = row_of[:, :, bass.ds(u, 1)].rearrange("p j a -> p (j a)")
                step(V.tensor_copy(unit_row, rows), 0, 1)
                step(V.tensor_scalar(unit_row, unit_row, -float(SLOTS), None, ALU.add), 0, 2)
                cols = gates[:, :, bass.ds(4 * u, 4)] if nb == 4 else gates[:, :, bass.ds(u, 4)]
                step(V.tensor_copy(unit_gate, cols), 0, 3)
                V.memset(yg, 0.0)
                V.tensor_scalar(pick_t[:, 0, :], row_index, unit_row[:, 0:1], None, ALU.is_equal)
                step(V.tensor_scalar(pick_t[:, 1, :], row_index, unit_row[:, 1:2], None, ALU.is_equal), 0, 4)
                dve.wait_ge(pe, ov_at("pe", t, u, 0, 2))
                for k in range(2):
                    src = psum[5 + k].rearrange("p (c t) -> p c t", c=4)
                    gain = par["l1_moe_norm_2"][:, 4 * k:4 * k + 4]
                    if t == "m2":
                        ins = V.tensor_tensor(xg[:, 4 * k:4 * k + 4, :], src, over(gain, 2, P), ALU.mult)
                    else:
                        ins = V.tensor_copy(xg[:, 4 * k:4 * k + 4, :], src)
                    step(ins, 0, 5 + k)
                step(V.tensor_copy(pick_r.rearrange("p j t -> p (j t)"), psum[7][:, 0:2 * P]), 0, 7)
                V.tensor_copy(row_gate, psum[7][:, 256:260]).then_inc(done, 1)

                def block_of(b):
                    dve.wait_ge(sem(f"ov_act_{t}"), ov_at("act", t, u, b, 1))
                    step(V.tensor_tensor(hid[:, 0, :], silu_buf[:, 0, :], psum[0][:, BLK:2 * BLK], ALU.mult), b, 9)
                    dve.wait_ge(pe, ov_at("pe", t, u, b, 4))
                    step(V.tensor_copy(hidT[:, 0].rearrange("p f t -> p (f t)"), psum[2][:, 0:BLK]), b, 10)
                    dve.wait_ge(pe, ov_at("pe", t, u, b, 5))
                    col = b if nb == 4 else 0
                    for half in range(2):
                        cols = slice(half * 512, (half + 1) * 512)
                        step(V.scalar_tensor_tensor(out=yg[:, cols], in0=psum[3 + half], scalar=row_gate[:, col:col + 1],
                                                    in1=yg[:, cols], op0=ALU.mult, op1=ALU.add), b, 11 + half)
                ov_blocks(dve, t, block_of)
                dve.wait_ge(pe, ov_at("pe", t, u, nb, 3))
                for k in range(4):
                    hv = h[:, k // 2, (k % 2) * 512:(k % 2 + 1) * 512]
                    step(V.tensor_tensor(hv, psum[(3, 4, 5, 6)[k]], hv, ALU.add), nb, 9 + k)

    FFR = {"m0": True, "m1": True, "m2": False}
    logit = tiny(T, 20)
    r_m, r_m2, r_sum, r_g = tiny(T, 1), tiny(T, 1), tiny(T, 1), tiny(T, 1)
    r_eq, r_sc = tiny(T, 8), tiny(T, 8)
    r_grp, r_one, r_two = tiny(T, 4), tiny(T, 8), tiny(T, 8)
    r_e = tiny(T, 12)
    r_sel = tiny(T, 8)
    r_tmp = tiny(T, 4, 4)
    rank = tiny(8)

    flags = sb("flags", [P, 3], I32)

    def first_max(vals, n, value, onehot):
        vlink(V.tensor_reduce(out=value, in_=vals, axis=AX, op=ALU.max))
        vlink(V.tensor_tensor(r_eq[:, :, 0:n], vals, value.to_broadcast([P, T, n]), ALU.is_equal))
        vlink(V.tensor_tensor(r_sc[:, :, 0:n], r_eq[:, :, 0:n], over(rank[:, 0:n], 1, T), ALU.mult))
        vlink(V.tensor_reduce(out=r_m2, in_=r_sc[:, :, 0:n], axis=AX, op=ALU.max))
        vlink(V.tensor_tensor(onehot, r_sc[:, :, 0:n], r_m2.to_broadcast([P, T, n]), ALU.is_equal))

    def route_vector(dve, t, bias):
        grouped = FFR[t]
        n = 4 if grouped else MOE2_E
        cols = 20 if grouped else MOE2_E
        dve.wait_ge(sem("route_logits"), ROUTER[t] + 1)
        src = psum[4][:, 0:32 * T].rearrange("p (j n) -> p j n", j=T)[:, :, 0:cols]
        if grouped:
            vlink(V.tensor_tensor(logit, src, over(bias, 1, T), ALU.add))
            first_max(logit[:, :, 0:4], 4, r_m, r_grp)
            vlink(V.tensor_tensor(r_e[:, :, 0:4], logit[:, :, 0:4], r_m.to_broadcast([P, T, 4]), ALU.subtract))
            for j in range(T):
                vlink(V.tensor_tensor(r_tmp[:, j], logit[:, j, 4:20].rearrange("p (g e) -> p g e", g=4),
                                      over(r_grp[:, j, :], 2, 4), ALU.mult))
                vlink(V.tensor_reduce(out=r_sel[:, j, 0:4], in_=r_tmp[:, j].rearrange("p g e -> p e g"), axis=AX,
                                      op=ALU.add))
            vals = r_sel[:, :, 0:4]
        else:
            vlink(V.tensor_copy(r_sel, src))
            vals = r_sel
        first_max(vals, n, r_m, r_one[:, :, 0:n])
        vlink(V.tensor_tensor(r_e[:, :, 4:4 + n], vals, r_m.to_broadcast([P, T, n]), ALU.subtract))
        vlink(V.scalar_tensor_tensor(out=r_two[:, :, 0:n], in0=r_one[:, :, 0:n], scalar=NEG, in1=vals,
                                     op0=ALU.mult, op1=ALU.add))
        if not grouped:
            vlink(V.tensor_copy(r_e[:, :, 0:4], r_e[:, :, 4:8]))
        else:
            vlink(V.memset(r_e[:, :, 8:12], 0.0))
        first_max(r_two[:, :, 0:n], n, r_g, r_sc[:, :, 0:n])
        vlink(V.tensor_tensor(r_one[:, :, 0:n], r_one[:, :, 0:n], r_sc[:, :, 0:n], ALU.add), sem("route_masked"))
        if grouped:
            vlink(V.memset(member[:, :, 4:8], 0.0))
            vlink(V.tensor_copy(member[:, :, 0:4], r_grp), sem("route_member"))
        else:
            vlink(V.tensor_copy(member, r_one), sem("route_member"))
        dve.wait_ge(sem("route_rows"), ROUTER[t] + 1)
        rows = psum[7][:, 0:16].rearrange("p (j n) -> p j n", j=T)
        vlink(V.scalar_tensor_tensor(out=row_of, in0=rows, scalar=1.0, in1=member, op0=ALU.add, op1=ALU.mult))
        vlink(V.tensor_scalar(row_of, row_of, -1.0, None, ALU.add))
        vlink(V.tensor_reduce(out=r_sum[:, 0], in_=psum[7][:, 16:24], axis=AX, op=ALU.max))
        vlink(V.tensor_scalar(r_sum[:, 0], r_sum[:, 0], SLOTS + 0.5, None, ALU.is_gt))
        vlink(V.tensor_copy(flags[:, ROUTER[t]:ROUTER[t] + 1], r_sum[:, 0]), sem("route_flag"))
        dve.wait_ge(sem("route_exp"), ROUTER[t] + 1)
        vlink(V.tensor_tensor(r_two[:, :, 0:n], r_e[:, :, 4:4 + n], r_one[:, :, 0:n], ALU.mult))
        vlink(V.tensor_reduce(out=r_sum, in_=r_two[:, :, 0:n], axis=AX, op=ALU.add))
        vlink(V.reciprocal(r_sum, r_sum))
        vlink(V.tensor_tensor(r_two[:, :, 0:n], r_two[:, :, 0:n], r_sum.to_broadcast([P, T, n]), ALU.mult))
        if grouped:
            vlink(V.tensor_reduce(out=r_g, in_=r_e[:, :, 0:4], axis=AX, op=ALU.add))
            vlink(V.reciprocal(r_g, r_g))
            vlink(V.tensor_tensor(r_two[:, :, 0:4], r_two[:, :, 0:4], r_g.to_broadcast([P, T, 4]), ALU.mult))
            for j in range(T):
                vlink(V.tensor_tensor(gates[:, j, :].rearrange("p (g e) -> p g e", g=4), over(r_grp[:, j, :], 2, 4),
                                      over(r_two[:, j, 0:4], 1, 4), ALU.mult))
        else:
            vlink(V.memset(gates[:, :, 8:16], 0.0))
            vlink(V.tensor_copy(gates[:, :, 0:8], r_two))

    def moe_first_vector(dve, t, i):
        to_features_vector(t)
        for j in range(T):
            vlink(V.tensor_copy(normed[:, j, :], h[:, j, :]))
            vlink(V.tensor_scalar(h[:, j, :], h[:, j, :], ALPHA, None, ALU.mult))
        route_vector(dve, t, par[f"route_b{i}"])
        ff_vector(dve, t)
        dve.wait_ge(sem("norm_landed"), 32 * (2 * i + 2))
        layer_norm()
        dve.sem_inc(sem("phase_done"), 1)

    def normed_vector(t):
        rms_scale(h, junk_row, D, rstd)
        for j in range(T):
            vlink(V.tensor_scalar(normed[:, j, :], h[:, j, :], rstd[:, j:j + 1], None, ALU.mult),
                  *([sem("normed")] if j else []))

    ca = carver()
    c_tok = ca(T, Q_RANK + KV_RANK + ROPE)
    fox_q, fox_k, fox_v = ca(4, S), ca(4, S), ca(T, FOX_W)
    c_norm = ca(T, Q_RANK + KV_RANK)
    cT = ca(3, S)
    q_cat, k_cat = ca(T, MLA_H, MLA_K), ca(T, MLA_H, MLA_K)
    v_mla = ca(T, MLA_H, V_DIM)
    mla_qT, mla_kT = ca(MLA_H, S), ca(MLA_H, S)
    odd_mix = ca(T, D)
    odd_mixT = ca(2, 4, S)
    at_masked, at_probs, at_probsT = ca(2, 3, P), ca(2, 3, P), ca(2, 3, P)
    fox_sum, fox_neg = ca(S), ca(S)
    mask_chunk = ca(3, P)
    rope_a, rope_b, rope_c, rope_d = (ca(8, 16) for _ in range(4))
    sel = odd_mixT.rearrange("p k c t -> p (k c) t")
    fox_bias = ca(2, 3, P)
    at_nbias, at_sums = tiny(16, 2), tiny(16, 2)
    log_f, f_e, f_x = tiny(T, FOX_H), tiny(T, FOX_H), tiny(T, FOX_H)
    c_rstd = tiny(2, T)

    def odd_tensor(pe):
        t = "od"
        pe.wait_ge(sem("phase_done"), 2)
        to_features_tensor(pe, t, h)
        project_tensor(pe, t, odd_pieces)
        n_p = len(odd_pieces)
        read_wait(pe, "od", 0, n_p)
        read_wait(pe, "od", 1, n_p)
        pe.wait_ge(sem("od_c_normed"), 1)
        for c in range(3):
            for j in range(T):
                last = nc.tensor.transpose(psum[6 + c // 2][:, (c % 2) * S + j * P:(c % 2) * S + (j + 1) * P],
                                           c_norm[:, j, c * P:(c + 1) * P], ident)
        last.then_inc(sem("od_c_turned"), 1)
        pe.wait_ge(sem("od_ct_ready"), 1)
        piece_wait(pe, odd_qup)
        wq = piece_ap(odd_qup)
        for j in range(T):
            for half, (a, b) in enumerate(((0, 512), (512, MLA_H * MLA_K))):
                for c in range(2):
                    last = nc.tensor.matmul(psum[2 * j + half][:, 0:b - a], cT[:, c, j * P:(j + 1) * P], wq[:, c, a:b],
                                            start=(c == 0), stop=(c == 1))
        last.then_inc(sem("od_qup"), 1)
        piece_wait(pe, odd_kvup)
        wkv = piece_ap(odd_kvup)
        for j in range(T):
            for half in range(2):
                last = nc.tensor.matmul(psum[4 + 2 * j + half], cT[:, 2, j * P:(j + 1) * P],
                                        wkv[:, half * 512:(half + 1) * 512], start=True, stop=True)
        last.then_inc(sem("od_kvup"), 1)
        pe.wait_ge(sem("od_cat_ready"), 1)
        for n in range(8):
            src = (q_cat, k_cat)[n // 4]
            if n >= 2:
                pe.wait_ge(sem("od_cat_read"), n - 1)
            for i in range(4):
                hd, j = 2 * (n % 4) + i // 2, i % 2
                last = nc.tensor.transpose(psum[6 + n % 2][0:MLA_K, i * P:(i + 1) * P], src[:, j, hd, :], ident)
            last.then_inc(sem("od_cat_turned"), 1)
        pe.wait_ge(sem("od_cat_read"), 8)

        def mla_logits(u, bank):
            nc.tensor.matmul(bank[:, 0:P], mla_qT[0:MLA_K, u, 0:P], mla_kT[0:MLA_K, u, 0:P], start=True, stop=True)
            return nc.tensor.matmul(bank[:, P:3 * P], mla_qT[0:MLA_K, u, P:S], mla_kT[0:MLA_K, u, :],
                                    start=True, stop=True)
        attention_tensor(pe, "mla", MLA_H, mla_logits, at_probs, at_probsT, lambda u, s: v_mla[:, s, u, :], V_DIM)
        pe.wait_ge(sem("od_logf"), 1)
        nc.tensor.matmul(psum[6][0:FOX_H, 0:P], log_f[:, 0, :], upto, start=True, stop=True)
        nc.tensor.matmul(psum[6][0:FOX_H, P:S], log_f[:, 0, :], ones, start=True, stop=False)
        nc.tensor.matmul(psum[6][0:FOX_H, P:S], log_f[:, 1, :], upto, start=False, stop=True)\
            .then_inc(sem("od_fsum"), 1)
        pe.wait_ge(sem("od_fsum_read"), 1)
        pe.wait_ge(sem("at_written"), MLA_H)

        def fox_logits(u, bank):
            if u >= 2:
                pe.wait_ge(sem("fox_biased"), u - 1)
            fb = psum[6 + u % 2]
            for j, (a, b) in enumerate(((0, P), (P, 3 * P))):
                nc.tensor.matmul(fb[:, a:b], fox_sum[0:FOX_H, j * P:(j + 1) * P], sel[0:FOX_H, u, 0:b - a],
                                 start=True, stop=False)
                last = nc.tensor.matmul(fb[:, a:b], sel[0:FOX_H, u, 0:P], fox_neg[0:FOX_H, 0:b - a],
                                        start=False, stop=True)
            last.then_inc(sem("fox_term"), 1)
            r = slice((u % 2) * 64, (u % 2) * 64 + 64)
            qq, kk = fox_q[r, u // 2, :], fox_k[r, u // 2, :]
            nc.tensor.matmul(bank[:, 0:P], qq[:, 0:P], kk[:, 0:P], start=True, stop=True)
            return nc.tensor.matmul(bank[:, P:3 * P], qq[:, P:S], kk, start=True, stop=True)
        attention_tensor(pe, "fox", FOX_H, fox_logits, at_probs, at_probsT,
                         lambda u, s: fox_v[:, s, u * HD:(u + 1) * HD], HD)
        out_tensor(pe, t, odd_mix, odd_mixT, odd_out)

    def odd_scalar(act):
        A = nc.scalar
        for n, (name, _, _, cols) in enumerate(odd_pieces):
            full_wait(act, "od", 0, n)
            b0 = psum[2 * (n % 3)]
            b0c = b0.rearrange("p (c t) -> p c t", c=2)
            if name == "q":
                ins = A.mul(fox_q[:, 0:2, :], b0c, HD ** -0.5)
            elif name == "k":
                ins = A.copy(fox_k[:, 0:2, :], b0c)
            else:
                ins = A.copy({"c": c_tok, "v": fox_v, "f": f_x}[name][:, 0, :], b0[:, 0:cols])
            ins.then_inc(sem("bank0_read"), 1)
            if name == "c":
                rsqrt_scalar(act, sq, T)
                rsqrt_scalar(act, sq, T)
        act.wait_ge(sem("od_qup"), 1)
        for j in range(T):
            qv = q_cat[:, j].rearrange("p h d -> p (h d)")
            A.copy(qv[:, 0:512], psum[2 * j])
            ins = A.copy(qv[:, 512:], psum[2 * j + 1][:, 0:MLA_H * MLA_K - 512])
        ins.then_inc(sem("od_qcat"), 1)
        act.wait_ge(sem("od_f_negabs"), 1)
        A.activation(f_e, f_e, ACT.Exp).then_inc(sem("od_f_exp"), 1)
        act.wait_ge(sem("od_f_exp"), 1)
        A.activation(f_e, f_e, ACT.Ln, bias=1.0).then_inc(sem("od_f_ln"), 1)
        attention_scalar(act, "mla", MLA_H, MLA_K ** -0.5, at_masked, at_nbias, at_probs, at_sums, at_probsT)
        attention_scalar(act, "fox", FOX_H, 1.0, at_masked, at_nbias[:, 8:], at_probs, at_sums[:, 8:], at_probsT)
        rsqrt_scalar(act, sq, T)

    def rope(x1, x2, cos, sin, tmps):
        a, b, c, d = tmps
        vlink(V.tensor_tensor(a, x1, cos, ALU.mult))
        vlink(V.tensor_tensor(b, x2, sin, ALU.mult))
        vlink(V.tensor_tensor(c, x2, cos, ALU.mult))
        vlink(V.tensor_tensor(d, x1, sin, ALU.mult))
        vlink(V.tensor_tensor(x1, a, b, ALU.subtract))
        vlink(V.tensor_tensor(x2, c, d, ALU.add))

    def odd_vector(dve):
        vlink(V.memset(mask_chunk, 0.0))
        for i in (0, 2):
            vlink(V.memset(mask_chunk[0:64, i, 64:P], NEG))
        to_features_vector("od")
        vlink(V.tensor_copy(sel[0:FOX_H], over(ident[0:FOX_H, 0:FOX_H], 2, S)))
        for n, (name, _, _, cols) in enumerate(odd_pieces):
            full_wait(dve, "od", 1, n)
            b1 = psum[2 * (n % 3) + 1]
            b1c = b1.rearrange("p (c t) -> p c t", c=2)
            if name == "q":
                ins = V.tensor_scalar(fox_q[:, 2:4, :], b1c, HD ** -0.5, None, ALU.mult)
            elif name == "k":
                ins = V.tensor_copy(fox_k[:, 2:4, :], b1c)
            else:
                ins = V.tensor_copy({"c": c_tok, "v": fox_v, "f": f_x}[name][:, 1, :], b1[:, 0:cols])
            vlink(ins, sem("bank1_read"))
            if name == "c":
                read_wait(dve, "od", 0, n + 1)
                for i, (a, b) in enumerate(((0, Q_RANK), (Q_RANK, Q_RANK + KV_RANK))):
                    rms_scale(c_tok[:, :, a:b], q_cat[:, 0].rearrange("p h d -> p (h d)")[:, 0:b - a], b - a, c_rstd[:, i, :])
                    for j in range(T):
                        vlink(V.tensor_scalar(c_norm[:, j, a:b], c_tok[:, j, a:b], c_rstd[:, i, j:j + 1], None, ALU.mult),
                              *([sem("od_c_normed")] if i and j else []))
        read_wait(dve, "od", 0, len(odd_pieces))
        vlink(V.tensor_tensor(f_x, f_x, over(par["f_bias"], 1, T), ALU.add))
        vlink(V.tensor_scalar(f_x, f_x, -1.0, None, ALU.mult))
        vlink(minus_abs(f_e, f_x), sem("od_f_negabs"))
        dve.wait_ge(sem("od_c_turned"), 1)
        vlink(V.tensor_tensor(cT[:, 0:2, :], psum[6].rearrange("p (c t) -> p c t", c=2), over(par["q_norm"], 2, S), ALU.mult))
        vlink(V.tensor_scalar(cT[:, 2, :], psum[7][:, 0:S], par["kv_norm"], None, ALU.mult), sem("od_ct_ready"))
        tab = par["tables"]
        for j in range(T):
            pe_k = c_tok[:, j:j + 1, Q_RANK + KV_RANK:]
            cos, sin = (over(tab[:, j, 16 * i:16 * i + 16], 1, 1) for i in range(2))
            rope(pe_k[:, :, 0:16], pe_k[:, :, 16:32], cos, sin, [x[:, 0:1, :] for x in (rope_a, rope_b, rope_c, rope_d)])
        dve.wait_ge(sem("od_kvup"), 1)
        for j in range(T):
            for half in range(2):
                kv = psum[4 + 2 * j + half].rearrange("p (h d) -> p h d", h=4)
                vlink(V.tensor_copy(k_cat[:, j, 4 * half:4 * half + 4, 0:NOPE], kv[:, :, 0:NOPE]))
                vlink(V.tensor_copy(v_mla[:, j, 4 * half:4 * half + 4, :], kv[:, :, NOPE:]))
            vlink(V.tensor_copy(k_cat[:, j, :, NOPE:], over(c_tok[:, j, Q_RANK + KV_RANK:], 1, MLA_H)))
        dve.wait_ge(sem("od_qcat"), 1)
        for j in range(T):
            cos, sin = (over(tab[:, j, 16 * i:16 * i + 16], 1, MLA_H) for i in range(2))
            rope(q_cat[:, j, :, NOPE:NOPE + 16], q_cat[:, j, :, NOPE + 16:], cos, sin, (rope_a, rope_b, rope_c, rope_d))
        vlink(V.memset(at_sums, 0.0), sem("od_cat_ready"))
        for n in range(8):
            dve.wait_ge(sem("od_cat_turned"), n + 1)
            dst = (mla_qT, mla_kT)[n // 4]
            vlink(V.tensor_copy(dst[0:MLA_K, 2 * (n % 4):2 * (n % 4) + 2, :],
                                psum[6 + n % 2][0:MLA_K, :].rearrange("p (h t) -> p h t", h=2)), sem("od_cat_read"))
        dve.wait_ge(sem("od_f_ln"), 1)
        vlink(V.scalar_tensor_tensor(out=log_f, in0=f_x, scalar=0.0, in1=f_e, op0=ALU.max, op1=ALU.add))
        vlink(V.tensor_scalar(log_f, log_f, -1.0, None, ALU.mult), sem("od_logf"))

        def head_writer(off, width):
            def write(u, bank, scale, done):
                vlink(V.tensor_tensor(odd_mix[:, :, off + u * width:off + (u + 1) * width],
                                      bank[:, 0:T * width].rearrange("p (j d) -> p j d", j=T),
                                      over(scale, 2, width), ALU.mult), done)
            return write
        attention_vector("mla", MLA_H, MLA_K ** -0.5, lambda u: mask_chunk, at_masked, at_nbias, at_sums,
                         head_writer(0, V_DIM))
        dve.wait_ge(sem("od_fsum"), 1)
        vlink(V.tensor_copy(fox_sum[0:FOX_H], psum[6][0:FOX_H, 0:S]))
        vlink(V.tensor_scalar(fox_neg[0:FOX_H], fox_sum[0:FOX_H], -1.0, None, ALU.mult), sem("od_fsum_read"))

        def fox_mask(u):
            dve.wait_ge(sem("fox_term"), u + 1)
            vlink(V.tensor_tensor(fox_bias[:, u % 2], psum[6 + u % 2][:, 0:3 * P].rearrange("p (i s) -> p i s", i=3),
                                  mask_causal, ALU.add), sem("fox_biased"))
            return fox_bias[:, u % 2]
        attention_vector("fox", FOX_H, 1.0, fox_mask, at_masked, at_nbias[:, 8:], at_sums[:, 8:],
                         head_writer(MLA_H * V_DIM, HD))
        vlink(V.memset(at_nbias[:, 0, :], 0.0), sem("mix_ready"))
        out_vector("od", odd_mixT, 2, ALPHA)
        dve.wait_ge(sem("norm_landed"), 96)
        layer_norm()
        dve.sem_inc(sem("phase_done"), 1)

    ca = carver()
    ca(3 * D)
    sg_mix = ca(T, SG_W)
    sg_v = ca(T, SG_W)
    sg_mixT = ca(4, 4, S)
    spatialT = ca(SG_G, P)
    sg_junk = ca(SG_W)

    def sg_tensor(pe):
        t = "sg"
        pe.wait_ge(sem("phase_done"), 4)
        pe.wait_ge(sem("normed"), 1)
        to_features_tensor(pe, t, normed)
        project_tensor(pe, t, sg_pieces)
        read_wait(pe, "sg", 0, 8)
        read_wait(pe, "sg", 1, 8)
        piece_wait(pe, sg_spatial)
        wsp = piece_ap(sg_spatial)
        for g in range(SG_G):
            last = nc.tensor.transpose(psum[6 + g // 4][:, (g % 4) * P:(g % 4 + 1) * P], wsp[:, g, :], ident)
        last.then_inc(sem("sg_w_turned"), 1)
        pe.wait_ge(sem("sg_w_ready"), 1)
        pe.wait_ge(sem("sg_v_ready"), 1)
        for n in range(8):
            j, g = n // 4, 2 * (n % 4)
            if n >= 4:
                pe.wait_ge(sem("sg_gated"), n - 3)
            for i in range(2):
                last = nc.tensor.matmul(psum[n % 4][:, i * SG_C:(i + 1) * SG_C], spatialT[:, g + i, :],
                                        sg_v[:, j, (g + i) * SG_C:(g + i + 1) * SG_C], start=True, stop=True)
            last.then_inc(sem("sg_mixed"), 1)
        out_tensor(pe, t, sg_mix, sg_mixT, sg_out)

    def sg_scalar(act):
        rsqrt_scalar(act, sq, T)
        for n in range(8):
            dst = sg_mix if n < 4 else sg_v
            for half in range(2):
                full_wait(act, "sg", half, n)
                nc.scalar.activation(dst[:, half, (n % 4) * 512:(n % 4 + 1) * 512], psum[2 * (n % 3) + half],
                                     ACT.Gelu_apprx_tanh).then_inc(sem(f"bank{half}_read"), 1)
        rsqrt_scalar(act, sq, T)

    def sg_vector(dve):
        normed_vector("sg")
        to_features_vector("sg", par["l0_mix_norm_2"])
        dve.wait_ge(sem("sg_w_turned"), 1)
        for i in range(2):
            vlink(V.tensor_tensor(spatialT[:, 4 * i:4 * i + 4, :], psum[6 + i].rearrange("p (g t) -> p g t", g=4),
                                  over(upto, 1, 4), ALU.mult), *([sem("sg_w_ready")] if i else []))
        read_wait(dve, "sg", 1, 8)
        rms_scale(sg_v, sg_junk, SG_W, rstd)
        dve.wait_ge(sem("norm_landed"), 160)
        for j in range(T):
            vlink(V.scalar_tensor_tensor(out=sg_v[:, j, :], in0=sg_v[:, j, :], scalar=rstd[:, j:j + 1], in1=norm_vec,
                                         op0=ALU.mult, op1=ALU.mult), *([sem("sg_v_ready")] if j else []))
        for n in range(8):
            j, g = n // 4, 2 * (n % 4)
            dve.wait_ge(sem("sg_mixed"), n + 1)
            for i in range(2):
                u = sg_mix[:, j, (g + i) * SG_C:(g + i + 1) * SG_C]
                vlink(V.scalar_tensor_tensor(out=u, in0=psum[n % 4][:, i * SG_C:(i + 1) * SG_C],
                                             scalar=par["b_spatial"][:, g + i:g + i + 1], in1=u, op0=ALU.add, op1=ALU.mult),
                      *([sem("sg_gated")] if i else []), *([sem("mix_ready")] if i and n == 7 else []))
        out_vector("sg", sg_mixT, 4, 1.0)
        dve.sem_inc(sem("phase_done"), 1)

    def dense_vector(dve):
        normed_vector("ff")
        to_features_vector("ff", par["l0_ffn_norm_2"])
        ff_vector(dve, "ff")
        dve.sem_inc(sem("phase_done"), 1)

    def moe_second_vector(dve):
        normed_vector("m2")
        to_features_vector("m2", par["l1_moe_norm_2"])
        route_vector(dve, "m2", None)
        ff_vector(dve, "m2")
        dve.sem_inc(sem("phase_done"), 1)

    ca = carver()
    ca(3 * D)
    MAPS = 2 * DA_H
    da_qk = ca(T, 2 * MAPS, HD)
    da_v = ca(T, D)
    da_qkT = ca(2 * DA_H, S)
    da_mix = ca(T, D)
    da_mixT = ca(2, 4, S)
    da_masked, da_probs, da_probsT = ca(2, 3, P), ca(2, 3, P), ca(2, 3, P)
    da_first = ca(T, P)
    da_tmps = [ca(2 * MAPS, 8) for _ in range(4)]
    da_sq = da_mixT.rearrange("p k c t -> p (k c t)").rearrange("p (m d) -> p m d", d=HD)
    da_ms = ca(T, 2 * MAPS)
    da_hs = ca(T, DA_H)
    da_ms_flat, da_hs_flat = da_ms.rearrange("p j m -> p (j m)"), da_hs.rearrange("p j h -> p (j h)")
    ang, turns, half_sin, cs_cos, cs_sin = (tiny(T, 8) for _ in range(5))
    posf = tiny(T)
    lam_tmp, lam_sum = ca(2, HD), tiny(2)
    neg_lam = tiny(1)

    def da_tensor(pe):
        t = "da"
        pe.wait_ge(sem("phase_done"), 6)
        pe.wait_ge(sem("normed"), 3)
        to_features_tensor(pe, t, normed)
        project_tensor(pe, t, da_pieces)
        pe.wait_ge(sem("da_rotated"), 1)
        for n in range(8):
            if n >= 2:
                pe.wait_ge(sem("da_qk_read"), n - 1)
            for i in range(4):
                c, j = 2 * n + i // 2, i % 2
                last = nc.tensor.transpose(psum[6 + n % 2][:, i * P:(i + 1) * P],
                                           da_qk[:, j, 2 * c:2 * c + 2, :].rearrange("p m d -> p (m d)"), ident)
            last.then_inc(sem("da_qk_turned"), 1)
        pe.wait_ge(sem("da_qk_read"), 8)
        read_wait(pe, "da", 0, 6)
        read_wait(pe, "da", 1, 6)

        def logits(u, bank):
            r = slice((u % 2) * 64, (u % 2) * 64 + 64)
            qq, kk = da_qkT[r, u // 2, :], da_qkT[r, DA_H + u // 2, :]
            nc.tensor.matmul(bank[:, 0:P], qq[:, 0:P], kk[:, 0:P], start=True, stop=True)
            return nc.tensor.matmul(bank[:, P:3 * P], qq[:, P:S], kk, start=True, stop=True)
        attention_tensor(pe, "dat", MAPS, logits, da_probs, da_probsT,
                         lambda u, s: da_v[:, s, (u // 2) * P:(u // 2 + 1) * P], P)
        out_tensor(pe, t, da_mix, da_mixT, da_out)

    def da_scalar(act):
        A = nc.scalar
        rsqrt_scalar(act, sq, T)
        for n in range(6):
            full_wait(act, "da", 0, n)
            dst = da_qk[:, 0].rearrange("p m d -> p (m d)")[:, n * 512:(n + 1) * 512] if n < 4 else \
                da_v[:, 0, (n - 4) * 512:(n - 3) * 512]
            A.copy(dst, psum[2 * (n % 3)]).then_inc(sem("bank0_read"), 1)
        act.wait_ge(sem("da_reduced"), 1)
        A.activation(cs_sin, ang, ACT.Sin)
        A.activation(half_sin, ang, ACT.Sin, scale=0.5).then_inc(sem("da_sines"), 1)
        act.wait_ge(sem("da_lam_sums"), 1)
        A.activation(lam_sum, lam_sum, ACT.Exp).then_inc(sem("da_lam_exp"), 1)
        rsqrt_scalar(act, da_ms_flat, T * 2 * MAPS)
        attention_scalar(act, "dat", MAPS, HD ** -0.5, da_masked, at_nbias, da_probs, at_sums, da_probsT)
        rsqrt_scalar(act, da_hs_flat, T * DA_H)

    def da_vector(dve):
        normed_vector("da")
        to_features_vector("da", par["l1_mix_norm_2"])
        two_pi = 2 * math.pi
        c1 = 6.28125
        c2 = float(np.float32(np.round((two_pi - c1) * 2 ** 22) / 2 ** 22))
        c3 = float(np.float32(two_pi - c1 - c2))
        magic = 12582912.0
        vlink(V.tensor_copy(posf, par["positions"]))
        vlink(V.tensor_tensor(ang, par["tables"][:, :, 32:40], over(posf, 2, 8), ALU.mult))
        vlink(V.tensor_scalar(turns, ang, 1.0 / two_pi, None, ALU.mult))
        vlink(V.tensor_scalar(turns, turns, magic, None, ALU.add))
        vlink(V.tensor_scalar(turns, turns, -magic, None, ALU.add))
        for c in (c1, c2, c3):
            vlink(V.scalar_tensor_tensor(out=ang, in0=turns, scalar=-c, in1=ang, op0=ALU.mult, op1=ALU.add))
        vlink(V.tensor_scalar(ang, ang, 3.1415925, -3.1415925, ALU.min, ALU.max), sem("da_reduced"))
        lam = par["lam"]
        for i in range(2):
            vlink(V.tensor_tensor_reduce(out=lam_tmp[:, i, :], in0=lam[:, 2 * i, :], in1=lam[:, 2 * i + 1, :], scale=1.0,
                                         scalar=0.0, op0=ALU.mult, op1=ALU.add, accum_out=lam_sum[:, i:i + 1]),
                  *([sem("da_lam_sums")] if i else []))
        for n in range(6):
            full_wait(dve, "da", 1, n)
            dst = da_qk[:, 1].rearrange("p m d -> p (m d)")[:, n * 512:(n + 1) * 512] if n < 4 else \
                da_v[:, 1, (n - 4) * 512:(n - 3) * 512]
            vlink(V.tensor_copy(dst, psum[2 * (n % 3) + 1]), sem("bank1_read"))
        read_wait(dve, "da", 0, 6)
        dve.wait_ge(sem("da_sines"), 1)
        vlink(V.tensor_tensor(cs_cos, half_sin, half_sin, ALU.mult))
        vlink(V.tensor_scalar(cs_cos, cs_cos, -2.0, 1.0, ALU.mult, ALU.add))
        dve.wait_ge(sem("da_lam_exp"), 1)
        vlink(V.tensor_tensor(neg_lam, lam_sum[:, 1:2], lam_sum[:, 0:1], ALU.subtract))
        vlink(V.tensor_scalar(neg_lam, neg_lam, -LAMBDA_INIT, None, ALU.add))
        for j in range(T):
            vlink(V.tensor_tensor(da_sq, da_qk[:, j], da_qk[:, j], ALU.mult))
            vlink(V.tensor_reduce(out=da_ms[:, j, :], in_=da_sq, axis=AX, op=ALU.add))
        vlink(V.tensor_scalar(da_ms, da_ms, 1.0 / HD, RMS_EPS, ALU.mult, ALU.add))
        rsqrt_vector(da_ms_flat, da_ms_flat, T * 2 * MAPS)
        for j in range(T):
            vlink(V.tensor_tensor(da_qk[:, j], da_qk[:, j], over(da_ms[:, j, :], 2, HD), ALU.mult))
            for i, gain in enumerate(("da_q_norm", "da_k_norm")):
                part = da_qk[:, j, i * MAPS:(i + 1) * MAPS, :]
                vlink(V.tensor_tensor(part, part, over(par[gain], 1, MAPS), ALU.mult))
            cos, sin = (over(x[:, j, :], 1, 2 * MAPS) for x in (cs_cos, cs_sin))
            rope(da_qk[:, j, :, 0:8], da_qk[:, j, :, 8:16], cos, sin, da_tmps)
        vlink(V.memset(at_sums, 0.0), sem("da_rotated"))
        for n in range(8):
            dve.wait_ge(sem("da_qk_turned"), n + 1)
            vlink(V.tensor_copy(da_qkT[:, 2 * n:2 * n + 2, :], psum[6 + n % 2].rearrange("p (c t) -> p c t", c=2)),
                  sem("da_qk_read"))

        def write(u, bank, scale, done):
            src = bank[:, 0:T * P].rearrange("p (j d) -> p j d", j=T)
            if u % 2 == 0:
                vlink(V.tensor_tensor(da_first, src, over(scale, 2, P), ALU.mult), done)
            else:
                dst = da_mix[:, :, (u // 2) * P:(u // 2 + 1) * P]
                vlink(V.tensor_tensor(dst, src, over(scale, 2, P), ALU.mult), done)
                vlink(V.scalar_tensor_tensor(out=dst, in0=dst, scalar=neg_lam, in1=da_first, op0=ALU.mult, op1=ALU.add))
        attention_vector("dat", MAPS, HD ** -0.5, lambda u: mask_causal, da_masked, at_nbias, at_sums, write)
        for j in range(T):
            y = da_mix[:, j, :].rearrange("p (h d) -> p h d", d=P)
            sqv = da_qk[:, 0].rearrange("p m d -> p (m d)")[:, 0:D].rearrange("p (h d) -> p h d", d=P)
            vlink(V.tensor_tensor(sqv, y, y, ALU.mult))
            vlink(V.tensor_reduce(out=da_hs[:, j, :], in_=sqv, axis=AX, op=ALU.add))
        vlink(V.tensor_scalar(da_hs, da_hs, 1.0 / P, RMS_EPS, ALU.mult, ALU.add))
        rsqrt_vector(da_hs_flat, da_hs_flat, T * DA_H)
        vlink(V.tensor_scalar(da_hs, da_hs, 1.0 - LAMBDA_INIT, None, ALU.mult))
        for j in range(T):
            y = da_mix[:, j, :].rearrange("p (h d) -> p h d", d=P)
            vlink(V.tensor_tensor(y, y, over(da_hs[:, j, :], 2, P), ALU.mult))
            vlink(V.tensor_tensor(y, y, over(par["subln"], 1, DA_H), ALU.mult), *([sem("mix_ready")] if j else []))
        out_vector("da", da_mixT, 2, 1.0)
        dve.sem_inc(sem("phase_done"), 1)

    block = nc.Block()
    with block as block:
        @block.sync
        def _(sp):
            sp.dma_start(h, w["x"][0].rearrange("(j p) d -> p j d", p=P)).then_inc(sem("x_landed"), 16)

            def load_pieces(a, b):
                for n in range(a, b):
                    if n >= PSLOTS:
                        name, count = released[n - PSLOTS]
                        sp.wait_ge(sem(name), count)
                    sp.dma_start(piece_ap(n), piece_list[n][0]).then_inc(sem(f"piece_landed{n % PSLOTS}"), 16)
            load_pieces(0, EVEN_END)
            ff_sync(sp, "m0", w["moe_w_gate"][0], w["moe_w_up"][0], w["moe_w_down"][0])
            load_pieces(EVEN_END, ODD_END)
            ff_sync(sp, "m1", w["moe_w_gate"][1], w["moe_w_up"][1], w["moe_w_down"][1])
            load_pieces(ODD_END, SG_END)
            ff_sync(sp, "ff", w["l0_ffn_w_gate_2"], w["l0_ffn_w_up_2"], w["l0_ffn_w_down_2"])
            load_pieces(SG_END, DA_END)
            ff_sync(sp, "m2", w["l1_moe_w_gate_2"], w["l1_moe_w_up_2"], w["l1_moe_w_down_2"])
            sp.wait_ge(sem("phase_done"), 8)
            sp.dma_start(out[0].rearrange("(j p) d -> p j d", p=P), h).then_inc(sem("out_written"), 16)
            sp.wait_ge(sem("out_written"), 16)

        @block.gpsimd
        def _(pool):
            setup_gpsimd(pool)
            phases_gpsimd(pool)

        @block.tensor
        def _(pe):
            credits_tensor(pe)
            even_tensor(pe)
            moe_tensor(pe, "m0", 1, par["route_w0"])
            odd_tensor(pe)
            moe_tensor(pe, "m1", 3, par["route_w1"])
            sg_tensor(pe)
            dense_tensor(pe)
            da_tensor(pe)
            moe_tensor(pe, "m2", 7, par["route_w2"])

        @block.scalar
        def _(act):
            even_scalar(act)
            ff_scalar(act, "m0")
            odd_scalar(act)
            ff_scalar(act, "m1")
            sg_scalar(act)
            ff_scalar(act, "ff")
            da_scalar(act)
            ff_scalar(act, "m2")

        @block.vector
        def _(dve):
            for i in range(8):
                vlink(V.memset(rank[:, i:i + 1], float(8 - i)))
            dve.wait_ge(sem("const_ready"), 1)
            dve.wait_ge(sem("index_ready"), 1)
            even_vector(dve)
            moe_first_vector(dve, "m0", 0)
            odd_vector(dve)
            moe_first_vector(dve, "m1", 1)
            sg_vector(dve)
            dense_vector(dve)
            da_vector(dve)
            moe_second_vector(dve)


INPUTS = [
    "x", "ev_w_in", "ev_conv_w", "ev_conv_b", "ev_dt_bias", "ev_a_log", "ev_d_skip", "ev_norm_g", "ev_w_out",
    "od_w_in", "od_q_norm_g", "od_w_q_up", "od_kv_norm_g", "od_w_kv_up", "od_f_bias", "od_w_out", "ln1_g",
    "ln1_b", "ln2_g", "ln2_b", "moe_w_group", "moe_b_group", "moe_w_expert", "moe_b_expert", "moe_w_gate",
    "moe_w_up", "moe_w_down", "positions_2", "l0_mix_norm_2", "l0_sg_w_in_2", "l0_sg_v_norm_2",
    "l0_sg_w_spatial_2", "l0_sg_b_spatial_2", "l0_sg_w_out_2", "l0_ffn_norm_2", "l0_ffn_w_gate_2",
    "l0_ffn_w_up_2", "l0_ffn_w_down_2", "l1_mix_norm_2", "l1_da_w_qkv_2", "l1_da_q_norm_2",
    "l1_da_k_norm_2", "l1_da_lambda_q1_2", "l1_da_lambda_k1_2", "l1_da_lambda_q2_2", "l1_da_lambda_k2_2",
    "l1_da_subln_2", "l1_da_w_out_2", "l1_moe_norm_2", "l1_moe_w_router_2", "l1_moe_w_gate_2",
    "l1_moe_w_up_2", "l1_moe_w_down_2",
]


def kernel(**inputs):
    import numpy as _np
    import concourse.bacc as _bacc
    from concourse import mybir as _mybir
    from concourse.bass_utils import run_bass_kernel_spmd as _run

    nc = _bacc.Bacc("TRN2", target_bir_lowering=False, num_devices=1)
    arrays, w = {}, {}
    for name in INPUTS:
        a = _np.ascontiguousarray(inputs[name])
        arrays[f"in_{name}"] = a
        w[name] = nc.dram_tensor(f"in_{name}", a.shape, _mybir.dt.from_np(a.dtype), kind="ExternalInput").ap()
    tables = shape_tables()
    arrays["in_tables"] = tables
    w["tables"] = nc.dram_tensor("in_tables", tables.shape, _mybir.dt.float32, kind="ExternalInput").ap()
    out = nc.dram_tensor("out", (1, S, D), _mybir.dt.float32, kind="ExternalOutput").ap()
    build(nc, w, out)
    r = _run(nc, [arrays], core_ids=[0])
    return r.results[0]["out"]
```

```python
import math

import numpy as np

import concourse.bass as bass
from concourse import mybir

F32 = mybir.dt.float32
F32R = mybir.dt.float32r
I32 = mybir.dt.int32
ALU = mybir.AluOpType
ACT = mybir.ActivationFunctionType
AX = mybir.AxisListType.X

P = 128
D = 1024
S = 256
T = S // P
DC = D // P
SSD_H, SSD_P, SSD_G, SSD_N = 16, 64, 2, 128
SSD_INNER = SSD_H * SSD_P
CONV_K = 4
CONV_DIM = SSD_INNER + 2 * SSD_G * SSD_N
CONV_C = CONV_DIM // P
SB_H = 8
HD = 64
SB_W = SB_H * HD
Q_RANK, KV_RANK, NOPE, ROPE, V_DIM = 256, 128, 64, 32, 64
MLA_H = 8
MLA_K = NOPE + ROPE
FOX_H = 8
FOX_W = FOX_H * HD
SG_W = 2 * D
SG_G = 8
SG_C = SG_W // SG_G
DA_H = 8
ROT = 16
BLK = 256
MOE_E, MOE_GRP = 16, 4
MOE2_E, MOE2_FF = 8, 3584
DENSE_FF = 2816
ALPHA = 4.0 ** 0.25
LN_EPS, RMS_EPS = 1e-5, 1e-6
LAMBDA_INIT = 0.8 - 0.6 * math.exp(-0.3)
NEG = -1.0e30
PW = 4096
PSLOTS = 2
ROPE_THETA, ROPE_THETA_2 = 10000.0, 500000.0


def shape_tables():
    inv = (np.float32(ROPE_THETA) ** (-(np.arange(0, ROPE, 2, dtype=np.float32) / np.float32(ROPE)))).astype(np.float32)
    ang = (np.arange(S, dtype=np.float32)[:, None] * inv[None, :]).astype(np.float32)
    inv2 = (np.float32(1.0) / (np.float32(ROPE_THETA_2) ** (np.arange(0, ROT, 2, dtype=np.float32) / np.float32(ROT)))).astype(np.float32)
    return np.concatenate([np.cos(ang), np.sin(ang), np.tile(inv2[None, :], (S, 1))], axis=1).astype(np.float32)


def build(nc, w, out):
    sems = {}

    def sem(name):
        if name not in sems:
            sems[name] = nc.alloc_semaphore(name)
        return sems[name]

    def sb(name, shape, dt=F32):
        return nc.alloc_sbuf_tensor(name, shape, dt).ap()

    h = sb("h", [P, T, D])
    xT = sb("xT", [P, DC, S])
    xt_at = nc.sbuf_base - 4 * DC * S
    ffw_gu = sb("ffw_gu", [P, 2, DC, 2 * BLK])
    ffw_d = sb("ffw_d", [P, 2, BLK // P, D])
    pieces = sb("pieces", [P, PSLOTS, PW])
    norm_vec = sb("norm_vec", [P, 2 * D])
    row_index = sb("row_index", [P, P])
    ident = sb("ident", [P, P])
    ones = sb("ones", [P, P])
    upto = sb("upto", [P, P])
    above = sb("above", [P, P])
    atleast = sb("atleast", [P, P])
    mask_causal = sb("mask_causal", [P, 3, P])
    mask_strict = sb("mask_strict", [P, 3, P])
    keep_strict = sb("keep_strict", [P, 3, P])
    ARENA = 22312
    SMALL = 896
    arena = sb("arena", [P, ARENA])
    arena_at = nc.sbuf_base - 4 * ARENA
    small = sb("small", [P, SMALL])

    psum = [nc.alloc_psum_tensor(f"bank{i}", [P, 512], F32).ap() for i in range(8)]

    par = {}
    par_loads = []

    def param(name, shape, src, dt=F32):
        par[name] = sb("par_" + name, shape, dt)
        par_loads.append((par[name], src))

    def bcast(v):
        return v.partition_broadcast(P)

    param("conv_w", [P, CONV_K, CONV_C], w["ev_conv_w"][0].rearrange("k (c p) -> p k c", p=P))
    param("conv_b", [P, CONV_C], w["ev_conv_b"][0].rearrange("(c p) -> p c", p=P))
    param("dt_bias", [P, SSD_H], bcast(w["ev_dt_bias"][0]))
    param("a_log", [P, SSD_H], bcast(w["ev_a_log"][0]))
    param("d_skip", [P, SSD_H], bcast(w["ev_d_skip"][0]))
    param("ssd_norm", [P, 2, 4], w["ev_norm_g"][0].rearrange("(k p c) -> p k c", k=2, c=4))
    param("q_norm", [P, 2], w["od_q_norm_g"][0].rearrange("(c p) -> p c", p=P))
    param("kv_norm", [P, 1], w["od_kv_norm_g"][0].rearrange("(c p) -> p c", p=P))
    param("f_bias", [P, FOX_H], bcast(w["od_f_bias"][0]))
    for i in range(2):
        param(f"route_b{i}", [P, 20], None)
        par_loads.pop()
        par_loads.append((par[f"route_b{i}"][:, 0:4], bcast(w["moe_b_group"][i])))
        par_loads.append((par[f"route_b{i}"][:, 4:20], bcast(w["moe_b_expert"][i])))
        param(f"route_w{i}", [P, DC, 20], None)
        par_loads.pop()
        par_loads.append((par[f"route_w{i}"][:, :, 0:4], w["moe_w_group"][i].rearrange("(p c) n -> p c n", c=DC)))
        par_loads.append((par[f"route_w{i}"][:, :, 4:20], w["moe_w_expert"][i].rearrange("(p c) n -> p c n", c=DC)))
    param("route_w2", [P, DC, MOE2_E], w["l1_moe_w_router_2"].rearrange("(p c) n -> p c n", c=DC))
    for name in ("l0_mix_norm_2", "l0_ffn_norm_2", "l1_mix_norm_2"):
        param(name, [P, DC], w[name].rearrange("(p c) -> p c", c=DC))
    param("b_spatial", [P, SG_G], w["l0_sg_b_spatial_2"].rearrange("g t -> t g"))
    param("da_q_norm", [P, HD], bcast(w["l1_da_q_norm_2"]))
    param("da_k_norm", [P, HD], bcast(w["l1_da_k_norm_2"]))
    param("lam", [P, 4, HD], None)
    par_loads.pop()
    for i, name in enumerate(("q1", "k1", "q2", "k2")):
        par_loads.append((par["lam"][:, i, :], bcast(w[f"l1_da_lambda_{name}_2"])))
    param("subln", [P, P], bcast(w["l1_da_subln_2"]))
    param("tables", [P, T, 40], w["tables"].rearrange("(j p) n -> p j n", p=P))
    param("positions", [P, T], w["positions_2"].rearrange("a (j p) -> p (a j)", p=P), I32)

    piece_list = []

    def piece(src, shape):
        piece_list.append((src, shape))
        return len(piece_list) - 1

    def piece_ap(n):
        shape = piece_list[n][1]
        size = int(np.prod(shape[1:]))
        flat = pieces[:, n % PSLOTS, 0:size]
        if len(shape) == 2:
            return flat
        return flat.rearrange("p (a b) -> p a b", a=shape[1])

    def columns(mat, c0, c1):
        return piece(mat[:, c0:c1].rearrange("(p c) n -> p c n", c=DC), [P, DC, c1 - c0])

    def rows(mat, k):
        return piece(mat[512 * k:512 * (k + 1), :].rearrange("(p c) n -> p c n", c=4), [P, 4, D])

    ev = w["ev_w_in"][0]
    o = SSD_INNER
    even_pieces = [("z", "tok", columns(ev, 0, 512), 512), ("z", "tok", columns(ev, 512, 1024), 512)]
    even_pieces += [("xbc", "feat", columns(ev, o + 512 * i, o + 512 * (i + 1)), 512) for i in range(3)]
    o += CONV_DIM
    even_pieces += [("dt", "tok", columns(ev, o, o + SSD_H), SSD_H)]
    o += SSD_H
    even_pieces += [("q", "feat", columns(ev, o, o + 512), 512), ("k", "feat", columns(ev, o + 512, o + 1024), 512),
                    ("v", "tok", columns(ev, o + 1024, o + 1536), 512)]
    even_out = [rows(w["ev_w_out"][0], k) for k in range(3)]
    EVEN_END = len(piece_list)
    od = w["od_w_in"][0]
    o = Q_RANK + KV_RANK + ROPE
    odd_pieces = [("c", "tok", columns(od, 0, o), o), ("q", "feat", columns(od, o, o + 512), 512),
                  ("k", "feat", columns(od, o + 512, o + 1024), 512),
                  ("v", "tok", columns(od, o + 1024, o + 1536), 512),
                  ("f", "tok", columns(od, o + 1536, o + 1536 + FOX_H), FOX_H)]
    odd_qup = piece(w["od_w_q_up"][0].rearrange("(c p) n -> p c n", p=P), [P, 2, MLA_H * MLA_K])
    odd_kvup = piece(w["od_w_kv_up"][0], [P, MLA_H * (NOPE + V_DIM)])
    odd_out = [rows(w["od_w_out"][0], k) for k in range(2)]
    ODD_END = len(piece_list)
    sg_in = w["l0_sg_w_in_2"]
    sg_pieces = [("z", "tok", columns(sg_in, 512 * i, 512 * (i + 1)), 512) for i in range(8)]
    sg_spatial = piece(w["l0_sg_w_spatial_2"].rearrange("g t s -> t g s"), [P, SG_G, P])
    sg_out = [rows(w["l0_sg_w_out_2"], k) for k in range(4)]
    SG_END = len(piece_list)
    qkv = w["l1_da_w_qkv_2"]
    da_pieces = [("qkv", "tok", columns(qkv, 512 * i, 512 * (i + 1)), 512) for i in range(6)]
    da_out = [rows(w["l1_da_w_out_2"], k) for k in range(2)]
    DA_END = len(piece_list)

    FIRST_P, FIRST_O, PHASE, MIXER = {}, {}, {}, {}
    at_p = at_o = 0
    for k, (t, plan, outs) in enumerate((("ev", even_pieces, even_out), ("od", odd_pieces, odd_out),
                                         ("sg", sg_pieces, sg_out), ("da", da_pieces, da_out))):
        FIRST_P[t], FIRST_O[t], MIXER[t] = at_p, at_o, k
        at_p, at_o = at_p + len(plan), at_o + len(outs)
    for k, t in enumerate(("ev", "m0", "od", "m1", "sg", "ff", "da", "m2")):
        PHASE[t] = k
    FIRST_U = {"mla": 0, "fox": MLA_H, "dat": MLA_H + FOX_H}
    ROUTER = {"m0": 0, "m1": 1, "m2": 2}

    def full_wait(eng, t, half, n):
        eng.wait_ge(sem(f"bank{half}_full"), FIRST_P[t] + n + 1)

    def read_wait(eng, t, half, n):
        eng.wait_ge(sem(f"bank{half}_read"), FIRST_P[t] + n)

    released = {}
    for t, plan, outs in (("ev", even_pieces, even_out), ("od", odd_pieces, odd_out), ("sg", sg_pieces, sg_out),
                          ("da", da_pieces, da_out)):
        for k, (_, _, n, _) in enumerate(plan):
            released[n] = ("bank1_full", FIRST_P[t] + k + 1)
        for k, n in enumerate(outs):
            released[n] = ("out_piece", FIRST_O[t] + k + 1)
    released[odd_qup], released[odd_kvup] = ("od_qup", 1), ("od_kvup", 1)
    released[sg_spatial] = ("sg_w_turned", 1)

    def piece_wait(eng, n):
        eng.wait_ge(sem(f"piece_landed{n % PSLOTS}"), 16 * (n // PSLOTS + 1))

    counts = {"dve": 0, "act": 0}

    def vlink(ins, *also):
        counts["dve"] += 1
        ins.then_inc(sem("vector_step"), 1)
        nc.vector.wait_ge(sem("vector_step"), counts["dve"])
        for s in also:
            nc.vector.sem_inc(s, 1)

    V = nc.vector

    arena_used = []

    def minus_abs(dst, x):
        return V.scalar_tensor_tensor(out=dst, in0=x, scalar=-1.0, in1=x, op0=ALU.mult, op1=ALU.min)

    def carver():
        used = [0]

        def carve(*shape):
            size = int(np.prod(shape))
            at = used[0]
            used[0] += size
            assert used[0] <= ARENA, used[0]
            arena_used.append(used[0])
            flat = arena[:, at:at + size]
            if len(shape) == 1:
                return flat
            names = "abcd"[:len(shape)]
            return flat.rearrange(f"p ({' '.join(names)}) -> p {' '.join(names)}",
                                  **{n: s for n, s in zip(names, shape)})
        return carve

    def parts_at(name, at, *shape):
        return nc.alloc_sbuf_tensor_at(name, [P] + list(shape), F32R, offset=at).ap()

    small_at = [0]

    def tiny(*shape):
        size = int(np.prod(shape))
        at = small_at[0]
        small_at[0] += size
        assert small_at[0] <= SMALL, small_at[0]
        flat = small[:, at:at + size]
        if len(shape) == 1:
            return flat
        names = "abcd"[:len(shape)]
        return flat.rearrange(f"p ({' '.join(names)}) -> p {' '.join(names)}",
                              **{n: s for n, s in zip(names, shape)})

    def over(ap, axis, n):
        a = ap.unsqueeze(axis)
        shape = list(a.shape)
        shape[axis] = n
        return a.to_broadcast(shape)

    stats, moments = tiny(T, 2, 6), tiny(T, 2)
    sq, rstd = tiny(T), tiny(T)
    root_y, root_t = tiny(T * 2 * 16), tiny(T * 2 * 16)
    roots = {"asked": 0, "answered": 0}

    def rsqrt_scalar(act, x, n):
        roots["answered"] += 1
        act.wait_ge(sem("root_asked"), roots["answered"])
        nc.scalar.activation(root_y[:, 0:n], x, ACT.Ln).then_inc(sem("root_ln"), 1)
        act.wait_ge(sem("root_ln"), roots["answered"])
        nc.scalar.activation(root_y[:, 0:n], root_y[:, 0:n], ACT.Exp, scale=-0.5).then_inc(sem("root_found"), 1)

    def rsqrt_vector(x, dst, n):
        roots["asked"] += 1
        V.sem_inc(sem("root_asked"), 1)
        V.wait_ge(sem("root_found"), roots["asked"])
        y, u = root_y[:, 0:n], root_t[:, 0:n]
        vlink(V.tensor_tensor(u, y, y, ALU.mult))
        vlink(V.tensor_tensor(u, u, x, ALU.mult))
        vlink(V.tensor_scalar(u, u, -0.5, 1.5, ALU.mult, ALU.add))
        vlink(V.tensor_tensor(dst, u, y, ALU.mult))

    def layer_norm():
        for j in range(T):
            for k in range(2):
                vlink(V.bn_stats(out=stats[:, j, k, :], in_=h[:, j, 512 * k:512 * (k + 1)]))
            vlink(V.bn_aggr(out=moments[:, j, :], in_=stats[:, j]))
        vlink(V.tensor_scalar(sq, moments[:, :, 1], LN_EPS, None, ALU.add))
        rsqrt_vector(sq, rstd, T)
        for j in range(T):
            vlink(V.tensor_scalar(h[:, j, :], h[:, j, :], moments[:, j, 0:1], rstd[:, j:j + 1], ALU.subtract, ALU.mult))
            vlink(V.tensor_tensor(h[:, j, :], h[:, j, :], norm_vec[:, 0:D], ALU.mult))
            vlink(V.tensor_tensor(h[:, j, :], h[:, j, :], norm_vec[:, D:2 * D], ALU.add))

    def rms_scale(src, junk, n, scale_out):
        for j in range(T):
            vlink(V.tensor_tensor_reduce(out=junk, in0=src[:, j, :], in1=src[:, j, :], scale=1.0, scalar=0.0,
                                         op0=ALU.mult, op1=ALU.add, accum_out=sq[:, j:j + 1]))
        vlink(V.tensor_scalar(sq, sq, 1.0 / n, RMS_EPS, ALU.mult, ALU.add))
        rsqrt_vector(sq, scale_out, T)

    def to_features_tensor(pe, t, src):
        for c in range(DC):
            for j in range(T):
                bank = psum[c // 2]
                last = nc.tensor.transpose(bank[:, (c % 2) * S + j * P:(c % 2) * S + (j + 1) * P],
                                           src[:, j, :].rearrange("t (p c) -> t c p", c=DC)[:, c, :], ident)
            if c % 2:
                last.then_inc(sem("xt_turned"), 1)

    def to_features_vector(t, gain=None):
        for b in range(DC // 2):
            V.wait_ge(sem("xt_turned"), DC // 2 * PHASE[t] + b + 1)
            src = psum[b].rearrange("p (c t) -> p c t", c=2)
            if gain is None:
                ins = V.tensor_copy(xT[:, 2 * b:2 * b + 2, :], src)
            else:
                ins = V.tensor_tensor(xT[:, 2 * b:2 * b + 2, :], src, over(gain[:, 2 * b:2 * b + 2], 2, S), ALU.mult)
            vlink(ins, *([sem("xt_ready")] if b == DC // 2 - 1 else []))

    def project_tensor(pe, t, plan):
        pe.wait_ge(sem("xt_ready"), PHASE[t] + 1)
        for n, (_, kind, g, cols) in enumerate(plan):
            piece_wait(pe, g)
            if n >= 3:
                read_wait(pe, t, 0, n - 2)
                read_wait(pe, t, 1, n - 2)
            wt = piece_ap(g)
            for half in range(2):
                bank = psum[2 * (n % 3) + half]
                if kind == "tok":
                    for c in range(DC):
                        last = nc.tensor.matmul(bank[:, 0:cols], xT[:, c, half * P:(half + 1) * P], wt[:, c, :],
                                                start=(c == 0), stop=(c == DC - 1))
                else:
                    for m in range(2):
                        m0 = (2 * half + m) * P
                        for c in range(DC):
                            last = nc.tensor.matmul(bank[:, m * S:(m + 1) * S], wt[:, c, m0:m0 + P], xT[:, c, :],
                                                    start=(c == 0), stop=(c == DC - 1))
                last.then_inc(sem(f"bank{half}_full"), 1)

    def out_tensor(pe, t, mix, mixT, plan):
        pe.wait_ge(sem("mix_ready"), MIXER[t] + 1)
        g = 0
        for k in range(len(plan)):
            for c in range(4):
                for j in range(T):
                    b = 4 + g // 4 % 2
                    if g % 4 == 0 and g >= 8:
                        pe.wait_ge(sem("mixt_read"), 2 * FIRST_O[t] + g // 4 - 1)
                    last = nc.tensor.transpose(psum[b][:, (g % 4) * P:(g % 4 + 1) * P],
                                               mix[:, j, 512 * k:512 * (k + 1)].rearrange("t (p c) -> t c p", c=4)[:, c, :],
                                               ident)
                    g += 1
                    if g % 4 == 0:
                        last.then_inc(sem("mixt_turned"), 1)
        for k, n in enumerate(plan):
            piece_wait(pe, n)
            pe.wait_ge(sem("mixt_read"), 2 * FIRST_O[t] + 2 * k + 2)
            wt = piece_ap(n)
            for j in range(T):
                for half in range(2):
                    for c in range(4):
                        last = nc.tensor.matmul(psum[2 * j + half], mixT[:, k, c, j * P:(j + 1) * P],
                                                wt[:, c, half * 512:(half + 1) * 512],
                                                start=(k == 0 and c == 0), stop=(k == len(plan) - 1 and c == 3))
            last.then_inc(sem("out_piece"), 1)

    def out_vector(t, mixT, n_pieces, scale, gain=None):
        for g in range(2 * n_pieces):
            V.wait_ge(sem("mixt_turned"), 2 * FIRST_O[t] + g + 1)
            k, c0 = g // 2, 2 * (g % 2)
            src = psum[4 + g % 2].rearrange("p (c t) -> p c t", c=2)
            dst = mixT[:, k, c0:c0 + 2, :]
            if gain is not None and k < gain.shape[1]:
                ins = V.tensor_tensor(dst, src, over(gain[:, k, c0:c0 + 2], 2, S), ALU.mult)
            else:
                ins = V.tensor_copy(dst, src)
            ins.then_inc(sem("mixt_read"), 1)
        V.wait_ge(sem("out_piece"), FIRST_O[t] + n_pieces)
        for j in range(T):
            for half in range(2):
                hv = h[:, j, half * 512:(half + 1) * 512]
                vlink(V.scalar_tensor_tensor(out=hv, in0=hv, scalar=scale, in1=psum[2 * j + half],
                                             op0=ALU.mult, op1=ALU.add))

    TRI = [(0, 0), (1, 0), (1, 1)]

    def attention_tensor(pe, t, units, logits, probs, probsT, value, dv):
        U0 = FIRST_U[t]
        for u in range(units + 2):
            if u < units:
                if u >= 2:
                    pe.wait_ge(sem("at_masked"), U0 + u - 1)
                logits(u, psum[u % 2]).then_inc(sem("at_logits"), 1)
            if 1 <= u <= units:
                v = u - 1
                pe.wait_ge(sem("at_probs"), U0 + v + 1)
                if v >= 2:
                    pe.wait_ge(sem("at_probst"), U0 + v - 1)
                for i in range(3):
                    last = nc.tensor.transpose(psum[2 + v % 2][:, i * P:(i + 1) * P], probs[:, v % 2, i, :], ident)
                last.then_inc(sem("at_turned"), 1)
            if u >= 2:
                v = u - 2
                pe.wait_ge(sem("at_probst"), U0 + v + 1)
                if v >= 2:
                    pe.wait_ge(sem("at_written"), U0 + v - 1)
                for i, (j, s) in enumerate(TRI):
                    last = nc.tensor.matmul(psum[4 + v % 2][:, j * dv:(j + 1) * dv], probsT[:, v % 2, i, :], value(v, s),
                                            start=(s == 0), stop=(s == j))
                last.then_inc(sem("at_outputs"), 1)

    def attention_scalar(act, t, units, scale, masked, nbias, probs, sums, probsT):
        U0 = FIRST_U[t]
        for u in range(units + 1):
            if u < units:
                act.wait_ge(sem("at_masked"), U0 + u + 1)
                if u >= 2:
                    act.wait_ge(sem("at_turned"), U0 + u - 1)
                for j, (a, b) in enumerate(((0, 1), (1, 3))):
                    ins = nc.scalar.activation(probs[:, u % 2, a:b, :], masked[:, u % 2, a:b, :], ACT.Exp,
                                               bias=nbias[:, u, j:j + 1], scale=scale, accum_out=sums[:, u, j:j + 1])
                ins.then_inc(sem("at_probs"), 1)
            if u >= 1:
                v = u - 1
                act.wait_ge(sem("at_turned"), U0 + v + 1)
                if v >= 2:
                    act.wait_ge(sem("at_outputs"), U0 + v - 1)
                nc.scalar.copy(probsT[:, v % 2, :, :], psum[2 + v % 2][:, 0:3 * P].rearrange("p (i t) -> p i t", i=3))\
                    .then_inc(sem("at_probst"), 1)

    def attention_vector(t, units, scale, mask_of, masked, nbias, sums, write):
        U0 = FIRST_U[t]
        for u in range(units + 1):
            if u < units:
                V.wait_ge(sem("at_logits"), U0 + u + 1)
                if u >= 2:
                    V.wait_ge(sem("at_probs"), U0 + u - 1)
                z = psum[u % 2][:, 0:3 * P].rearrange("p (i s) -> p i s", i=3)
                mask = mask_of(u)
                for j, (a, b) in enumerate(((0, 1), (1, 3))):
                    vlink(V.tensor_tensor_reduce(out=masked[:, u % 2, a:b, :], in0=z[:, a:b, :], in1=mask[:, a:b, :],
                                                 scale=1.0, scalar=-3.0e38, op0=ALU.add, op1=ALU.max,
                                                 accum_out=nbias[:, u, j:j + 1]))
                vlink(V.tensor_scalar(nbias[:, u, :], nbias[:, u, :], -scale, None, ALU.mult), sem("at_masked"))
            if u >= 1:
                v = u - 1
                V.wait_ge(sem("at_outputs"), U0 + v + 1)
                vlink(V.reciprocal(sums[:, v, :], sums[:, v, :]))
                write(v, psum[4 + v % 2], sums[:, v, :], sem("at_written"))

    def setup_gpsimd(pool):
        for ap, src in par_loads:
            pool.dma_start(ap, src, allow_slow_non_contiguous=True).then_inc(sem("params_landed"), 16)
        g = nc.gpsimd
        for m, v in ((ident, 0.0), (ones, 1.0), (upto, 1.0), (above, 1.0), (atleast, 1.0), (mask_causal, 0.0),
                     (mask_strict, 0.0), (keep_strict, 1.0)):
            last = g.memset(m, v)
        last.then_inc(sem("const_filled"), 1)
        pool.wait_ge(sem("const_filled"), 1)

        g.iota(row_index, [[1, P]], base=0, channel_multiplier=0, allow_small_or_imprecise_dtypes=True)\
            .then_inc(sem("index_ready"), 1)

        def select(m, op, fill, cm, step, base=0):
            return g.affine_select(out=m, in_=m, compare_op=op, fill=fill, base=base, pattern=[[step, P]],
                                   channel_multiplier=cm)
        select(ident, ALU.not_equal, 1.0, 1, -1)
        select(upto, ALU.is_ge, 0.0, -1, 1)
        select(above, ALU.is_gt, 0.0, 1, -1)
        select(atleast, ALU.is_ge, 0.0, 1, -1)
        for i in (0, 2):
            select(mask_causal[:, i, :], ALU.is_ge, NEG, 1, -1)
            select(mask_strict[:, i, :], ALU.is_gt, NEG, -1, 1)
            last = select(keep_strict[:, i, :], ALU.is_gt, 0.0, -1, 1)
        last.then_inc(sem("const_ready"), 1)

    def zeros_gpsimd(pool):
        nc.gpsimd.memset(zeros.bitcast(F32), 0.0).then_inc(sem("zeros_ready"), 1)

    def phases_gpsimd(pool):
        plan = [(0, w["ln1_g"][0], w["ln1_b"][0], None), (1, w["ln2_g"][0], w["ln2_b"][0], "m0"),
                (2, w["ln1_g"][1], w["ln1_b"][1], None), (3, w["ln2_g"][1], w["ln2_b"][1], "m1"),
                (4, w["l0_sg_v_norm_2"][0:D], w["l0_sg_v_norm_2"][D:2 * D], None),
                (5, w["l1_moe_norm_2"], None, "ff"), (7, None, None, "m2")]
        for phase, a, b, t in plan:
            if phase:
                pool.wait_ge(sem("phase_done"), phase)
            if a is not None:
                pool.dma_start(norm_vec[:, 0:D], bcast(a)).then_inc(sem("norm_landed"), 16)
            if b is not None:
                pool.dma_start(norm_vec[:, D:2 * D], bcast(b)).then_inc(sem("norm_landed"), 16)
            if t is not None:
                zeros_gpsimd(pool)

    ca = carver()
    zs = ca(T, SSD_INNER)
    xp_flat = ca(CONV_C * (S + CONV_K - 1))
    xp = xp_flat.rearrange("p (c t) -> p c t", c=CONV_C)
    xc = ca(CONV_C, S)
    sbq, sbk, sbv = ca(4, S), ca(4, S), ca(T, SB_W)
    xs_tok, xdt = ca(T, SSD_INNER), ca(T, SSD_INNER)
    ev_mix = ca(T, SSD_INNER + SB_W)
    b_tok = ca(T, SSD_G, P)
    cbm = ca(T, SSD_G, P)
    steps = ca(2, 4, P)
    decay = ca(2, 4, P)
    sb_w = ca(2, 3, P)
    sb_e = xc[:, 0:3, :].rearrange("p c t -> p (c t)").rearrange("p (b i t) -> p b i t", b=2, i=3)
    sb_l = xc[:, 3:6, :].rearrange("p c t -> p (c t)").rearrange("p (b i t) -> p b i t", b=2, i=3)
    ev_mixT = xp_flat[:, 0:3 * 4 * S].rearrange("p (k c t) -> p k c t", k=3, c=4)
    xdd = xT[:, 0:4, :].rearrange("p c t -> p (c t)")
    state = xT[:, 4:8, :].rearrange("p c t -> p (c t)")
    dt_raw, dt, dt_e, da = tiny(T, SSD_H), tiny(T, SSD_H), tiny(T, SSD_H), tiny(T, SSD_H)
    a_neg = tiny(SSD_H)
    carry = tiny(2, T, SSD_H)
    y_bank = {(0, 0): 2, (0, 1): 3, (1, 0): 0, (1, 1): 1}

    def even_tensor(pe):
        t = "ev"
        pe.wait_ge(sem("const_ready"), 1)
        pe.wait_ge(sem("x_landed"), 16)
        to_features_tensor(pe, t, h)
        project_tensor(pe, t, even_pieces)
        groups = [[(j, 4 * k + c) for c in range(4)] for k in range(2) for j in range(T)]
        groups.append([(j, 8 + g) for j in range(T) for g in range(SSD_G)])
        pe.wait_ge(sem("ev_conv_out"), CONV_C)
        for n, group in enumerate(groups):
            if n >= 2:
                pe.wait_ge(sem("ev_tok_read"), n - 1)
            for i, (j, c) in enumerate(group):
                last = nc.tensor.transpose(psum[6 + n % 2][:, i * P:(i + 1) * P], xc[:, c, j * P:(j + 1) * P], ident)
            last.then_inc(sem("ev_tok_turned"), 1)
        read_wait(pe, "ev", 0, len(even_pieces))
        read_wait(pe, "ev", 1, len(even_pieces))
        for j in range(T):
            for g in range(SSD_G):
                i = j * SSD_G + g
                last = nc.tensor.matmul(psum[4][:, i * P:(i + 1) * P], xc[:, 8 + g, j * P:(j + 1) * P],
                                        xc[:, 10 + g, j * P:(j + 1) * P], start=True, stop=True)
        last.then_inc(sem("ev_cb"), 1)
        pe.wait_ge(sem("ev_da_ready"), 1)
        dav = da.rearrange("p j h -> p (j h)")
        nc.tensor.matmul(psum[5][:, 0:32], upto, dav, start=True, stop=True)
        nc.tensor.matmul(psum[5][:, 32:64], above, dav, start=True, stop=True).then_inc(sem("ev_sums"), 1)
        pe.wait_ge(sem("ev_xdd_ready"), 1)
        for g in range(SSD_G):
            last = nc.tensor.matmul(psum[g], b_tok[:, 0, g, :], xdd[:, g * 512:(g + 1) * 512], start=True, stop=True)
        last.then_inc(sem("ev_state_full"), 1)
        for s in range(9):
            if s < 8:
                j, q = divmod(s, 4)
                pe.wait_ge(sem("ev_steps"), s + 1)
                if s >= 2:
                    pe.wait_ge(sem("ev_decay"), s - 1)
                for i in range(4):
                    last = nc.tensor.matmul(psum[6 + s % 2][:, i * P:(i + 1) * P], steps[:, s % 2, i, :], upto,
                                            start=True, stop=True)
                last.then_inc(sem("ev_seg"), 1)
            if s >= 1:
                j, q = divmod(s - 1, 4)
                pe.wait_ge(sem("ev_weights"), s)
                if s - 1 == 4:
                    pe.wait_ge(sem("ev_state"), 1)
                for i in range(4):
                    head = 4 * q + i
                    b = psum[y_bank[j, q // 2]]
                    last = nc.tensor.matmul(b[:, (q % 2) * 256 + i * 64:(q % 2) * 256 + (i + 1) * 64],
                                            decay[:, (s - 1) % 2, i, :], xdt[:, j, head * 64:(head + 1) * 64],
                                            start=True, stop=True)
                last.then_inc(sem("ev_diag"), 1)
        for g in range(SSD_G):
            last = nc.tensor.matmul(psum[4 + g], xc[:, 10 + g, P:S], state[:, g * 512:(g + 1) * 512], start=True, stop=True)
        last.then_inc(sem("ev_off"), 1)
        pe.wait_ge(sem("ev_ssd_read"), 1)
        for s in range(SB_H + 2):
            if s < SB_H:
                if s >= 2:
                    pe.wait_ge(sem("ev_sb_expo"), s - 1)
                r = slice((s % 2) * 64, (s % 2) * 64 + 64)
                kk, qq = sbk[r, s // 2, :], sbq[r, s // 2, :]
                nc.tensor.matmul(psum[s % 2][:, 0:S], kk[:, 0:P], qq, start=True, stop=True)
                nc.tensor.matmul(psum[s % 2][:, S:3 * P], kk[:, P:S], qq[:, P:S], start=True, stop=True)\
                    .then_inc(sem("ev_sb_z"), 1)
            if 1 <= s <= SB_H:
                v = s - 1
                pe.wait_ge(sem("ev_sb_l"), v + 1)
                lv = sb_l[:, v % 2].rearrange("p i t -> p (i t)")
                cum = psum[2 + v % 2]
                nc.tensor.matmul(cum[:, 0:P], atleast, lv[:, 0:P], start=True, stop=True)
                nc.tensor.matmul(cum[:, P:S], atleast, lv[:, P:S], start=True, stop=False)
                nc.tensor.matmul(cum[:, P:S], ones, lv[:, S:3 * P], start=False, stop=True)
                nc.tensor.matmul(cum[:, S:3 * P], atleast, lv[:, S:3 * P], start=True, stop=True)\
                    .then_inc(sem("ev_sb_cum"), 1)
            if s >= 2:
                v = s - 2
                pe.wait_ge(sem("ev_sb_w"), v + 1)
                vc = slice(v * 64, (v + 1) * 64)
                nc.tensor.matmul(psum[4][:, vc], sb_w[:, v % 2, 0, :], sbv[:, 0, vc], start=True, stop=True)
                nc.tensor.matmul(psum[5][:, vc], sb_w[:, v % 2, 1, :], sbv[:, 0, vc], start=True, stop=False)
                nc.tensor.matmul(psum[5][:, vc], sb_w[:, v % 2, 2, :], sbv[:, 1, vc], start=False, stop=True)\
                    .then_inc(sem("ev_sb_out"), 1)
        out_tensor(pe, t, ev_mix, ev_mixT, even_out)

    def even_scalar(act):
        A = nc.scalar
        n = 0
        for n, (name, _, _, _) in enumerate(even_pieces):
            full_wait(act, "ev", 0, n)
            b0 = psum[2 * (n % 3)]
            if name == "z":
                A.activation(zs[:, 0, n * 512:(n + 1) * 512], b0, ACT.Silu).then_inc(sem("bank0_read"), 1)
            elif name == "xbc":
                c = 4 * (n - 2)
                A.copy(xp[:, c:c + 2, 3:], b0.rearrange("p (c t) -> p c t", c=2)).then_inc(sem("bank0_read"), 1)
            elif name == "dt":
                A.copy(dt_raw[:, 0, :], b0[:, 0:SSD_H]).then_inc(sem("bank0_read"), 1)
            elif name == "q":
                A.mul(sbq[:, 0:2, :], b0.rearrange("p (c t) -> p c t", c=2), HD ** -0.5)\
                    .then_inc(sem("bank0_read"), 1)
            elif name == "k":
                A.copy(sbk[:, 0:2, :], b0.rearrange("p (c t) -> p c t", c=2)).then_inc(sem("bank0_read"), 1)
            else:
                A.copy(sbv[:, 0, :], b0).then_inc(sem("bank0_read"), 1)
        read_wait(act, "ev", 1, 2)
        A.activation(zs[:, 1, :], zs[:, 1, :], ACT.Silu).then_inc(sem("ev_z_ready"), 1)
        for c in range(CONV_C):
            act.wait_ge(sem("ev_conv_sum"), c + 1)
            A.activation(xc[:, c, :], xc[:, c, :], ACT.Silu, bias=par["conv_b"][:, c:c + 1])\
                .then_inc(sem("ev_conv_out"), 1)
        act.wait_ge(sem("ev_dt_negabs"), 1)
        A.activation(dt_e, dt_e, ACT.Exp).then_inc(sem("ev_dt_exp"), 1)
        act.wait_ge(sem("ev_dt_exp"), 1)
        A.activation(dt_e, dt_e, ACT.Ln, bias=1.0).then_inc(sem("ev_dt_ln"), 1)
        A.activation(a_neg, par["a_log"], ACT.Exp).then_inc(sem("ev_a_exp"), 1)
        act.wait_ge(sem("ev_sums"), 1)
        A.activation(carry.rearrange("p a j h -> p (a j h)"), psum[5][:, 0:64], ACT.Exp).then_inc(sem("ev_carry"), 1)
        act.wait_ge(sem("ev_state_full"), 1)
        A.copy(state[:, 0:512], psum[0])
        A.copy(state[:, 512:1024], psum[1]).then_inc(sem("ev_state"), 1)
        for s in range(8):
            act.wait_ge(sem("ev_seg"), s + 1)
            if s >= 2:
                act.wait_ge(sem("ev_diag"), s - 1)
            A.activation(decay[:, s % 2], psum[6 + s % 2].rearrange("p (i l) -> p i l", i=4), ACT.Exp)\
                .then_inc(sem("ev_decay"), 1)
        for s in range(SB_H + 2):
            if s >= 2:
                v = s - 2
                act.wait_ge(sem("ev_sb_expo"), v + 1)
                A.activation(sb_w[:, v % 2], sb_w[:, v % 2], ACT.Exp).then_inc(sem("ev_sb_w"), 1)
            if s < SB_H:
                act.wait_ge(sem("ev_sb_z"), s + 1)
                if s >= 2:
                    act.wait_ge(sem("ev_sb_l"), s - 1)
                A.activation(sb_e[:, s % 2], psum[s % 2][:, 0:3 * P].rearrange("p (i t) -> p i t", i=3), ACT.Abs)\
                    .then_inc(sem("ev_sb_abs"), 1)
                act.wait_ge(sem("ev_sb_abs"), s + 1)
                A.activation(sb_e[:, s % 2], sb_e[:, s % 2], ACT.Exp, scale=-1.0).then_inc(sem("ev_sb_exp"), 1)
                act.wait_ge(sem("ev_sb_exp"), s + 1)
                A.activation(sb_e[:, s % 2], sb_e[:, s % 2], ACT.Ln, bias=1.0).then_inc(sem("ev_sb_ln"), 1)
        rsqrt_scalar(act, sq, T)
        rsqrt_scalar(act, sq, T)

    def even_vector(dve):
        V.memset(xp[:, :, 0:3], 0.0).then_inc(sem("ev_pad"), 1)
        dve.wait_ge(sem("ev_pad"), 1)
        to_features_vector("ev")
        dve.wait_ge(sem("params_landed"), 16 * len(par_loads))
        for n, (name, _, _, _) in enumerate(even_pieces):
            full_wait(dve, "ev", 1, n)
            b1 = psum[2 * (n % 3) + 1]
            b1c = b1.rearrange("p (c t) -> p c t", c=2)
            read = sem("bank1_read")
            if name == "z":
                vlink(V.tensor_copy(zs[:, 1, n * 512:(n + 1) * 512], b1), read)
            elif name == "xbc":
                c = 4 * (n - 2)
                vlink(V.tensor_copy(xp[:, c + 2:c + 4, 3:], b1c), read)
                read_wait(dve, "ev", 0, n + 1)
                for c in range(c, c + 4):
                    vlink(V.tensor_scalar(xc[:, c, :], xp[:, c, 0:S], par["conv_w"][:, 0, c:c + 1], None, ALU.mult))
                    for k in range(1, CONV_K):
                        vlink(V.scalar_tensor_tensor(out=xc[:, c, :], in0=xp[:, c, k:k + S],
                                                     scalar=par["conv_w"][:, k, c:c + 1], in1=xc[:, c, :],
                                                     op0=ALU.mult, op1=ALU.add),
                              *([sem("ev_conv_sum")] if k == CONV_K - 1 else []))
            elif name == "dt":
                vlink(V.tensor_copy(dt_raw[:, 1, :], b1[:, 0:SSD_H]), read)
            elif name == "q":
                vlink(V.tensor_scalar(sbq[:, 2:4, :], b1c, HD ** -0.5, None, ALU.mult), read)
            elif name == "k":
                vlink(V.tensor_copy(sbk[:, 2:4, :], b1c), read)
            else:
                vlink(V.tensor_copy(sbv[:, 1, :], b1), read)
        read_wait(dve, "ev", 0, 6)
        vlink(V.tensor_tensor(dt_raw, dt_raw, over(par["dt_bias"], 1, T), ALU.add))
        vlink(minus_abs(dt_e, dt_raw), sem("ev_dt_negabs"))
        dve.wait_ge(sem("ev_dt_ln"), 1)
        vlink(V.scalar_tensor_tensor(out=dt, in0=dt_raw, scalar=0.0, in1=dt_e, op0=ALU.max, op1=ALU.add))
        dve.wait_ge(sem("ev_a_exp"), 1)
        vlink(V.scalar_tensor_tensor(out=da, in0=dt, scalar=-1.0, in1=over(a_neg, 1, T), op0=ALU.mult, op1=ALU.mult),
              sem("ev_da_ready"))
        for n in range(5):
            dve.wait_ge(sem("ev_tok_turned"), n + 1)
            if n < 4:
                k, j = divmod(n, 2)
                vlink(V.tensor_copy(xs_tok[:, j, k * 512:(k + 1) * 512], psum[6 + n % 2]), sem("ev_tok_read"))
            else:
                vlink(V.tensor_copy(b_tok, psum[6].rearrange("p (j g n) -> p j g n", j=T, g=SSD_G)), sem("ev_tok_read"))
        dve.wait_ge(sem("ev_cb"), 1)
        vlink(V.tensor_tensor(cbm.rearrange("p j g l -> p (j g) l"), psum[4].rearrange("p (i l) -> p i l", i=4),
                              over(upto, 1, 4), ALU.mult))
        for j in range(T):
            vlink(V.tensor_tensor(xdt[:, j, :].rearrange("p (h d) -> p h d", d=SSD_P),
                                  xs_tok[:, j, :].rearrange("p (h d) -> p h d", d=SSD_P),
                                  over(dt[:, j, :], 2, SSD_P), ALU.mult))
        dve.wait_ge(sem("ev_carry"), 1)
        vlink(V.tensor_tensor(xdd.rearrange("p (h d) -> p h d", d=SSD_P),
                              xdt[:, 0, :].rearrange("p (h d) -> p h d", d=SSD_P),
                              over(carry[:, 1, 0, :], 2, SSD_P), ALU.mult), sem("ev_xdd_ready"))
        for s in range(9):
            if s < 8:
                j, q = divmod(s, 4)
                if s >= 2:
                    dve.wait_ge(sem("ev_seg"), s - 1)
                vlink(V.tensor_tensor(steps[:, s % 2], over(above, 1, 4), over(da[:, j, 4 * q:4 * q + 4], 2, P), ALU.mult),
                      sem("ev_steps"))
            if s >= 1:
                j, q = divmod(s - 1, 4)
                dve.wait_ge(sem("ev_decay"), s)
                vlink(V.tensor_tensor(decay[:, (s - 1) % 2], decay[:, (s - 1) % 2], over(cbm[:, j, q // 2, :], 1, 4),
                                      ALU.mult), sem("ev_weights"))
        dve.wait_ge(sem("ev_diag"), 8)
        dve.wait_ge(sem("ev_off"), 1)
        dve.wait_ge(sem("ev_z_ready"), 1)
        for j in range(T):
            for half in range(2):
                heads = slice(8 * half, 8 * half + 8)
                cols = slice(512 * half, 512 * half + 512)

                def by_head(ap):
                    return ap.rearrange("p (h d) -> p h d", d=SSD_P)
                y = ev_mix[:, j, cols]
                vlink(V.tensor_tensor(by_head(y), by_head(xs_tok[:, j, cols]), over(par["d_skip"][:, heads], 2, SSD_P),
                                      ALU.mult))
                vlink(V.tensor_tensor(y, y, psum[y_bank[j, half]], ALU.add))
                if j == 1:
                    off = xdt[:, 0, cols]
                    vlink(V.tensor_tensor(by_head(off), by_head(psum[4 + half]), over(carry[:, 0, 1, heads], 2, SSD_P),
                                          ALU.mult))
                    vlink(V.tensor_tensor(y, y, off, ALU.add))
                vlink(V.tensor_tensor(y, y, zs[:, j, cols], ALU.mult),
                      *([sem("ev_ssd_read")] if (j, half) == (1, 1) else []))
        for s in range(SB_H + 2):
            if s >= 2:
                v = s - 2
                dve.wait_ge(sem("ev_sb_cum"), v + 1)
                if v >= 2:
                    dve.wait_ge(sem("ev_sb_out"), v - 1)
                zv = psum[v % 2][:, 0:3 * P].rearrange("p (i t) -> p i t", i=3)
                cv = psum[2 + v % 2][:, 0:3 * P].rearrange("p (i t) -> p i t", i=3)
                vlink(V.tensor_copy(sb_w[:, v % 2], zv))
                vlink(V.tensor_tensor(sb_w[:, v % 2], sb_w[:, v % 2], cv, ALU.subtract))
                vlink(V.tensor_tensor(sb_w[:, v % 2], sb_w[:, v % 2], mask_strict, ALU.add), sem("ev_sb_expo"))
            if 1 <= s <= SB_H:
                v = s - 1
                dve.wait_ge(sem("ev_sb_ln"), v + 1)
                if v >= 2:
                    dve.wait_ge(sem("ev_sb_cum"), v - 1)
                zv = psum[v % 2][:, 0:3 * P].rearrange("p (i t) -> p i t", i=3)
                vlink(V.scalar_tensor_tensor(out=sb_l[:, v % 2], in0=zv, scalar=0.0, in1=sb_e[:, v % 2],
                                             op0=ALU.max, op1=ALU.add))
                vlink(V.tensor_tensor(sb_l[:, v % 2], sb_l[:, v % 2], keep_strict, ALU.mult), sem("ev_sb_l"))
        rms_scale(ev_mix[:, :, 0:SSD_INNER], xdt[:, 1, :], SSD_INNER, rstd)
        for j in range(T):
            vlink(V.tensor_scalar(ev_mix[:, j, 0:SSD_INNER], ev_mix[:, j, 0:SSD_INNER], rstd[:, j:j + 1], None, ALU.mult))
        dve.wait_ge(sem("ev_sb_out"), SB_H)
        for j in range(T):
            vlink(V.tensor_copy(ev_mix[:, j, SSD_INNER:], psum[4 + j]), *([sem("mix_ready")] if j else []))
        out_vector("ev", ev_mixT, 3, ALPHA, par["ssd_norm"])
        dve.wait_ge(sem("norm_landed"), 32)
        layer_norm()
        dve.sem_inc(sem("phase_done"), 1)

    carved = [0]

    def parts(name, *shape):
        at = carved[0]
        carved[0] += int(np.prod(shape))
        assert carved[0] <= ARENA
        return parts_at(name, arena_at + 4 * at, *shape)

    def plain(size):
        at = carved[0]
        carved[0] += size
        assert carved[0] <= ARENA
        return arena[:, at:at + size]

    GU_PIECES, DOWN_PIECES = DC // 2, BLK // P
    gu_hi, gu_lo = parts("gu_hi", DC, 2 * BLK), parts("gu_lo", DC, 2 * BLK)
    dn_hi, dn_lo = parts("dn_hi", DOWN_PIECES, D), parts("dn_lo", DOWN_PIECES, D)
    tok_at = arena_at + 4 * carved[0]
    tok_hi, tok_lo = parts("tok_hi", T, D), parts("tok_lo", T, D)
    xt_hi, xt_lo = parts_at("xt_hi", tok_at, DC, S), parts_at("xt_lo", tok_at + 4 * DC * S, DC, S)
    silu_buf = plain(2 * BLK).rearrange("p (a b) -> p a b", a=2)
    hid = plain(2 * BLK).rearrange("p (a b) -> p a b", a=2)
    junk_row = arena[:, carved[0]:carved[0] + D]
    hidT_hi, hidT_lo = parts("hidt_hi", 2, 2, P), parts("hidt_lo", 2, 2, P)
    pick_t = parts("pick_t", T, P)
    pick_r = parts("pick_r", T, P)
    zeros = parts("zeros", P)
    normed = arena[:, carved[0]:carved[0] + T * D].rearrange("p (j d) -> p j d", j=T)
    yg_hi, yg_lo = parts("yg_hi", D), parts("yg_lo", D)
    xg_hi, xg_lo = parts_at("xg_hi", xt_at, DC, P), parts_at("xg_lo", xt_at + 4 * DC * P, DC, P)
    ov_x = pieces[:, 0, 0:DC * P].rearrange("p (c t) -> p c t", c=DC)
    ov_y = pieces[:, 0, DC * P:DC * P + D]
    ov_hidT = pieces[:, 1, 0:2 * P].rearrange("p (f t) -> p f t", f=2)
    gates = tiny(T, MOE_E)
    member = tiny(T, 8)
    row_of = tiny(T, 8)
    unit_row, unit_gate = tiny(T), tiny(T, 4)
    row_gate = tiny(4)
    SLOTS = P

    FFS = {"m0": (0, 0, 0, MOE_GRP, 4), "m1": (16, 16, 4, MOE_GRP, 4), "ff": (32, 32, 8, 1, DENSE_FF // BLK),
           "m2": (43, 54, 8, MOE2_E, MOE2_FF // BLK)}
    FF_PHASE = {"m0": 0, "m1": 1, "ff": 2, "m2": 3}
    CREDIT = 2
    GU_CREDIT = 2 * GU_PIECES
    DOWN_CREDIT = 2 * DOWN_PIECES
    GU_USED, DOWN_USED = GU_PIECES, 2 * DOWN_PIECES

    def credits_tensor(pe):
        for name in ("hid_done", "scattered", "scatter_read"):
            pe.sem_inc(sem(name), CREDIT)
        pe.sem_inc(sem("gu_piece"), GU_USED)
        pe.sem_inc(sem("down_piece"), DOWN_USED)

    def make_step(t, u, i, c):
        b0, s0, _, _, nb = FFS[t]
        if t == "ff":
            blk = b0 + c // 2
            return {"s": s0 + 4 * i + c, "G": blk + 2 * i, "slot": blk % 2, "uses": blk // 2 + i + 1, "par": c % 2,
                    "col": None, "tile": c % 2}
        return {"s": s0 + nb * u + 2 * i + c, "G": b0 + nb * u + 2 * i + c, "slot": (b0 + c) % 2,
                "uses": (b0 + c) // 2 + nb // 2 * u + i + 1, "par": c % 2, "col": (2 * i + c if nb == 4 else 0), "tile": 0}

    def middle(eng, t, u, fn):
        nb = FFS[t][4]
        period, n = (4, 2 * nb) if t == "ff" else (2, nb)
        loops = (n - 2) // period

        def run(i):
            for c in range(1, period + 1):
                fn(make_step(t, u, i, c), make_step(t, u, i, c - 1), make_step(t, u, i, c + 1))
        if loops == 1:
            run(0)
        else:
            with eng.Fori(0, loops) as i:
                run(i)
        last = make_step(t, u, loops, 1)
        fn(last, make_step(t, u, loops, 0), None)
        return last

    def units(eng, t, unit):
        n = FFS[t][3]
        with eng.Fori(0, n - 1) as u:
            unit(u, False)
        unit(n - 1, True)

    def three_products(bank, a, b, start, stop):
        (a_hi, a_lo), (b_hi, b_lo) = a, b
        nc.tensor.matmul(bank, a_lo, b_hi, start=start, stop=False)
        nc.tensor.matmul(bank, a_hi, b_lo, start=False, stop=False)
        return nc.tensor.matmul(bank, a_hi, b_hi, start=False, stop=stop)

    def gate_up_tensor(pe, st, x, pair):
        if pair == 0:
            pe.wait_ge(sem("hid_done"), st["s"] - 1 + CREDIT)
        for k in (2 * pair, 2 * pair + 1):
            pe.wait_ge(sem("gu_split"), GU_PIECES * st["G"] + k + 1 + GU_CREDIT)
            for c in (2 * k, 2 * k + 1):
                last = three_products(psum[st["par"]], x(c), (gu_hi[:, c, :], gu_lo[:, c, :]), c == 0, c == DC - 1)
            last.then_inc(sem("gu_piece"), 1)

    def turn_tensor(pe, st):
        pe.wait_ge(sem("hid_done"), st["s"] + 1 + CREDIT)
        for f in range(2):
            at = st["par"] * BLK + f * P
            last = nc.tensor.transpose(psum[2][:, at:at + P], hid[:, st["par"], f * P:(f + 1) * P], ident)
        last.then_inc(sem("hid_turned"), 1)

    def down_tensor(pe, st, final=False):
        pe.wait_ge(sem("hidt_split"), st["s"] + 1)
        for f in range(DOWN_PIECES):
            pe.wait_ge(sem("down_split"), DOWN_PIECES * st["G"] + f + 1 + DOWN_CREDIT)
            for half in range(2):
                cols = slice(half * 512, (half + 1) * 512)
                last = three_products(psum[3 + 2 * st["tile"] + half],
                                      (hidT_hi[:, st["par"], f, :], hidT_lo[:, st["par"], f, :]),
                                      (dn_hi[:, f, cols], dn_lo[:, f, cols]), False, final and f == 1)
            last.then_inc(sem("down_piece"), 1)

    def clear_tensor(banks):
        for b in banks:
            for k in range(4):
                nc.tensor.matmul(psum[b][:, k * P:(k + 1) * P], zeros, zeros, start=(k == 0), stop=False)

    def gather_matmuls():
        for c in range(DC):
            for j in range(T):
                for k, src in enumerate((tok_lo, tok_hi)):
                    last = nc.tensor.matmul(psum[5 + c // 4][:, (c % 4) * P:(c % 4 + 1) * P],
                                            src[:, j, :].rearrange("t (p c) -> t c p", c=DC)[:, c, :], pick_t[:, j, :],
                                            start=(j == 0 and k == 0), stop=(j == T - 1 and k == 1))
            if c % 4 == 3:
                yield last

    def gather_tensor(pe, q):
        pe.wait_ge(sem("pick_ready"), q + 1)
        if not (isinstance(q, int) and q == 0):
            pe.wait_ge(sem("scatter_read"), 4 * (q - 1) + CREDIT)
        for last in gather_matmuls():
            last.then_inc(sem("gathered"), 1)

    def permute_tensor(pe, signal):
        for j in range(T):
            nc.tensor.transpose(psum[7][:, j * P:(j + 1) * P], pick_t[:, j, :].bitcast(F32), ident)
        for j in range(T):
            last = nc.tensor.matmul(psum[7][:, 256:260], pick_t[:, j, :].bitcast(F32), unit_gate[:, j, :],
                                    start=(j == 0), stop=(j == T - 1))
        last.then_inc(signal, 1)

    def scatter_tensor(pe, q):
        pe.wait_ge(sem("yg_split"), q + 1)
        pe.wait_ge(sem("scatter_read"), 4 * q + CREDIT)
        for k in range(4):
            j, half = divmod(k, 2)
            if k >= 2:
                pe.wait_ge(sem("scatter_read"), 4 * q + k - 1 + CREDIT)
            for part, src in enumerate((yg_lo, yg_hi)):
                last = nc.tensor.matmul(psum[5 + k % 2], pick_r[:, j, :], src[:, half * 512:(half + 1) * 512],
                                        start=(part == 0), stop=(part == 1))
            last.then_inc(sem("scattered"), 1)

    def ff_begin_tensor(pe, t, phase, route):
        pe.wait_ge(sem("phase_done"), phase)
        src = h
        if t in ("ff", "m2"):
            pe.wait_ge(sem("normed"), PHASE[t] - 3)
            src = normed
        to_features_tensor(pe, t, src)
        pe.wait_ge(sem("xt_ready"), PHASE[t] + 1)
        if route is not None:
            n = route.shape[2]
            for j in range(T):
                for c in range(DC):
                    last = nc.tensor.matmul(psum[4][:, 32 * j:32 * j + n], xT[:, c, j * P:(j + 1) * P], route[:, c, :],
                                            start=(c == 0), stop=(c == DC - 1))
            last.then_inc(sem("route_logits"), 1)
            pe.wait_ge(sem("route_member"), ROUTER[t] + 1)
            before = keep_strict[:, 0, :]
            nc.tensor.matmul(psum[7][:, 0:8], before, member[:, 0, :], start=True, stop=True)
            nc.tensor.matmul(psum[7][:, 8:16], ones, member[:, 0, :], start=True, stop=False)
            nc.tensor.matmul(psum[7][:, 8:16], before, member[:, 1, :], start=False, stop=True)
            nc.tensor.matmul(psum[7][:, 16:24], ones, member[:, 0, :], start=True, stop=False)
            nc.tensor.matmul(psum[7][:, 16:24], ones, member[:, 1, :], start=False, stop=True)\
                .then_inc(sem("route_rows"), 1)
        pe.wait_ge(sem("zeros_ready"), FF_PHASE[t] + 1)

    def dense_tensor(pe):
        ff_begin_tensor(pe, "ff", 5, None)
        clear_tensor((3, 4, 5, 6))
        pe.wait_ge(sem("tok_split"), FF_PHASE["ff"] + 1)

        def x_of(st):
            rows = slice(st["tile"] * P, (st["tile"] + 1) * P)
            return lambda c: (xt_hi[:, c, rows], xt_lo[:, c, rows])

        def step(st, prev, following):
            gate_up_tensor(pe, st, x_of(st), 0)
            turn_tensor(pe, prev)
            gate_up_tensor(pe, st, x_of(st), 1)
            down_tensor(pe, prev, following is None)
        first = make_step("ff", 0, 0, 0)
        gate_up_tensor(pe, first, x_of(first), 0)
        gate_up_tensor(pe, first, x_of(first), 1)
        last = middle(pe, "ff", 0, step)
        turn_tensor(pe, last)
        down_tensor(pe, last, True)

    def moe_tensor(pe, t, phase, route):
        ff_begin_tensor(pe, t, phase, route)
        q0 = FFS[t][2]

        def x(c):
            return xg_hi[:, c, :], xg_lo[:, c, :]

        def first_step(u, q):
            pe.wait_ge(sem("rows_split"), 2 * q + 2)
            st = make_step(t, u, 0, 0)
            gate_up_tensor(pe, st, x, 0)
            gate_up_tensor(pe, st, x, 1)

        def step(st, prev, following):
            gate_up_tensor(pe, st, x, 0)
            turn_tensor(pe, prev)
            gate_up_tensor(pe, st, x, 1)
            down_tensor(pe, prev)

        def unit(u, final):
            q = q0 + u
            last = middle(pe, t, u, step)
            if not final:
                gather_tensor(pe, q + 1)
                pe.wait_ge(sem("pickr_ready"), q + 1)
                permute_tensor(pe, sem("permuted"))
            turn_tensor(pe, last)
            down_tensor(pe, last, True)
            if not final:
                first_step(u + 1, q + 1)
            scatter_tensor(pe, q)
            if not final:
                clear_tensor((3, 4))
        pe.wait_ge(sem("tok_split"), FF_PHASE[t] + 1)
        gather_tensor(pe, q0)
        permute_tensor(pe, sem("permuted"))
        clear_tensor((3, 4))
        first_step(0, q0)
        units(pe, t, unit)
        overflow_tensor(pe, t)

    def gu_hi_scalar(act, blk, ks):
        for k in ks:
            if k == 0:
                act.wait_ge(sem(f"gu_landed{blk['slot']}"), 32 * blk["uses"])
            act.wait_ge(sem("gu_piece"), GU_PIECES * (blk["s"] - 1) + k + 1 + GU_USED)
            nc.scalar.copy(gu_hi[:, 2 * k:2 * k + 2, :], ffw_gu[:, blk["slot"], 2 * k:2 * k + 2, :])\
                .then_inc(sem("gu_hi_ready"), 1)

    def down_hi_scalar(act, blk, f):
        if f == 0:
            act.wait_ge(sem(f"down_landed{blk['slot']}"), 16 * blk["uses"])
        act.wait_ge(sem("down_piece"), DOWN_PIECES * (blk["s"] - 1) + f + 1 + DOWN_USED)
        nc.scalar.copy(dn_hi[:, f, :], ffw_d[:, blk["slot"], f, :]).then_inc(sem("down_hi_ready"), 1)

    def silu_scalar(act, st):
        act.wait_ge(sem("gu_piece"), GU_PIECES * (st["s"] + 1) + GU_USED)
        act.wait_ge(sem("hid_done"), st["s"] - 1 + CREDIT)
        nc.scalar.activation(silu_buf[:, st["par"], :], psum[st["par"]][:, 0:BLK], ACT.Silu).then_inc(sem("silu_done"), 1)

    def hidt_hi_scalar(act, st):
        act.wait_ge(sem("hid_turned"), st["s"] + 1)
        act.wait_ge(sem("down_piece"), DOWN_PIECES * (st["s"] - 1) + DOWN_USED)
        nc.scalar.copy(hidT_hi[:, st["par"]].rearrange("p f t -> p (f t)"),
                       psum[2][:, st["par"] * BLK:(st["par"] + 1) * BLK]).then_inc(sem("hidt_hi_ready"), 1)

    def rows_hi_scalar(act, q):
        for k in range(2):
            act.wait_ge(sem("gathered"), 2 * q + k + 1)
            nc.scalar.copy(xg_hi[:, 4 * k:4 * k + 4, :].rearrange("p c t -> p (c t)"), psum[5 + k])\
                .then_inc(sem("rows_hi_ready"), 1)

    def sums_hi_scalar(act, q, last):
        act.wait_ge(sem("scattered"), 4 * q + CREDIT)
        act.wait_ge(sem("down_piece"), DOWN_PIECES * (last["s"] + 1) + DOWN_USED)
        for half in range(2):
            nc.scalar.copy(yg_hi[:, half * 512:(half + 1) * 512], psum[3 + half]).then_inc(sem("yg_hi_ready"), 1)

    def ff_scalar(act, t):
        act.wait_ge(sem("phase_done"), PHASE[t])
        if t in ("ff", "m2"):
            rsqrt_scalar(act, sq, T)
            act.wait_ge(sem("normed"), PHASE[t] - 3)
        if t == "ff":
            act.wait_ge(sem("xt_ready"), PHASE[t] + 1)
            src, dst = xT.rearrange("p (j c) t -> p j (c t)", j=2), xt_hi.rearrange("p (j c) t -> p j (c t)", j=2)
        else:
            src, dst = (h if t != "m2" else normed), tok_hi
        for j in range(T):
            nc.scalar.copy(dst[:, j, :], src[:, j, :]).then_inc(sem("tok_hi_ready"), 1)

        def begin(st, following):
            gu_hi_scalar(act, following, (0, 1, 2))
            silu_scalar(act, st)
            gu_hi_scalar(act, following, (3,))
            down_hi_scalar(act, st, 0)
            down_hi_scalar(act, st, 1)
        if t == "ff":
            def step(st, prev, following):
                if st["tile"]:
                    if following is not None:
                        gu_hi_scalar(act, following, (0, 1))
                    hidt_hi_scalar(act, prev)
                    if following is not None:
                        gu_hi_scalar(act, following, (2,))
                    silu_scalar(act, st)
                    if following is not None:
                        gu_hi_scalar(act, following, (3,))
                else:
                    hidt_hi_scalar(act, prev)
                    silu_scalar(act, st)
                    down_hi_scalar(act, st, 0)
                    down_hi_scalar(act, st, 1)
            first = make_step(t, 0, 0, 0)
            gu_hi_scalar(act, first, (0, 1, 2, 3))
            silu_scalar(act, first)
            down_hi_scalar(act, first, 0)
            down_hi_scalar(act, first, 1)
            hidt_hi_scalar(act, middle(act, t, 0, step))
            return
        gu_hi_scalar(act, make_step(t, 0, 0, 0), (0, 1, 2, 3))
        act.wait_ge(sem("route_masked"), ROUTER[t] + 1)
        nc.scalar.activation(r_e, r_e, ACT.Exp).then_inc(sem("route_exp"), 1)
        q0, nb = FFS[t][2], FFS[t][4]

        def unit(u, final):
            def step(st, prev, following):
                nxt = following if following is not None else (None if final else make_step(t, u + 1, 0, 0))
                if nxt is not None:
                    gu_hi_scalar(act, nxt, (0, 1))
                hidt_hi_scalar(act, prev)
                if nxt is not None:
                    gu_hi_scalar(act, nxt, (2,))
                silu_scalar(act, st)
                if nxt is not None:
                    gu_hi_scalar(act, nxt, (3,))
                down_hi_scalar(act, st, 0)
                down_hi_scalar(act, st, 1)
            last = middle(act, t, u, step)
            if not final:
                rows_hi_scalar(act, q0 + u + 1)
            hidt_hi_scalar(act, last)
            sums_hi_scalar(act, q0 + u, last)
            if not final:
                begin(make_step(t, u + 1, 0, 0), make_step(t, u + 1, 0, 1))
        rows_hi_scalar(act, q0)
        begin(make_step(t, 0, 0, 0), make_step(t, 0, 0, 1))
        units(act, t, unit)
        overflow_scalar(act, t)
        if t in ("m0", "m1"):
            rsqrt_scalar(act, sq, T)

    def rest(out, x, hi):
        return V.tensor_tensor(out, x, hi.bitcast(F32), ALU.subtract)

    def tokens_lo_vector(dve, t, src):
        lo, hi = (xt_lo, xt_hi) if t == "ff" else (tok_lo, tok_hi)
        if t == "ff":
            lo, hi = (a.rearrange("p (j c) t -> p j (c t)", j=2) for a in (lo, hi))
        for j in range(T):
            dve.wait_ge(sem("tok_hi_ready"), T * FF_PHASE[t] + j + 1)
            vlink(rest(lo[:, j, :], src[:, j, :], hi[:, j, :]), *([sem("tok_split")] if j else []))

    def gu_lo_vector(dve, blk, ks):
        for k in ks:
            dve.wait_ge(sem("gu_hi_ready"), GU_PIECES * blk["G"] + k + 1)
            rest(gu_lo[:, 2 * k:2 * k + 2, :], ffw_gu[:, blk["slot"], 2 * k:2 * k + 2, :], gu_hi[:, 2 * k:2 * k + 2, :])\
                .then_inc(sem("gu_split"), 1)

    def down_lo_vector(dve, blk, f):
        dve.wait_ge(sem("down_hi_ready"), DOWN_PIECES * blk["G"] + f + 1)
        rest(dn_lo[:, f, :], ffw_d[:, blk["slot"], f, :], dn_hi[:, f, :]).then_inc(sem("down_split"), 1)

    def first_weights_vector(dve, t, ks):
        gu_lo_vector(dve, make_step(t, 0, 0, 0), ks)

    def hidden_vector(dve, st):
        dve.wait_ge(sem("silu_done"), st["s"] + 1)
        up = psum[st["par"]][:, BLK:2 * BLK]
        if st["col"] is None:
            ins = V.tensor_tensor(hid[:, st["par"], :], silu_buf[:, st["par"], :], up, ALU.mult)
        else:
            ins = V.scalar_tensor_tensor(out=hid[:, st["par"], :], in0=silu_buf[:, st["par"], :],
                                         scalar=row_gate[:, st["col"]:st["col"] + 1], in1=up, op0=ALU.mult, op1=ALU.mult)
        ins.then_inc(sem("hid_done"), 1)

    def hidt_lo_vector(dve, st):
        dve.wait_ge(sem("hidt_hi_ready"), st["s"] + 1)
        rest(hidT_lo[:, st["par"]].rearrange("p f t -> p (f t)"), psum[2][:, st["par"] * BLK:(st["par"] + 1) * BLK],
             hidT_hi[:, st["par"]].rearrange("p f t -> p (f t)")).then_inc(sem("hidt_split"), 1)

    def pick_vector(dve, t, u, q):
        if not (isinstance(q, int) and q == 0):
            dve.wait_ge(sem("pick_ready"), q)
        V.tensor_copy(unit_row, row_of[:, :, bass.ds(u, 1)].rearrange("p j a -> p (j a)")).then_inc(sem("unit_picked"), 1)
        cols = gates[:, :, bass.ds(4 * u, 4)] if t != "m2" else gates[:, :, bass.ds(u, 4)]
        V.tensor_copy(unit_gate, cols).then_inc(sem("unit_picked"), 1)
        dve.wait_ge(sem("unit_picked"), 2 * q + 2)
        for j in range(T):
            ins = V.tensor_scalar(pick_t[:, j, :], row_index, unit_row[:, j:j + 1], None, ALU.is_equal)
        ins.then_inc(sem("pick_ready"), 1)

    def rows_lo_vector(dve, q):
        for k in range(2):
            dve.wait_ge(sem("rows_hi_ready"), 2 * q + k + 1)
            rest(xg_lo[:, 4 * k:4 * k + 4, :].rearrange("p c t -> p (c t)"), psum[5 + k],
                 xg_hi[:, 4 * k:4 * k + 4, :].rearrange("p c t -> p (c t)")).then_inc(sem("rows_split"), 1)

    def row_gate_vector(dve, q, s):
        dve.wait_ge(sem("permuted"), q + 1)
        dve.wait_ge(sem("hid_done"), s + CREDIT)
        V.tensor_copy(row_gate, psum[7][:, 256:260]).then_inc(sem("rowgate_ready"), 1)

    def pickr_vector(dve, q):
        dve.wait_ge(sem("scattered"), 4 * q + CREDIT)
        V.tensor_copy(pick_r.rearrange("p j t -> p (j t)"), psum[7][:, 0:2 * P]).then_inc(sem("pickr_ready"), 1)

    def sums_lo_vector(dve, q):
        for half in range(2):
            dve.wait_ge(sem("yg_hi_ready"), 2 * q + half + 1)
            cols = slice(half * 512, (half + 1) * 512)
            last = rest(yg_lo[:, cols], psum[3 + half], yg_hi[:, cols])
        last.then_inc(sem("yg_split"), 1)

    def scatter_vector(dve, q):
        for k in range(4):
            j, half = divmod(k, 2)
            dve.wait_ge(sem("scattered"), 4 * q + k + 1 + CREDIT)
            hv = h[:, j, half * 512:(half + 1) * 512]
            V.tensor_tensor(hv, psum[5 + k % 2], hv, ALU.add).then_inc(sem("scatter_read"), 1)

    def ff_vector(dve, t):
        b0, s0, q0, n_units, nb = FFS[t]
        if t == "ff":
            def step(st, prev, following):
                if st["tile"]:
                    if following is not None:
                        gu_lo_vector(dve, following, (0, 1))
                    hidt_lo_vector(dve, prev)
                    if following is not None:
                        gu_lo_vector(dve, following, (2,))
                    hidden_vector(dve, st)
                    if following is not None:
                        gu_lo_vector(dve, following, (3,))
                else:
                    hidt_lo_vector(dve, prev)
                    hidden_vector(dve, st)
                    down_lo_vector(dve, st, 0)
                    down_lo_vector(dve, st, 1)
            first = make_step(t, 0, 0, 0)
            gu_lo_vector(dve, first, (0, 1, 2, 3))
            hidden_vector(dve, first)
            down_lo_vector(dve, first, 0)
            down_lo_vector(dve, first, 1)
            hidt_lo_vector(dve, middle(dve, t, 0, step))
            dve.wait_ge(sem("down_piece"), DOWN_PIECES * (s0 + 2 * nb) + DOWN_USED)
            for k in range(4):
                hv = h[:, k // 2, (k % 2) * 512:(k % 2 + 1) * 512]
                vlink(V.tensor_tensor(hv, psum[3 + k], hv, ALU.add))
            return

        def begin(st, following, q):
            gu_lo_vector(dve, following, (0, 1, 2))
            dve.wait_ge(sem("rowgate_ready"), q + 1)
            hidden_vector(dve, st)
            if not (isinstance(q, int) and q == q0):
                scatter_vector(dve, q - 1)
                pickr_vector(dve, q)
            gu_lo_vector(dve, following, (3,))
            down_lo_vector(dve, st, 0)
            down_lo_vector(dve, st, 1)

        def unit(u, final):
            q = q0 + u
            if not final:
                pick_vector(dve, t, u + 1, q + 1)

            def step(st, prev, following):
                nxt = following if following is not None else (None if final else make_step(t, u + 1, 0, 0))
                if nxt is not None:
                    gu_lo_vector(dve, nxt, (0, 1))
                hidt_lo_vector(dve, prev)
                if nxt is not None:
                    gu_lo_vector(dve, nxt, (2,))
                hidden_vector(dve, st)
                if nxt is not None:
                    gu_lo_vector(dve, nxt, (3,))
                down_lo_vector(dve, st, 0)
                down_lo_vector(dve, st, 1)
            last = middle(dve, t, u, step)
            if not final:
                rows_lo_vector(dve, q + 1)
            hidt_lo_vector(dve, last)
            if not final:
                row_gate_vector(dve, q + 1, s0 + nb * (u + 1))
            sums_lo_vector(dve, q)
            if not final:
                begin(make_step(t, u + 1, 0, 0), make_step(t, u + 1, 0, 1), q + 1)
            else:
                scatter_vector(dve, q)
        pick_vector(dve, t, 0, q0)
        first_weights_vector(dve, t, (2, 3))
        rows_lo_vector(dve, q0)
        row_gate_vector(dve, q0, s0)
        pickr_vector(dve, q0)
        begin(make_step(t, 0, 0, 0), make_step(t, 0, 0, 1), q0)
        units(dve, t, unit)
        dve.wait_ge(sem("scatter_read"), 4 * (q0 + n_units) + CREDIT)
        overflow_vector(dve, t)

    def block_part(m, e, b, axis):
        m = m.unsqueeze(0) if e is None else m[bass.ds(e, 1)]
        if b is None:
            return m
        return m[:, :, bass.ds(b * BLK, BLK)] if axis else m[:, bass.ds(b * BLK, BLK), :]

    def load_gate_up(sp, wg, wu, e, b, slot, landed):
        for k, m in enumerate((wg, wu)):
            sp.dma_start(ffw_gu[:, slot, :, k * BLK:(k + 1) * BLK],
                         block_part(m, e, b, 1).rearrange("a (p c) n -> p (a c) n", c=DC)).then_inc(landed, 16)

    def load_down(sp, wd, e, b, slot, landed):
        sp.dma_start(ffw_d[:, slot], block_part(wd, e, b, 0).rearrange("a (f p) n -> p (a f) n", p=P))\
            .then_inc(landed, 16)

    def ff_sync(sp, t, wg, wu, wd):
        b0, _, q0, n_units, nb = FFS[t]
        if t == "m2":
            def place(u, i, c):
                return u, 2 * i + c, nb * u + 2 * i + c
        elif t == "ff":
            def place(u, i, c):
                return None, 2 * i + c, 2 * i + c
        else:
            def place(u, i, c):
                return 2 * i + c, None, 2 * i + c

        def gate_up(u, i, c):
            e, b, n = place(u, i, c)
            slot = (b0 + c) % 2
            sp.wait_ge(sem("gu_split"), GU_PIECES * (b0 + n - 1) + GU_CREDIT)
            load_gate_up(sp, wg, wu, e, b, slot, sem(f"gu_landed{slot}"))

        def down(u, i, c):
            e, b, n = place(u, i, c)
            slot = (b0 + c) % 2
            sp.wait_ge(sem("down_split"), DOWN_PIECES * (b0 + n - 1) + DOWN_CREDIT)
            load_down(sp, wd, e, b, slot, sem(f"down_landed{slot}"))

        def pairs(u, lo, hi):
            with sp.Fori(lo, hi) as i:
                for c in range(2):
                    gate_up(u, i, c + 1)
                    down(u, i, c)

        def last_pair(u, i, following):
            gate_up(u, i, 1)
            down(u, i, 0)
            if following:
                gate_up(u + 1, 0, 0)
            down(u, i, 1)
        gate_up(0, 0, 0)
        if t == "ff":
            pairs(0, 0, nb // 2)
            down(0, nb // 2, 0)
            return
        if t == "m2":
            with sp.Fori(0, n_units - 1) as u:
                pairs(u, 0, nb // 2 - 1)
                last_pair(u, nb // 2 - 1, True)
            pairs(n_units - 1, 0, nb // 2 - 1)
            last_pair(n_units - 1, nb // 2 - 1, False)
        else:
            pairs(0, 0, n_units * nb // 2 - 1)
            last_pair(0, n_units * nb // 2 - 1, False)
        overflow_sync(sp, t, wg, wu, wd)

    OV_UNIT = {"pe": 3, "dve": 12, "act": 0}
    OV_BLOCK = {"pe": 3, "dve": 4, "act": 1}

    def ov_at(eng, t, u, b, k):
        nb = FFS[t][4]
        return (OV_UNIT[eng] + nb * OV_BLOCK[eng]) * u + OV_BLOCK[eng] * b + k

    def ov_begin(eng, t):
        eng.wait_ge(sem("route_flag"), ROUTER[t] + 1)
        return eng.value_load(flags[0:1, ROUTER[t]:ROUTER[t] + 1], min_val=0, max_val=1)

    def ov_blocks(eng, t, fn):
        nb = FFS[t][4]
        if nb == 4:
            for b in range(nb):
                fn(b)
        else:
            with eng.Fori(0, nb) as b:
                fn(b)

    def overflow_sync(sp, t, wg, wu, wd):
        flag = ov_begin(sp, t)
        b0, s0, q0, n_units, nb = FFS[t]
        with sp.If(flag > 0):
            sp.wait_ge(sem("gu_split"), GU_PIECES * (b0 + nb * n_units) + GU_CREDIT)
            sp.wait_ge(sem("down_split"), DOWN_PIECES * (b0 + nb * n_units) + DOWN_CREDIT)
            with sp.Fori(0, n_units) as u:
                def load(b):
                    sp.wait_ge(sem(f"ov_dve_{t}"), ov_at("dve", t, u, b, 8))
                    e, col = (4 * u + b, None) if nb == 4 else (u, b)
                    load_gate_up(sp, wg, wu, e, col, 0, sem(f"ov_load_{t}"))
                    load_down(sp, wd, e, col, 0, sem(f"ov_load_{t}"))
                ov_blocks(sp, t, load)
            sp.wait_ge(sem(f"ov_pe_{t}"), ov_at("pe", t, n_units, 0, 0))

    def overflow_tensor(pe, t):
        flag = ov_begin(pe, t)
        n_units, nb = FFS[t][3], FFS[t][4]
        done, dve, act = sem(f"ov_pe_{t}"), sem(f"ov_dve_{t}"), sem(f"ov_act_{t}")
        with pe.If(flag > 0):
            with pe.Fori(0, n_units) as u:
                pe.wait_ge(dve, ov_at("dve", t, u, 0, 4))
                for last in gather_matmuls():
                    pass
                last.then_inc(done, 1)
                permute_tensor(pe, done)

                def block_of(b):
                    pe.wait_ge(dve, ov_at("dve", t, u, b, 8))
                    pe.wait_ge(sem(f"ov_load_{t}"), 48 * (nb * u + b + 1))
                    for c in range(DC):
                        last = nc.tensor.matmul(psum[0], ov_x[:, c, :], ffw_gu[:, 0, c, :], start=(c == 0), stop=(c == DC - 1))
                    last.then_inc(done, 1)
                    pe.wait_ge(dve, ov_at("dve", t, u, b, 9))
                    for f in range(2):
                        last = nc.tensor.transpose(psum[2][:, f * P:(f + 1) * P], hid[:, 0, f * P:(f + 1) * P], ident)
                    last.then_inc(done, 1)
                    pe.wait_ge(dve, ov_at("dve", t, u, b, 10))
                    for half in range(2):
                        for f in range(2):
                            last = nc.tensor.matmul(psum[3 + half], ov_hidT[:, f, :],
                                                    ffw_d[:, 0, f, half * 512:(half + 1) * 512], start=(f == 0), stop=(f == 1))
                    last.then_inc(done, 1)
                ov_blocks(pe, t, block_of)
                pe.wait_ge(dve, ov_at("dve", t, u, nb, 8))
                for k in range(4):
                    last = nc.tensor.matmul(psum[(3, 4, 5, 6)[k]], pick_r[:, k // 2, :].bitcast(F32),
                                            ov_y[:, (k % 2) * 512:(k % 2 + 1) * 512], start=True, stop=True)
                last.then_inc(done, 1)

    def overflow_scalar(act, t):
        flag = ov_begin(act, t)
        with act.If(flag > 0):
            with act.Fori(0, FFS[t][3]) as u:
                def block_of(b):
                    act.wait_ge(sem(f"ov_pe_{t}"), ov_at("pe", t, u, b, 3))
                    nc.scalar.activation(silu_buf[:, 0, :], psum[0][:, 0:BLK], ACT.Silu).then_inc(sem(f"ov_act_{t}"), 1)
                ov_blocks(act, t, block_of)

    def overflow_vector(dve, t):
        flag = ov_begin(dve, t)
        n_units, nb = FFS[t][3], FFS[t][4]
        done, pe = sem(f"ov_dve_{t}"), sem(f"ov_pe_{t}")
        with dve.If(flag > 0):
            with dve.Fori(0, n_units) as u:
                def step(ins, b, k):
                    ins.then_inc(done, 1)
                    dve.wait_ge(done, ov_at("dve", t, u, b, k))
                rows = row_of[:, :, bass.ds(u, 1)].rearrange("p j a -> p (j a)")
                step(V.tensor_copy(unit_row, rows), 0, 1)
                step(V.tensor_scalar(unit_row, unit_row, -float(SLOTS), None, ALU.add), 0, 2)
                cols = gates[:, :, bass.ds(4 * u, 4)] if nb == 4 else gates[:, :, bass.ds(u, 4)]
                step(V.tensor_copy(unit_gate, cols), 0, 3)
                V.memset(ov_y, 0.0)
                V.tensor_scalar(pick_t[:, 0, :], row_index, unit_row[:, 0:1], None, ALU.is_equal)
                step(V.tensor_scalar(pick_t[:, 1, :], row_index, unit_row[:, 1:2], None, ALU.is_equal), 0, 4)
                dve.wait_ge(pe, ov_at("pe", t, u, 0, 2))
                for k in range(2):
                    src = psum[5 + k].rearrange("p (c t) -> p c t", c=4)
                    step(V.tensor_copy(ov_x[:, 4 * k:4 * k + 4, :], src), 0, 5 + k)
                step(V.tensor_copy(pick_r.rearrange("p j t -> p (j t)"), psum[7][:, 0:2 * P]), 0, 7)
                V.tensor_copy(row_gate, psum[7][:, 256:260]).then_inc(done, 1)

                def block_of(b):
                    dve.wait_ge(sem(f"ov_act_{t}"), ov_at("act", t, u, b, 1))
                    step(V.tensor_tensor(hid[:, 0, :], silu_buf[:, 0, :], psum[0][:, BLK:2 * BLK], ALU.mult), b, 9)
                    dve.wait_ge(pe, ov_at("pe", t, u, b, 4))
                    step(V.tensor_copy(ov_hidT.rearrange("p f t -> p (f t)"), psum[2][:, 0:BLK]), b, 10)
                    dve.wait_ge(pe, ov_at("pe", t, u, b, 5))
                    col = b if nb == 4 else 0
                    for half in range(2):
                        cols = slice(half * 512, (half + 1) * 512)
                        step(V.scalar_tensor_tensor(out=ov_y[:, cols], in0=psum[3 + half], scalar=row_gate[:, col:col + 1],
                                                    in1=ov_y[:, cols], op0=ALU.mult, op1=ALU.add), b, 11 + half)
                ov_blocks(dve, t, block_of)
                dve.wait_ge(pe, ov_at("pe", t, u, nb, 3))
                for k in range(4):
                    hv = h[:, k // 2, (k % 2) * 512:(k % 2 + 1) * 512]
                    step(V.tensor_tensor(hv, psum[(3, 4, 5, 6)[k]], hv, ALU.add), nb, 9 + k)

    FFR = {"m0": True, "m1": True, "m2": False}
    logit = tiny(T, 20)
    r_m, r_m2, r_sum, r_g = tiny(T, 1), tiny(T, 1), tiny(T, 1), tiny(T, 1)
    r_eq, r_sc = tiny(T, 8), tiny(T, 8)
    r_grp, r_one, r_two = tiny(T, 4), tiny(T, 8), tiny(T, 8)
    r_e = tiny(T, 12)
    r_sel = tiny(T, 8)
    r_tmp = tiny(T, 4, 4)
    rank = tiny(8)

    flags = sb("flags", [P, 3], I32)

    def first_max(vals, n, value, onehot):
        vlink(V.tensor_reduce(out=value, in_=vals, axis=AX, op=ALU.max))
        vlink(V.tensor_tensor(r_eq[:, :, 0:n], vals, value.to_broadcast([P, T, n]), ALU.is_equal))
        vlink(V.tensor_tensor(r_sc[:, :, 0:n], r_eq[:, :, 0:n], over(rank[:, 0:n], 1, T), ALU.mult))
        vlink(V.tensor_reduce(out=r_m2, in_=r_sc[:, :, 0:n], axis=AX, op=ALU.max))
        vlink(V.tensor_tensor(onehot, r_sc[:, :, 0:n], r_m2.to_broadcast([P, T, n]), ALU.is_equal))

    def route_vector(dve, t, bias):
        grouped = FFR[t]
        n = 4 if grouped else MOE2_E
        cols = 20 if grouped else MOE2_E
        dve.wait_ge(sem("route_logits"), ROUTER[t] + 1)
        src = psum[4][:, 0:32 * T].rearrange("p (j n) -> p j n", j=T)[:, :, 0:cols]
        if grouped:
            vlink(V.tensor_tensor(logit, src, over(bias, 1, T), ALU.add))
            first_max(logit[:, :, 0:4], 4, r_m, r_grp)
            vlink(V.tensor_tensor(r_e[:, :, 0:4], logit[:, :, 0:4], r_m.to_broadcast([P, T, 4]), ALU.subtract))
            for j in range(T):
                vlink(V.tensor_tensor(r_tmp[:, j], logit[:, j, 4:20].rearrange("p (g e) -> p g e", g=4),
                                      over(r_grp[:, j, :], 2, 4), ALU.mult))
                vlink(V.tensor_reduce(out=r_sel[:, j, 0:4], in_=r_tmp[:, j].rearrange("p g e -> p e g"), axis=AX,
                                      op=ALU.add))
            vals = r_sel[:, :, 0:4]
        else:
            vlink(V.tensor_copy(r_sel, src))
            vals = r_sel
        first_max(vals, n, r_m, r_one[:, :, 0:n])
        vlink(V.tensor_tensor(r_e[:, :, 4:4 + n], vals, r_m.to_broadcast([P, T, n]), ALU.subtract))
        vlink(V.scalar_tensor_tensor(out=r_two[:, :, 0:n], in0=r_one[:, :, 0:n], scalar=NEG, in1=vals,
                                     op0=ALU.mult, op1=ALU.add))
        if not grouped:
            vlink(V.tensor_copy(r_e[:, :, 0:4], r_e[:, :, 4:8]))
        else:
            vlink(V.memset(r_e[:, :, 8:12], 0.0))
        first_max(r_two[:, :, 0:n], n, r_g, r_sc[:, :, 0:n])
        vlink(V.tensor_tensor(r_one[:, :, 0:n], r_one[:, :, 0:n], r_sc[:, :, 0:n], ALU.add), sem("route_masked"))
        if grouped:
            vlink(V.memset(member[:, :, 4:8], 0.0))
            vlink(V.tensor_copy(member[:, :, 0:4], r_grp), sem("route_member"))
        else:
            vlink(V.tensor_copy(member, r_one), sem("route_member"))
        dve.wait_ge(sem("route_rows"), ROUTER[t] + 1)
        rows = psum[7][:, 0:16].rearrange("p (j n) -> p j n", j=T)
        vlink(V.scalar_tensor_tensor(out=row_of, in0=rows, scalar=1.0, in1=member, op0=ALU.add, op1=ALU.mult))
        vlink(V.tensor_scalar(row_of, row_of, -1.0, None, ALU.add))
        vlink(V.tensor_reduce(out=r_sum[:, 0], in_=psum[7][:, 16:24], axis=AX, op=ALU.max))
        vlink(V.tensor_scalar(r_sum[:, 0], r_sum[:, 0], SLOTS + 0.5, None, ALU.is_gt))
        vlink(V.tensor_copy(flags[:, ROUTER[t]:ROUTER[t] + 1], r_sum[:, 0]), sem("route_flag"))
        dve.wait_ge(sem("route_exp"), ROUTER[t] + 1)
        vlink(V.tensor_tensor(r_two[:, :, 0:n], r_e[:, :, 4:4 + n], r_one[:, :, 0:n], ALU.mult))
        vlink(V.tensor_reduce(out=r_sum, in_=r_two[:, :, 0:n], axis=AX, op=ALU.add))
        vlink(V.reciprocal(r_sum, r_sum))
        vlink(V.tensor_tensor(r_two[:, :, 0:n], r_two[:, :, 0:n], r_sum.to_broadcast([P, T, n]), ALU.mult))
        if grouped:
            vlink(V.tensor_reduce(out=r_g, in_=r_e[:, :, 0:4], axis=AX, op=ALU.add))
            vlink(V.reciprocal(r_g, r_g))
            vlink(V.tensor_tensor(r_two[:, :, 0:4], r_two[:, :, 0:4], r_g.to_broadcast([P, T, 4]), ALU.mult))
            for j in range(T):
                vlink(V.tensor_tensor(gates[:, j, :].rearrange("p (g e) -> p g e", g=4), over(r_grp[:, j, :], 2, 4),
                                      over(r_two[:, j, 0:4], 1, 4), ALU.mult))
        else:
            vlink(V.memset(gates[:, :, 8:16], 0.0))
            vlink(V.tensor_copy(gates[:, :, 0:8], r_two))

    def moe_first_vector(dve, t, i):
        to_features_vector(t)
        tokens_lo_vector(dve, t, h)
        for j in range(T):
            vlink(V.tensor_scalar(h[:, j, :], h[:, j, :], ALPHA, None, ALU.mult))
        first_weights_vector(dve, t, (0, 1))
        route_vector(dve, t, par[f"route_b{i}"])
        ff_vector(dve, t)
        dve.wait_ge(sem("norm_landed"), 32 * (2 * i + 2))
        layer_norm()
        dve.sem_inc(sem("phase_done"), 1)

    def normed_vector(t, gain=None):
        rms_scale(h, junk_row, D, rstd)
        for j in range(T):
            last = [sem("normed")] if j else []
            if gain is None:
                vlink(V.tensor_scalar(normed[:, j, :], h[:, j, :], rstd[:, j:j + 1], None, ALU.mult), *last)
            else:
                vlink(V.scalar_tensor_tensor(out=normed[:, j, :], in0=h[:, j, :], scalar=rstd[:, j:j + 1], in1=gain,
                                             op0=ALU.mult, op1=ALU.mult), *last)

    ca = carver()
    c_tok = ca(T, Q_RANK + KV_RANK + ROPE)
    fox_q, fox_k, fox_v = ca(4, S), ca(4, S), ca(T, FOX_W)
    c_norm = ca(T, Q_RANK + KV_RANK)
    cT = ca(3, S)
    q_cat, k_cat = ca(T, MLA_H, MLA_K), ca(T, MLA_H, MLA_K)
    v_mla = ca(T, MLA_H, V_DIM)
    mla_qT, mla_kT = ca(MLA_H, S), ca(MLA_H, S)
    odd_mix = ca(T, D)
    odd_mixT = ca(2, 4, S)
    at_masked, at_probs, at_probsT = ca(2, 3, P), ca(2, 3, P), ca(2, 3, P)
    fox_sum, fox_neg = ca(S), ca(S)
    mask_chunk = ca(3, P)
    rope_a, rope_b, rope_c, rope_d = (ca(8, 16) for _ in range(4))
    sel = odd_mixT.rearrange("p k c t -> p (k c) t")
    fox_bias = ca(2, 3, P)
    at_nbias, at_sums = tiny(16, 2), tiny(16, 2)
    log_f, f_e, f_x = tiny(T, FOX_H), tiny(T, FOX_H), tiny(T, FOX_H)
    c_rstd = tiny(2, T)

    def odd_tensor(pe):
        t = "od"
        pe.wait_ge(sem("phase_done"), 2)
        to_features_tensor(pe, t, h)
        project_tensor(pe, t, odd_pieces)
        n_p = len(odd_pieces)
        read_wait(pe, "od", 0, n_p)
        read_wait(pe, "od", 1, n_p)
        pe.wait_ge(sem("od_c_normed"), 1)
        for c in range(3):
            for j in range(T):
                last = nc.tensor.transpose(psum[6 + c // 2][:, (c % 2) * S + j * P:(c % 2) * S + (j + 1) * P],
                                           c_norm[:, j, c * P:(c + 1) * P], ident)
        last.then_inc(sem("od_c_turned"), 1)
        pe.wait_ge(sem("od_ct_ready"), 1)
        piece_wait(pe, odd_qup)
        wq = piece_ap(odd_qup)
        for j in range(T):
            for half, (a, b) in enumerate(((0, 512), (512, MLA_H * MLA_K))):
                for c in range(2):
                    last = nc.tensor.matmul(psum[2 * j + half][:, 0:b - a], cT[:, c, j * P:(j + 1) * P], wq[:, c, a:b],
                                            start=(c == 0), stop=(c == 1))
        last.then_inc(sem("od_qup"), 1)
        piece_wait(pe, odd_kvup)
        wkv = piece_ap(odd_kvup)
        for j in range(T):
            for half in range(2):
                last = nc.tensor.matmul(psum[4 + 2 * j + half], cT[:, 2, j * P:(j + 1) * P],
                                        wkv[:, half * 512:(half + 1) * 512], start=True, stop=True)
        last.then_inc(sem("od_kvup"), 1)
        pe.wait_ge(sem("od_cat_ready"), 1)
        for n in range(8):
            src = (q_cat, k_cat)[n // 4]
            if n >= 2:
                pe.wait_ge(sem("od_cat_read"), n - 1)
            for i in range(4):
                hd, j = 2 * (n % 4) + i // 2, i % 2
                last = nc.tensor.transpose(psum[6 + n % 2][0:MLA_K, i * P:(i + 1) * P], src[:, j, hd, :], ident)
            last.then_inc(sem("od_cat_turned"), 1)
        pe.wait_ge(sem("od_cat_read"), 8)

        def mla_logits(u, bank):
            nc.tensor.matmul(bank[:, 0:P], mla_qT[0:MLA_K, u, 0:P], mla_kT[0:MLA_K, u, 0:P], start=True, stop=True)
            return nc.tensor.matmul(bank[:, P:3 * P], mla_qT[0:MLA_K, u, P:S], mla_kT[0:MLA_K, u, :],
                                    start=True, stop=True)
        attention_tensor(pe, "mla", MLA_H, mla_logits, at_probs, at_probsT, lambda u, s: v_mla[:, s, u, :], V_DIM)
        pe.wait_ge(sem("od_logf"), 1)
        nc.tensor.matmul(psum[6][0:FOX_H, 0:P], log_f[:, 0, :], upto, start=True, stop=True)
        nc.tensor.matmul(psum[6][0:FOX_H, P:S], log_f[:, 0, :], ones, start=True, stop=False)
        nc.tensor.matmul(psum[6][0:FOX_H, P:S], log_f[:, 1, :], upto, start=False, stop=True)\
            .then_inc(sem("od_fsum"), 1)
        pe.wait_ge(sem("od_fsum_read"), 1)
        pe.wait_ge(sem("at_written"), MLA_H)

        def fox_logits(u, bank):
            if u >= 2:
                pe.wait_ge(sem("fox_biased"), u - 1)
            fb = psum[6 + u % 2]
            for j, (a, b) in enumerate(((0, P), (P, 3 * P))):
                nc.tensor.matmul(fb[:, a:b], fox_sum[0:FOX_H, j * P:(j + 1) * P], sel[0:FOX_H, u, 0:b - a],
                                 start=True, stop=False)
                last = nc.tensor.matmul(fb[:, a:b], sel[0:FOX_H, u, 0:P], fox_neg[0:FOX_H, 0:b - a],
                                        start=False, stop=True)
            last.then_inc(sem("fox_term"), 1)
            r = slice((u % 2) * 64, (u % 2) * 64 + 64)
            qq, kk = fox_q[r, u // 2, :], fox_k[r, u // 2, :]
            nc.tensor.matmul(bank[:, 0:P], qq[:, 0:P], kk[:, 0:P], start=True, stop=True)
            return nc.tensor.matmul(bank[:, P:3 * P], qq[:, P:S], kk, start=True, stop=True)
        attention_tensor(pe, "fox", FOX_H, fox_logits, at_probs, at_probsT,
                         lambda u, s: fox_v[:, s, u * HD:(u + 1) * HD], HD)
        out_tensor(pe, t, odd_mix, odd_mixT, odd_out)

    def odd_scalar(act):
        A = nc.scalar
        for n, (name, _, _, cols) in enumerate(odd_pieces):
            full_wait(act, "od", 0, n)
            b0 = psum[2 * (n % 3)]
            b0c = b0.rearrange("p (c t) -> p c t", c=2)
            if name == "q":
                ins = A.mul(fox_q[:, 0:2, :], b0c, HD ** -0.5)
            elif name == "k":
                ins = A.copy(fox_k[:, 0:2, :], b0c)
            else:
                ins = A.copy({"c": c_tok, "v": fox_v, "f": f_x}[name][:, 0, :], b0[:, 0:cols])
            ins.then_inc(sem("bank0_read"), 1)
            if name == "c":
                rsqrt_scalar(act, sq, T)
                rsqrt_scalar(act, sq, T)
        act.wait_ge(sem("od_qup"), 1)
        for j in range(T):
            qv = q_cat[:, j].rearrange("p h d -> p (h d)")
            A.copy(qv[:, 0:512], psum[2 * j])
            ins = A.copy(qv[:, 512:], psum[2 * j + 1][:, 0:MLA_H * MLA_K - 512])
        ins.then_inc(sem("od_qcat"), 1)
        act.wait_ge(sem("od_f_negabs"), 1)
        A.activation(f_e, f_e, ACT.Exp).then_inc(sem("od_f_exp"), 1)
        act.wait_ge(sem("od_f_exp"), 1)
        A.activation(f_e, f_e, ACT.Ln, bias=1.0).then_inc(sem("od_f_ln"), 1)
        attention_scalar(act, "mla", MLA_H, MLA_K ** -0.5, at_masked, at_nbias, at_probs, at_sums, at_probsT)
        attention_scalar(act, "fox", FOX_H, 1.0, at_masked, at_nbias[:, 8:], at_probs, at_sums[:, 8:], at_probsT)
        rsqrt_scalar(act, sq, T)

    def rope(x1, x2, cos, sin, tmps):
        a, b, c, d = tmps
        vlink(V.tensor_tensor(a, x1, cos, ALU.mult))
        vlink(V.tensor_tensor(b, x2, sin, ALU.mult))
        vlink(V.tensor_tensor(c, x2, cos, ALU.mult))
        vlink(V.tensor_tensor(d, x1, sin, ALU.mult))
        vlink(V.tensor_tensor(x1, a, b, ALU.subtract))
        vlink(V.tensor_tensor(x2, c, d, ALU.add))

    def odd_vector(dve):
        vlink(V.memset(mask_chunk, 0.0))
        for i in (0, 2):
            vlink(V.memset(mask_chunk[0:64, i, 64:P], NEG))
        to_features_vector("od")
        vlink(V.tensor_copy(sel[0:FOX_H], over(ident[0:FOX_H, 0:FOX_H], 2, S)))
        for n, (name, _, _, cols) in enumerate(odd_pieces):
            full_wait(dve, "od", 1, n)
            b1 = psum[2 * (n % 3) + 1]
            b1c = b1.rearrange("p (c t) -> p c t", c=2)
            if name == "q":
                ins = V.tensor_scalar(fox_q[:, 2:4, :], b1c, HD ** -0.5, None, ALU.mult)
            elif name == "k":
                ins = V.tensor_copy(fox_k[:, 2:4, :], b1c)
            else:
                ins = V.tensor_copy({"c": c_tok, "v": fox_v, "f": f_x}[name][:, 1, :], b1[:, 0:cols])
            vlink(ins, sem("bank1_read"))
            if name == "c":
                read_wait(dve, "od", 0, n + 1)
                for i, (a, b) in enumerate(((0, Q_RANK), (Q_RANK, Q_RANK + KV_RANK))):
                    rms_scale(c_tok[:, :, a:b], q_cat[:, 0].rearrange("p h d -> p (h d)")[:, 0:b - a], b - a, c_rstd[:, i, :])
                    for j in range(T):
                        vlink(V.tensor_scalar(c_norm[:, j, a:b], c_tok[:, j, a:b], c_rstd[:, i, j:j + 1], None, ALU.mult),
                              *([sem("od_c_normed")] if i and j else []))
        read_wait(dve, "od", 0, len(odd_pieces))
        vlink(V.tensor_tensor(f_x, f_x, over(par["f_bias"], 1, T), ALU.add))
        vlink(V.tensor_scalar(f_x, f_x, -1.0, None, ALU.mult))
        vlink(minus_abs(f_e, f_x), sem("od_f_negabs"))
        dve.wait_ge(sem("od_c_turned"), 1)
        vlink(V.tensor_tensor(cT[:, 0:2, :], psum[6].rearrange("p (c t) -> p c t", c=2), over(par["q_norm"], 2, S), ALU.mult))
        vlink(V.tensor_scalar(cT[:, 2, :], psum[7][:, 0:S], par["kv_norm"], None, ALU.mult), sem("od_ct_ready"))
        tab = par["tables"]
        for j in range(T):
            pe_k = c_tok[:, j:j + 1, Q_RANK + KV_RANK:]
            cos, sin = (over(tab[:, j, 16 * i:16 * i + 16], 1, 1) for i in range(2))
            rope(pe_k[:, :, 0:16], pe_k[:, :, 16:32], cos, sin, [x[:, 0:1, :] for x in (rope_a, rope_b, rope_c, rope_d)])
        dve.wait_ge(sem("od_kvup"), 1)
        for j in range(T):
            for half in range(2):
                kv = psum[4 + 2 * j + half].rearrange("p (h d) -> p h d", h=4)
                vlink(V.tensor_copy(k_cat[:, j, 4 * half:4 * half + 4, 0:NOPE], kv[:, :, 0:NOPE]))
                vlink(V.tensor_copy(v_mla[:, j, 4 * half:4 * half + 4, :], kv[:, :, NOPE:]))
            vlink(V.tensor_copy(k_cat[:, j, :, NOPE:], over(c_tok[:, j, Q_RANK + KV_RANK:], 1, MLA_H)))
        dve.wait_ge(sem("od_qcat"), 1)
        for j in range(T):
            cos, sin = (over(tab[:, j, 16 * i:16 * i + 16], 1, MLA_H) for i in range(2))
            rope(q_cat[:, j, :, NOPE:NOPE + 16], q_cat[:, j, :, NOPE + 16:], cos, sin, (rope_a, rope_b, rope_c, rope_d))
        vlink(V.memset(at_sums, 0.0), sem("od_cat_ready"))
        for n in range(8):
            dve.wait_ge(sem("od_cat_turned"), n + 1)
            dst = (mla_qT, mla_kT)[n // 4]
            vlink(V.tensor_copy(dst[0:MLA_K, 2 * (n % 4):2 * (n % 4) + 2, :],
                                psum[6 + n % 2][0:MLA_K, :].rearrange("p (h t) -> p h t", h=2)), sem("od_cat_read"))
        dve.wait_ge(sem("od_f_ln"), 1)
        vlink(V.scalar_tensor_tensor(out=log_f, in0=f_x, scalar=0.0, in1=f_e, op0=ALU.max, op1=ALU.add))
        vlink(V.tensor_scalar(log_f, log_f, -1.0, None, ALU.mult), sem("od_logf"))

        def head_writer(off, width):
            def write(u, bank, scale, done):
                vlink(V.tensor_tensor(odd_mix[:, :, off + u * width:off + (u + 1) * width],
                                      bank[:, 0:T * width].rearrange("p (j d) -> p j d", j=T),
                                      over(scale, 2, width), ALU.mult), done)
            return write
        attention_vector("mla", MLA_H, MLA_K ** -0.5, lambda u: mask_chunk, at_masked, at_nbias, at_sums,
                         head_writer(0, V_DIM))
        dve.wait_ge(sem("od_fsum"), 1)
        vlink(V.tensor_copy(fox_sum[0:FOX_H], psum[6][0:FOX_H, 0:S]))
        vlink(V.tensor_scalar(fox_neg[0:FOX_H], fox_sum[0:FOX_H], -1.0, None, ALU.mult), sem("od_fsum_read"))

        def fox_mask(u):
            dve.wait_ge(sem("fox_term"), u + 1)
            vlink(V.tensor_tensor(fox_bias[:, u % 2], psum[6 + u % 2][:, 0:3 * P].rearrange("p (i s) -> p i s", i=3),
                                  mask_causal, ALU.add), sem("fox_biased"))
            return fox_bias[:, u % 2]
        attention_vector("fox", FOX_H, 1.0, fox_mask, at_masked, at_nbias[:, 8:], at_sums[:, 8:],
                         head_writer(MLA_H * V_DIM, HD))
        vlink(V.memset(at_nbias[:, 0, :], 0.0), sem("mix_ready"))
        out_vector("od", odd_mixT, 2, ALPHA)
        dve.wait_ge(sem("norm_landed"), 96)
        layer_norm()
        dve.sem_inc(sem("phase_done"), 1)

    ca = carver()
    ca(3 * D)
    sg_mix = ca(T, SG_W)
    sg_v = ca(T, SG_W)
    sg_mixT = ca(4, 4, S)
    spatialT = ca(SG_G, P)
    sg_junk = ca(SG_W)

    def sg_tensor(pe):
        t = "sg"
        pe.wait_ge(sem("phase_done"), 4)
        pe.wait_ge(sem("normed"), 1)
        to_features_tensor(pe, t, normed)
        project_tensor(pe, t, sg_pieces)
        read_wait(pe, "sg", 0, 8)
        read_wait(pe, "sg", 1, 8)
        piece_wait(pe, sg_spatial)
        wsp = piece_ap(sg_spatial)
        for g in range(SG_G):
            last = nc.tensor.transpose(psum[6 + g // 4][:, (g % 4) * P:(g % 4 + 1) * P], wsp[:, g, :], ident)
        last.then_inc(sem("sg_w_turned"), 1)
        pe.wait_ge(sem("sg_w_ready"), 1)
        pe.wait_ge(sem("sg_v_ready"), 1)
        for n in range(8):
            j, g = n // 4, 2 * (n % 4)
            if n >= 4:
                pe.wait_ge(sem("sg_gated"), n - 3)
            for i in range(2):
                last = nc.tensor.matmul(psum[n % 4][:, i * SG_C:(i + 1) * SG_C], spatialT[:, g + i, :],
                                        sg_v[:, j, (g + i) * SG_C:(g + i + 1) * SG_C], start=True, stop=True)
            last.then_inc(sem("sg_mixed"), 1)
        out_tensor(pe, t, sg_mix, sg_mixT, sg_out)

    def sg_scalar(act):
        rsqrt_scalar(act, sq, T)
        for n in range(8):
            dst = sg_mix if n < 4 else sg_v
            for half in range(2):
                full_wait(act, "sg", half, n)
                nc.scalar.activation(dst[:, half, (n % 4) * 512:(n % 4 + 1) * 512], psum[2 * (n % 3) + half],
                                     ACT.Gelu_apprx_tanh).then_inc(sem(f"bank{half}_read"), 1)
        rsqrt_scalar(act, sq, T)

    def sg_vector(dve):
        normed_vector("sg")
        to_features_vector("sg", par["l0_mix_norm_2"])
        dve.wait_ge(sem("sg_w_turned"), 1)
        for i in range(2):
            vlink(V.tensor_tensor(spatialT[:, 4 * i:4 * i + 4, :], psum[6 + i].rearrange("p (g t) -> p g t", g=4),
                                  over(upto, 1, 4), ALU.mult), *([sem("sg_w_ready")] if i else []))
        read_wait(dve, "sg", 1, 8)
        rms_scale(sg_v, sg_junk, SG_W, rstd)
        dve.wait_ge(sem("norm_landed"), 160)
        for j in range(T):
            vlink(V.scalar_tensor_tensor(out=sg_v[:, j, :], in0=sg_v[:, j, :], scalar=rstd[:, j:j + 1], in1=norm_vec,
                                         op0=ALU.mult, op1=ALU.mult), *([sem("sg_v_ready")] if j else []))
        for n in range(8):
            j, g = n // 4, 2 * (n % 4)
            dve.wait_ge(sem("sg_mixed"), n + 1)
            for i in range(2):
                u = sg_mix[:, j, (g + i) * SG_C:(g + i + 1) * SG_C]
                vlink(V.scalar_tensor_tensor(out=u, in0=psum[n % 4][:, i * SG_C:(i + 1) * SG_C],
                                             scalar=par["b_spatial"][:, g + i:g + i + 1], in1=u, op0=ALU.add, op1=ALU.mult),
                      *([sem("sg_gated")] if i else []), *([sem("mix_ready")] if i and n == 7 else []))
        out_vector("sg", sg_mixT, 4, 1.0)
        dve.sem_inc(sem("phase_done"), 1)

    def dense_vector(dve):
        normed_vector("ff")
        to_features_vector("ff", par["l0_ffn_norm_2"])
        tokens_lo_vector(dve, "ff", xT.rearrange("p (j c) t -> p j (c t)", j=2))
        ff_vector(dve, "ff")
        dve.sem_inc(sem("phase_done"), 1)

    def moe_second_vector(dve):
        dve.wait_ge(sem("norm_landed"), 176)
        normed_vector("m2", norm_vec[:, 0:D])
        to_features_vector("m2")
        tokens_lo_vector(dve, "m2", normed)
        first_weights_vector(dve, "m2", (0, 1))
        route_vector(dve, "m2", None)
        ff_vector(dve, "m2")
        dve.sem_inc(sem("phase_done"), 1)

    ca = carver()
    ca(3 * D)
    MAPS = 2 * DA_H
    da_qk = ca(T, 2 * MAPS, HD)
    da_v = ca(T, D)
    da_qkT = ca(2 * DA_H, S)
    da_mix = ca(T, D)
    da_mixT = ca(2, 4, S)
    da_masked, da_probs, da_probsT = ca(2, 3, P), ca(2, 3, P), ca(2, 3, P)
    da_first = ca(T, P)
    da_tmps = [ca(2 * MAPS, 8) for _ in range(4)]
    da_sq = da_mixT.rearrange("p k c t -> p (k c t)").rearrange("p (m d) -> p m d", d=HD)
    da_ms = ca(T, 2 * MAPS)
    da_hs = ca(T, DA_H)
    da_ms_flat, da_hs_flat = da_ms.rearrange("p j m -> p (j m)"), da_hs.rearrange("p j h -> p (j h)")
    ang, turns, half_sin, cs_cos, cs_sin = (tiny(T, 8) for _ in range(5))
    posf = tiny(T)
    lam_tmp, lam_sum = ca(2, HD), tiny(2)
    neg_lam = tiny(1)

    def da_tensor(pe):
        t = "da"
        pe.wait_ge(sem("phase_done"), 6)
        pe.wait_ge(sem("normed"), 3)
        to_features_tensor(pe, t, normed)
        project_tensor(pe, t, da_pieces)
        pe.wait_ge(sem("da_rotated"), 1)
        for n in range(8):
            if n >= 2:
                pe.wait_ge(sem("da_qk_read"), n - 1)
            for i in range(4):
                c, j = 2 * n + i // 2, i % 2
                last = nc.tensor.transpose(psum[6 + n % 2][:, i * P:(i + 1) * P],
                                           da_qk[:, j, 2 * c:2 * c + 2, :].rearrange("p m d -> p (m d)"), ident)
            last.then_inc(sem("da_qk_turned"), 1)
        pe.wait_ge(sem("da_qk_read"), 8)
        read_wait(pe, "da", 0, 6)
        read_wait(pe, "da", 1, 6)

        def logits(u, bank):
            r = slice((u % 2) * 64, (u % 2) * 64 + 64)
            qq, kk = da_qkT[r, u // 2, :], da_qkT[r, DA_H + u // 2, :]
            nc.tensor.matmul(bank[:, 0:P], qq[:, 0:P], kk[:, 0:P], start=True, stop=True)
            return nc.tensor.matmul(bank[:, P:3 * P], qq[:, P:S], kk, start=True, stop=True)
        attention_tensor(pe, "dat", MAPS, logits, da_probs, da_probsT,
                         lambda u, s: da_v[:, s, (u // 2) * P:(u // 2 + 1) * P], P)
        out_tensor(pe, t, da_mix, da_mixT, da_out)

    def da_scalar(act):
        A = nc.scalar
        rsqrt_scalar(act, sq, T)
        for n in range(6):
            full_wait(act, "da", 0, n)
            dst = da_qk[:, 0].rearrange("p m d -> p (m d)")[:, n * 512:(n + 1) * 512] if n < 4 else \
                da_v[:, 0, (n - 4) * 512:(n - 3) * 512]
            A.copy(dst, psum[2 * (n % 3)]).then_inc(sem("bank0_read"), 1)
        act.wait_ge(sem("da_reduced"), 1)
        A.activation(cs_sin, ang, ACT.Sin)
        A.activation(half_sin, ang, ACT.Sin, scale=0.5).then_inc(sem("da_sines"), 1)
        act.wait_ge(sem("da_lam_sums"), 1)
        A.activation(lam_sum, lam_sum, ACT.Exp).then_inc(sem("da_lam_exp"), 1)
        rsqrt_scalar(act, da_ms_flat, T * 2 * MAPS)
        attention_scalar(act, "dat", MAPS, HD ** -0.5, da_masked, at_nbias, da_probs, at_sums, da_probsT)
        rsqrt_scalar(act, da_hs_flat, T * DA_H)

    def da_vector(dve):
        normed_vector("da")
        to_features_vector("da", par["l1_mix_norm_2"])
        two_pi = 2 * math.pi
        c1 = 6.28125
        c2 = float(np.float32(np.round((two_pi - c1) * 2 ** 22) / 2 ** 22))
        c3 = float(np.float32(two_pi - c1 - c2))
        magic = 12582912.0
        vlink(V.tensor_copy(posf, par["positions"]))
        vlink(V.tensor_tensor(ang, par["tables"][:, :, 32:40], over(posf, 2, 8), ALU.mult))
        vlink(V.tensor_scalar(turns, ang, 1.0 / two_pi, None, ALU.mult))
        vlink(V.tensor_scalar(turns, turns, magic, None, ALU.add))
        vlink(V.tensor_scalar(turns, turns, -magic, None, ALU.add))
        for c in (c1, c2, c3):
            vlink(V.scalar_tensor_tensor(out=ang, in0=turns, scalar=-c, in1=ang, op0=ALU.mult, op1=ALU.add))
        vlink(V.tensor_scalar(ang, ang, 3.1415925, -3.1415925, ALU.min, ALU.max), sem("da_reduced"))
        lam = par["lam"]
        for i in range(2):
            vlink(V.tensor_tensor_reduce(out=lam_tmp[:, i, :], in0=lam[:, 2 * i, :], in1=lam[:, 2 * i + 1, :], scale=1.0,
                                         scalar=0.0, op0=ALU.mult, op1=ALU.add, accum_out=lam_sum[:, i:i + 1]),
                  *([sem("da_lam_sums")] if i else []))
        for n in range(6):
            full_wait(dve, "da", 1, n)
            dst = da_qk[:, 1].rearrange("p m d -> p (m d)")[:, n * 512:(n + 1) * 512] if n < 4 else \
                da_v[:, 1, (n - 4) * 512:(n - 3) * 512]
            vlink(V.tensor_copy(dst, psum[2 * (n % 3) + 1]), sem("bank1_read"))
        read_wait(dve, "da", 0, 6)
        dve.wait_ge(sem("da_sines"), 1)
        vlink(V.tensor_tensor(cs_cos, half_sin, half_sin, ALU.mult))
        vlink(V.tensor_scalar(cs_cos, cs_cos, -2.0, 1.0, ALU.mult, ALU.add))
        dve.wait_ge(sem("da_lam_exp"), 1)
        vlink(V.tensor_tensor(neg_lam, lam_sum[:, 1:2], lam_sum[:, 0:1], ALU.subtract))
        vlink(V.tensor_scalar(neg_lam, neg_lam, -LAMBDA_INIT, None, ALU.add))
        for j in range(T):
            vlink(V.tensor_tensor(da_sq, da_qk[:, j], da_qk[:, j], ALU.mult))
            vlink(V.tensor_reduce(out=da_ms[:, j, :], in_=da_sq, axis=AX, op=ALU.add))
        vlink(V.tensor_scalar(da_ms, da_ms, 1.0 / HD, RMS_EPS, ALU.mult, ALU.add))
        rsqrt_vector(da_ms_flat, da_ms_flat, T * 2 * MAPS)
        for j in range(T):
            vlink(V.tensor_tensor(da_qk[:, j], da_qk[:, j], over(da_ms[:, j, :], 2, HD), ALU.mult))
            for i, gain in enumerate(("da_q_norm", "da_k_norm")):
                part = da_qk[:, j, i * MAPS:(i + 1) * MAPS, :]
                vlink(V.tensor_tensor(part, part, over(par[gain], 1, MAPS), ALU.mult))
            cos, sin = (over(x[:, j, :], 1, 2 * MAPS) for x in (cs_cos, cs_sin))
            rope(da_qk[:, j, :, 0:8], da_qk[:, j, :, 8:16], cos, sin, da_tmps)
        vlink(V.memset(at_sums, 0.0), sem("da_rotated"))
        for n in range(8):
            dve.wait_ge(sem("da_qk_turned"), n + 1)
            vlink(V.tensor_copy(da_qkT[:, 2 * n:2 * n + 2, :], psum[6 + n % 2].rearrange("p (c t) -> p c t", c=2)),
                  sem("da_qk_read"))

        def write(u, bank, scale, done):
            src = bank[:, 0:T * P].rearrange("p (j d) -> p j d", j=T)
            if u % 2 == 0:
                vlink(V.tensor_tensor(da_first, src, over(scale, 2, P), ALU.mult), done)
            else:
                dst = da_mix[:, :, (u // 2) * P:(u // 2 + 1) * P]
                vlink(V.tensor_tensor(dst, src, over(scale, 2, P), ALU.mult), done)
                vlink(V.scalar_tensor_tensor(out=dst, in0=dst, scalar=neg_lam, in1=da_first, op0=ALU.mult, op1=ALU.add))
        attention_vector("dat", MAPS, HD ** -0.5, lambda u: mask_causal, da_masked, at_nbias, at_sums, write)
        for j in range(T):
            y = da_mix[:, j, :].rearrange("p (h d) -> p h d", d=P)
            sqv = da_qk[:, 0].rearrange("p m d -> p (m d)")[:, 0:D].rearrange("p (h d) -> p h d", d=P)
            vlink(V.tensor_tensor(sqv, y, y, ALU.mult))
            vlink(V.tensor_reduce(out=da_hs[:, j, :], in_=sqv, axis=AX, op=ALU.add))
        vlink(V.tensor_scalar(da_hs, da_hs, 1.0 / P, RMS_EPS, ALU.mult, ALU.add))
        rsqrt_vector(da_hs_flat, da_hs_flat, T * DA_H)
        vlink(V.tensor_scalar(da_hs, da_hs, 1.0 - LAMBDA_INIT, None, ALU.mult))
        for j in range(T):
            y = da_mix[:, j, :].rearrange("p (h d) -> p h d", d=P)
            vlink(V.tensor_tensor(y, y, over(da_hs[:, j, :], 2, P), ALU.mult))
            vlink(V.tensor_tensor(y, y, over(par["subln"], 1, DA_H), ALU.mult), *([sem("mix_ready")] if j else []))
        out_vector("da", da_mixT, 2, 1.0)
        dve.sem_inc(sem("phase_done"), 1)

    block = nc.Block()
    with block as block:
        @block.sync
        def _(sp):
            sp.dma_start(h, w["x"][0].rearrange("(j p) d -> p j d", p=P)).then_inc(sem("x_landed"), 16)

            def load_pieces(a, b):
                for n in range(a, b):
                    if n >= PSLOTS:
                        name, count = released[n - PSLOTS]
                        sp.wait_ge(sem(name), count)
                    sp.dma_start(piece_ap(n), piece_list[n][0]).then_inc(sem(f"piece_landed{n % PSLOTS}"), 16)
            load_pieces(0, EVEN_END)
            ff_sync(sp, "m0", w["moe_w_gate"][0], w["moe_w_up"][0], w["moe_w_down"][0])
            load_pieces(EVEN_END, ODD_END)
            ff_sync(sp, "m1", w["moe_w_gate"][1], w["moe_w_up"][1], w["moe_w_down"][1])
            load_pieces(ODD_END, SG_END)
            ff_sync(sp, "ff", w["l0_ffn_w_gate_2"], w["l0_ffn_w_up_2"], w["l0_ffn_w_down_2"])
            load_pieces(SG_END, DA_END)
            ff_sync(sp, "m2", w["l1_moe_w_gate_2"], w["l1_moe_w_up_2"], w["l1_moe_w_down_2"])
            sp.wait_ge(sem("phase_done"), 8)
            sp.dma_start(out[0].rearrange("(j p) d -> p j d", p=P), h).then_inc(sem("out_written"), 16)
            sp.wait_ge(sem("out_written"), 16)

        @block.gpsimd
        def _(pool):
            setup_gpsimd(pool)
            phases_gpsimd(pool)

        @block.tensor
        def _(pe):
            credits_tensor(pe)
            even_tensor(pe)
            moe_tensor(pe, "m0", 1, par["route_w0"])
            odd_tensor(pe)
            moe_tensor(pe, "m1", 3, par["route_w1"])
            sg_tensor(pe)
            dense_tensor(pe)
            da_tensor(pe)
            moe_tensor(pe, "m2", 7, par["route_w2"])

        @block.scalar
        def _(act):
            even_scalar(act)
            ff_scalar(act, "m0")
            odd_scalar(act)
            ff_scalar(act, "m1")
            sg_scalar(act)
            ff_scalar(act, "ff")
            da_scalar(act)
            ff_scalar(act, "m2")

        @block.vector
        def _(dve):
            for i in range(8):
                vlink(V.memset(rank[:, i:i + 1], float(8 - i)))
            dve.wait_ge(sem("const_ready"), 1)
            dve.wait_ge(sem("index_ready"), 1)
            dve.sem_inc(sem("gu_split"), GU_CREDIT)
            dve.sem_inc(sem("down_split"), DOWN_CREDIT)
            even_vector(dve)
            moe_first_vector(dve, "m0", 0)
            odd_vector(dve)
            moe_first_vector(dve, "m1", 1)
            sg_vector(dve)
            dense_vector(dve)
            da_vector(dve)
            moe_second_vector(dve)


INPUTS = [
    "x", "ev_w_in", "ev_conv_w", "ev_conv_b", "ev_dt_bias", "ev_a_log", "ev_d_skip", "ev_norm_g", "ev_w_out",
    "od_w_in", "od_q_norm_g", "od_w_q_up", "od_kv_norm_g", "od_w_kv_up", "od_f_bias", "od_w_out", "ln1_g",
    "ln1_b", "ln2_g", "ln2_b", "moe_w_group", "moe_b_group", "moe_w_expert", "moe_b_expert", "moe_w_gate",
    "moe_w_up", "moe_w_down", "positions_2", "l0_mix_norm_2", "l0_sg_w_in_2", "l0_sg_v_norm_2",
    "l0_sg_w_spatial_2", "l0_sg_b_spatial_2", "l0_sg_w_out_2", "l0_ffn_norm_2", "l0_ffn_w_gate_2",
    "l0_ffn_w_up_2", "l0_ffn_w_down_2", "l1_mix_norm_2", "l1_da_w_qkv_2", "l1_da_q_norm_2",
    "l1_da_k_norm_2", "l1_da_lambda_q1_2", "l1_da_lambda_k1_2", "l1_da_lambda_q2_2", "l1_da_lambda_k2_2",
    "l1_da_subln_2", "l1_da_w_out_2", "l1_moe_norm_2", "l1_moe_w_router_2", "l1_moe_w_gate_2",
    "l1_moe_w_up_2", "l1_moe_w_down_2",
]


def kernel(**inputs):
    import numpy as _np
    import concourse.bacc as _bacc
    from concourse import mybir as _mybir
    from concourse.bass_utils import run_bass_kernel_spmd as _run

    nc = _bacc.Bacc("TRN2", target_bir_lowering=False, num_devices=1)
    arrays, w = {}, {}
    for name in INPUTS:
        a = _np.ascontiguousarray(inputs[name])
        arrays[f"in_{name}"] = a
        w[name] = nc.dram_tensor(f"in_{name}", a.shape, _mybir.dt.from_np(a.dtype), kind="ExternalInput").ap()
    tables = shape_tables()
    arrays["in_tables"] = tables
    w["tables"] = nc.dram_tensor("in_tables", tables.shape, _mybir.dt.float32, kind="ExternalInput").ap()
    out = nc.dram_tensor("out", (1, S, D), _mybir.dt.float32, kind="ExternalOutput").ap()
    build(nc, w, out)
    r = _run(nc, [arrays], core_ids=[0])
    return r.results[0]["out"]
```
